# Optimizing a Trainium2 kernel written in Bass

```python
import jax, jax.numpy as jnp
from jax import lax
import numpy as np
import math

D_MODEL = 1024
BATCH = 1
SEQ = 256
DEPTH = 2

D_MIX = D_MODEL
SB_HEAD_DIM = 64
SB_HEADS = (D_MIX // 2) // SB_HEAD_DIM
SB_WIDTH = SB_HEADS * SB_HEAD_DIM
SB_BLOCK = 128
GLA_HEADS = 4
GLA_DV = (D_MIX // 2) // GLA_HEADS
GLA_DK = GLA_DV // 2
GLA_K_WIDTH = GLA_HEADS * GLA_DK
GLA_V_WIDTH = GLA_HEADS * GLA_DV
GLA_RANK = 16
GLA_GATE_NORM = 16.0
GLA_CHUNK = 64
D_IN_PROJ = 3 * SB_WIDTH + 2 * GLA_K_WIDTH + 2 * GLA_V_WIDTH + GLA_RANK
N_GROUPS = 4
EXPERTS_PER_GROUP = 8
TOP_K_IN_GROUP = 2
D_EXPERT = 256
N_MOD = 6
EPS = 1e-6


def rms_norm(x, gain):
    xf = x.astype(jnp.float32)
    y = xf * lax.rsqrt(jnp.mean(xf * xf, axis=-1, keepdims=True) + EPS)
    return (y * gain.astype(jnp.float32)).astype(x.dtype)

def split_heads(t, n_heads):
    b, s, w = t.shape
    return t.reshape(b, s, n_heads, w // n_heads).transpose(0, 2, 1, 3)

def merge_heads(t):
    b, h, s, d = t.shape
    return t.transpose(0, 2, 1, 3).reshape(b, s, h * d)

def stick_breaking_attention(q, k, v):
    B, H, S, d = q.shape
    nb = S // SB_BLOCK
    scale = d ** -0.5
    q_blocks = jnp.moveaxis(q.reshape(B, H, nb, SB_BLOCK, d), 2, 0)
    key_pos = jnp.arange(S)

    def one_block(args):
        q_blk, blk = args
        z = jnp.einsum('bhqd,bhkd->bhqk', q_blk, k).astype(jnp.float32) * scale
        query_pos = blk * SB_BLOCK + jnp.arange(SB_BLOCK)
        before = key_pos[None, :] < query_pos[:, None]
        log_fail = jnp.where(before, -jax.nn.softplus(z), 0.0)
        suffix = lax.cumsum(log_fail, axis=3, reverse=True) - log_fail
        w = jnp.where(before, jnp.exp(jax.nn.log_sigmoid(z) + suffix), 0.0)
        return jnp.einsum('bhqk,bhkd->bhqd', w.astype(v.dtype), v)

    out = lax.map(one_block, (q_blocks, jnp.arange(nb)))
    return jnp.moveaxis(out, 0, 2).reshape(B, H, S, d)

def gla_chunked(q, k, v, log_g):
    B, H, S, dk = q.shape
    dv = v.shape[-1]
    C = GLA_CHUNK
    nc = S // C
    f32 = jnp.float32
    qc = q.astype(f32).reshape(B, H, nc, C, dk) * (dk ** -0.5)
    kc = k.astype(f32).reshape(B, H, nc, C, dk)
    vc = v.astype(f32).reshape(B, H, nc, C, dv)
    b = jnp.cumsum(log_g.astype(f32).reshape(B, H, nc, C, dk), axis=3)
    b_last = b[:, :, :, -1:, :]
    q_dec = qc * jnp.exp(b)
    k_inv = kc * jnp.exp(-b)
    causal = jnp.tril(jnp.ones((C, C), dtype=bool))
    scores = jnp.where(causal, jnp.einsum('bhnqd,bhnkd->bhnqk', q_dec, k_inv), 0.0)
    intra = jnp.einsum('bhnqk,bhnkv->bhnqv', scores, vc)
    chunk_kv = jnp.einsum('bhnkd,bhnkv->bhndv', kc * jnp.exp(b_last - b), vc)
    chunk_decay = jnp.exp(b_last[:, :, :, 0, :])

    def step(state, inp):
        dec, kv_c = inp
        return dec[..., None] * state + kv_c, state

    _, prev = lax.scan(step, jnp.zeros((B, H, dk, dv), f32),
                       (jnp.moveaxis(chunk_decay, 2, 0), jnp.moveaxis(chunk_kv, 2, 0)))
    prev = jnp.moveaxis(prev, 0, 2)
    inter = jnp.einsum('bhnqd,bhndv->bhnqv', q_dec, prev)
    return (intra + inter).reshape(B, H, S, dv).astype(v.dtype)

def hybrid_mixer(h, w_in, w_gk2, b_gk, q_gain, k_gain, gla_gain, w_out):
    proj = h @ w_in
    widths = (SB_WIDTH, SB_WIDTH, SB_WIDTH, GLA_K_WIDTH, GLA_K_WIDTH,
              GLA_V_WIDTH, GLA_V_WIDTH, GLA_RANK)
    cuts = np.cumsum(widths)[:-1].tolist()
    sb_q, sb_k, sb_v, g_q, g_k, g_v, g_r, g_lr = jnp.split(proj, cuts, axis=-1)
    qa = rms_norm(split_heads(sb_q, SB_HEADS), q_gain)
    ka = rms_norm(split_heads(sb_k, SB_HEADS), k_gain)
    out_a = merge_heads(stick_breaking_attention(qa, ka, split_heads(sb_v, SB_HEADS)))
    log_g = jax.nn.log_sigmoid((g_lr @ w_gk2 + b_gk).astype(jnp.float32)) / GLA_GATE_NORM
    o_b = gla_chunked(split_heads(g_q, GLA_HEADS), split_heads(g_k, GLA_HEADS),
                      split_heads(g_v, GLA_HEADS), split_heads(log_g, GLA_HEADS))
    out_b = merge_heads(rms_norm(o_b, gla_gain)) * jax.nn.silu(g_r)
    return jnp.concatenate([out_a, out_b], axis=-1) @ w_out

def hierarchical_moe(h, w_router_grp, b_router_grp, w_router_exp, b_router_exp,
                     w_gate, w_up, w_down):
    B, S, D = h.shape
    hf = h.reshape(B * S, D)
    f32 = jnp.float32
    grp_prob = jax.nn.softmax((hf @ w_router_grp + b_router_grp).astype(f32), axis=-1)
    grp_w, grp_idx = lax.top_k(grp_prob, 1)
    exp_logits = (hf @ w_router_exp + b_router_exp).astype(f32).reshape(-1, N_GROUPS, EXPERTS_PER_GROUP)
    sel_logits = jnp.take_along_axis(exp_logits, grp_idx[:, :, None], axis=1)[:, 0]
    top_logit, top_idx = lax.top_k(sel_logits, TOP_K_IN_GROUP)
    top_w = jax.nn.softmax(top_logit, axis=-1) * grp_w
    exp_w = jnp.sum(jax.nn.one_hot(top_idx, EXPERTS_PER_GROUP, dtype=f32) * top_w[..., None], axis=1)
    comb = (jax.nn.one_hot(grp_idx[:, 0], N_GROUPS, dtype=f32)[:, :, None]
            * exp_w[:, None, :]).astype(h.dtype)
    y = jnp.zeros_like(hf)
    for g in range(N_GROUPS):
        a = jnp.einsum('nd,edf->nef', hf, w_gate[g])
        u = jnp.einsum('nd,edf->nef', hf, w_up[g])
        y = y + jnp.einsum('nef,efd->nd', jax.nn.silu(a) * u * comb[:, g, :, None], w_down[g])
    return y.reshape(B, S, D)

def first_inputs(seed: int = 0) -> dict:
    key = jax.random.key(seed)
    ks = jax.random.split(key, 20)
    f32 = jnp.float32
    nrm = lambda k, shape, s: jax.random.normal(k, shape, f32) * s
    L, D = DEPTH, D_MODEL
    return {
        "x": nrm(ks[0], (BATCH, SEQ, D), 1.0),
        "c": nrm(ks[1], (BATCH, D), 1.0),
        "w_ada": nrm(ks[2], (L, D, N_MOD * D), 0.5 * D ** -0.5),
        "b_ada": nrm(ks[3], (L, N_MOD * D), 0.02),
        "norm_mix": 1.0 + nrm(ks[4], (L, D), 0.02),
        "norm_ffn": 1.0 + nrm(ks[5], (L, D), 0.02),
        "w_in": nrm(ks[6], (L, D, D_IN_PROJ), D ** -0.5),
        "w_gk2": nrm(ks[7], (L, GLA_RANK, GLA_K_WIDTH), GLA_RANK ** -0.5),
        "b_gk": 2.0 + nrm(ks[8], (L, GLA_K_WIDTH), 0.1),
        "q_gain": 1.0 + nrm(ks[9], (L, SB_HEAD_DIM), 0.02),
        "k_gain": 1.0 + nrm(ks[10], (L, SB_HEAD_DIM), 0.02),
        "gla_gain": 1.0 + nrm(ks[11], (L, GLA_DV), 0.02),
        "w_out": nrm(ks[12], (L, D_MIX, D), D_MIX ** -0.5),
        "w_router_grp": nrm(ks[13], (L, D, N_GROUPS), D ** -0.5),
        "b_router_grp": nrm(ks[14], (L, N_GROUPS), 0.01),
        "w_router_exp": nrm(ks[15], (L, D, N_GROUPS * EXPERTS_PER_GROUP), D ** -0.5),
        "b_router_exp": nrm(ks[16], (L, N_GROUPS * EXPERTS_PER_GROUP), 0.01),
        "w_gate": nrm(ks[17], (L, N_GROUPS, EXPERTS_PER_GROUP, D, D_EXPERT), D ** -0.5),
        "w_up": nrm(ks[18], (L, N_GROUPS, EXPERTS_PER_GROUP, D, D_EXPERT), D ** -0.5),
        "w_down": nrm(ks[19], (L, N_GROUPS, EXPERTS_PER_GROUP, D_EXPERT, D), D_EXPERT ** -0.5),
    }

def first_block(x, c, w_ada, b_ada, norm_mix, norm_ffn, w_in, w_gk2, b_gk, q_gain, k_gain,
              gla_gain, w_out, w_router_grp, b_router_grp, w_router_exp, b_router_exp,
              w_gate, w_up, w_down):
    c_act = jax.nn.silu(c)
    for l in range(DEPTH):
        mod = (c_act @ w_ada[l] + b_ada[l])[:, None, :]
        shift_m, scale_m, gate_m, shift_f, scale_f, gate_f = jnp.split(mod, N_MOD, axis=-1)
        h = rms_norm(x, norm_mix[l]) * (1.0 + scale_m) + shift_m
        x = x + gate_m * hybrid_mixer(h, w_in[l], w_gk2[l], b_gk[l], q_gain[l], k_gain[l],
                                      gla_gain[l], w_out[l])
        h = rms_norm(x, norm_ffn[l]) * (1.0 + scale_f) + shift_f
        x = x + gate_f * hierarchical_moe(h, w_router_grp[l], b_router_grp[l], w_router_exp[l],
                                          b_router_exp[l], w_gate[l], w_up[l], w_down[l])
    return x


MIX_WIDTH = D_MODEL
LRU_WIDTH = MIX_WIDTH // 2
LRU_BLOCKS = 8
LRU_BLOCK_DIM = LRU_WIDTH // LRU_BLOCKS
CONV_WIDTH = 4
LRU_C = 8.0
N_HEADS = 8
HEAD_DIM = (MIX_WIDTH - LRU_WIDTH) // N_HEADS
N_KV = 2
Q_PER_KV = N_HEADS // N_KV
NSA_WIDTH = N_HEADS * HEAD_DIM
KV_WIDTH = N_KV * HEAD_DIM
N_BRANCHES = 3
CMP_BLOCK = 32
CMP_STRIDE = 16
SEL_BLOCK = 64
SEL_TOPN = 16
WINDOW = 512
Q_BLOCK = 128
FORCE_BONUS = 1e4
NEG = -1e30
PEER_HEADS = 8
PEER_KEYS = 128
PEER_TOPK = 16
PEER_KEY_DIM = 128
N_EXPERTS = PEER_KEYS * PEER_KEYS
PEER_CHUNK = 512
IN_SPLITS = (LRU_WIDTH, LRU_WIDTH, NSA_WIDTH, KV_WIDTH, KV_WIDTH, KV_WIDTH, KV_WIDTH, KV_WIDTH, KV_WIDTH, N_HEADS * N_BRANCHES)
IN_COLS = sum(IN_SPLITS)
ALPHA = (2 * DEPTH) ** 0.25
BETA = (8 * DEPTH) ** -0.25
LN_EPS = 1e-5


def _layer_norm(x, g, b):
    xf = x.astype(jnp.float32)
    mu = jnp.mean(xf, -1, keepdims=True)
    var = jnp.mean(jnp.square(xf - mu), -1, keepdims=True)
    return ((xf - mu) * lax.rsqrt(var + LN_EPS) * g.astype(jnp.float32) + b.astype(jnp.float32)).astype(x.dtype)

def _rms_norm(x, g):
    xf = x.astype(jnp.float32)
    return (xf * lax.rsqrt(jnp.mean(jnp.square(xf), -1, keepdims=True) + LN_EPS) * g.astype(jnp.float32)).astype(x.dtype)

def _alibi_slopes(n):
    return jnp.asarray(np.array([2.0 ** (-8.0 * (h + 1) / n) for h in range(n)], np.float32))

def _rg_lru(xb, gate, conv_w, conv_b, wa, ba, wx, bx, lam):
    B, S, C = xb.shape
    xc = lax.conv_general_dilated(xb, conv_w[:, None, :], window_strides=(1,), padding=[(CONV_WIDTH - 1, 0)],
                                  dimension_numbers=('NWC', 'WIO', 'NWC'), feature_group_count=C) + conv_b
    xr = xc.reshape(B, S, LRU_BLOCKS, LRU_BLOCK_DIM)
    r = jax.nn.sigmoid(jnp.einsum('bsnd,nde->bsne', xr, wa) + ba.reshape(LRU_BLOCKS, LRU_BLOCK_DIM)).reshape(B, S, C)
    i = jax.nn.sigmoid(jnp.einsum('bsnd,nde->bsne', xr, wx) + bx.reshape(LRU_BLOCKS, LRU_BLOCK_DIM)).reshape(B, S, C)
    log_a = -LRU_C * r.astype(jnp.float32) * jax.nn.softplus(-lam.astype(jnp.float32))
    a = jnp.exp(log_a)
    u = jnp.sqrt(-jnp.expm1(2.0 * log_a)) * (i * xc).astype(jnp.float32)

    def combine(left, right):
        a1, b1 = left
        a2, b2 = right
        return a1 * a2, a2 * b1 + b2

    _, h = lax.associative_scan(combine, (a, u), axis=1)
    return h.astype(xb.dtype) * jax.nn.gelu(gate)

def _compress(k, pos, w1, b1, w2, b2):
    B, S, G, hd = k.shape
    nc = (S - CMP_BLOCK) // CMP_STRIDE + 1
    idx = np.arange(nc)[:, None] * CMP_STRIDE + np.arange(CMP_BLOCK)[None, :]
    blk = k[:, idx] + pos[None, None, :, None, :]
    flat = blk.transpose(0, 1, 3, 2, 4).reshape(B, nc, G, CMP_BLOCK * hd)
    return jax.nn.gelu(flat @ w1 + b1) @ w2 + b2

def _selection_matrix(n_cmp, n_sel):
    cs = np.arange(n_cmp)[:, None] * CMP_STRIDE
    ss = np.arange(n_sel)[None, :] * SEL_BLOCK
    ov = np.clip(np.minimum(cs + CMP_BLOCK, ss + SEL_BLOCK) - np.maximum(cs, ss), 0, None)
    return (ov / CMP_STRIDE).astype(np.float32)

def _nsa(q, kc, vc, ks, vs, kw, vw, gates):
    B, S = q.shape[:2]
    G, R, hd = N_KV, Q_PER_KV, HEAD_DIM
    nb = S // Q_BLOCK
    qb_all = (q * (hd ** -0.5)).reshape(B, nb, Q_BLOCK, G, R, hd).transpose(1, 0, 2, 3, 4, 5)
    g_all = jax.nn.sigmoid(gates).reshape(B, nb, Q_BLOCK, G, R, N_BRANCHES).transpose(1, 0, 2, 3, 4, 5)
    slopes = _alibi_slopes(N_HEADS).reshape(G, R)
    nc = kc.shape[1]
    cmp_end = jnp.arange(nc) * CMP_STRIDE + CMP_BLOCK - 1
    n_sel = S // SEL_BLOCK
    n_top = min(SEL_TOPN, n_sel)
    sel_mat = jnp.asarray(_selection_matrix(nc, n_sel))
    ks_blk = ks.transpose(0, 2, 1, 3).reshape(B, G, n_sel, SEL_BLOCK, hd)
    vs_blk = vs.transpose(0, 2, 1, 3).reshape(B, G, n_sel, SEL_BLOCK, hd)
    kw_pad = jnp.pad(kw, ((0, 0), (WINDOW, 0), (0, 0), (0, 0)))
    vw_pad = jnp.pad(vw, ((0, 0), (WINDOW, 0), (0, 0), (0, 0)))
    gather = jax.vmap(jax.vmap(lambda blk, ix: blk[ix]))
    blk_id = jnp.arange(n_sel)

    def one_block(args):
        qb, q_blk, g_blk = args
        t = qb * Q_BLOCK + jnp.arange(Q_BLOCK)
        s = jnp.einsum('bqgrd,bcgd->bgrqc', q_blk, kc).astype(jnp.float32)
        dist_c = (t[:, None] - cmp_end[None, :]).astype(jnp.float32)
        s = s - slopes[:, :, None, None] * jnp.abs(dist_c)
        valid_c = cmp_end[None, :] <= t[:, None]
        p_c = jax.nn.softmax(jnp.where(valid_c, s, NEG), axis=-1) * valid_c.any(-1)[:, None].astype(jnp.float32)
        o_c = jnp.einsum('bgrqc,bcgd->bqgrd', p_c.astype(vc.dtype), vc)
        imp = jnp.einsum('bgrqc,cj->bgqj', p_c, sel_mat)
        cur = t // SEL_BLOCK
        vblk = blk_id[None, :] <= cur[:, None]
        forced = (blk_id[None, :] == 0) | (blk_id[None, :] == cur[:, None]) | (blk_id[None, :] == cur[:, None] - 1)
        imp = jnp.where(vblk, imp + jnp.where(forced, FORCE_BONUS, 0.0), NEG)
        _, idx = lax.top_k(imp, n_top)
        k_sel = gather(ks_blk, idx)
        v_sel = gather(vs_blk, idx)
        tok = idx[..., None] * SEL_BLOCK + jnp.arange(SEL_BLOCK)
        dist_s = (t[None, None, :, None, None] - tok)[:, :, None]
        s = jnp.einsum('bqgrd,bgqnld->bgrqnl', q_blk, k_sel).astype(jnp.float32)
        s = s - slopes[None, :, :, None, None, None] * jnp.abs(dist_s).astype(jnp.float32)
        s = jnp.where(dist_s >= 0, s, NEG)
        p_s = jax.nn.softmax(s.reshape(s.shape[:4] + (n_top * SEL_BLOCK,)), axis=-1).reshape(s.shape)
        o_s = jnp.einsum('bgrqnl,bgqnld->bqgrd', p_s.astype(v_sel.dtype), v_sel)
        k_w = lax.dynamic_slice_in_dim(kw_pad, qb * Q_BLOCK, WINDOW + Q_BLOCK, axis=1)
        v_w = lax.dynamic_slice_in_dim(vw_pad, qb * Q_BLOCK, WINDOW + Q_BLOCK, axis=1)
        pos = qb * Q_BLOCK - WINDOW + jnp.arange(WINDOW + Q_BLOCK)
        dist_w = t[:, None] - pos[None, :]
        valid_w = (dist_w >= 0) & (dist_w < WINDOW) & (pos >= 0)[None, :]
        s = jnp.einsum('bqgrd,bkgd->bgrqk', q_blk, k_w).astype(jnp.float32)
        s = s - slopes[:, :, None, None] * dist_w.astype(jnp.float32)
        p_w = jax.nn.softmax(jnp.where(valid_w, s, NEG), axis=-1)
        o_w = jnp.einsum('bgrqk,bkgd->bqgrd', p_w.astype(v_w.dtype), v_w)
        return g_blk[..., 0:1] * o_c + g_blk[..., 1:2] * o_s + g_blk[..., 2:3] * o_w

    out = lax.map(one_block, (jnp.arange(nb), qb_all, g_all))
    return out.transpose(1, 0, 2, 3, 4, 5).reshape(B, S, N_HEADS * hd)

def _peer(x, wq, subkeys, u_tab, v_tab):
    B, S, D = x.shape
    T = B * S
    xf = x.reshape(T, D)
    q = (xf @ wq).reshape(T, PEER_HEADS, 2, PEER_KEY_DIM)
    s = jnp.einsum('thcd,ckd->thck', q, subkeys).astype(jnp.float32)
    sv, si = lax.top_k(s, PEER_TOPK)
    cand = (sv[:, :, 0, :, None] + sv[:, :, 1, None, :]).reshape(T, PEER_HEADS, PEER_TOPK * PEER_TOPK)
    cv, ci = lax.top_k(cand, PEER_TOPK)
    ea = jnp.take_along_axis(si[:, :, 0], ci // PEER_TOPK, axis=-1)
    eb = jnp.take_along_axis(si[:, :, 1], ci % PEER_TOPK, axis=-1)
    experts = (ea * PEER_KEYS + eb).reshape(T, PEER_HEADS * PEER_TOPK)
    gate = jax.nn.softmax(cv, axis=-1).reshape(T, PEER_HEADS * PEER_TOPK).astype(x.dtype)
    chunk = math.gcd(T, PEER_CHUNK)
    nch = T // chunk

    def one_chunk(args):
        xc, ec, gc = args
        act = jax.nn.gelu(jnp.einsum('cd,ced->ce', xc, u_tab[ec]))
        return jnp.einsum('ce,ced->cd', act * gc, v_tab[ec])

    y = lax.map(one_chunk, (xf.reshape(nch, chunk, D), experts.reshape(nch, chunk, -1), gate.reshape(nch, chunk, -1)))
    return y.reshape(B, S, D)

def second_inputs(seed: int = 0) -> dict:
    key = jax.random.key(seed)
    ks = jax.random.split(key, 40)
    L = DEPTH

    def nrm(k, shape, scale):
        return jax.random.normal(k, shape, jnp.float32) * scale

    col_scale = np.concatenate([np.full(n, s, np.float32) for n, s in zip(
        IN_SPLITS, (BETA, 1.0, 1.0, 1.0, BETA, 1.0, BETA, 1.0, BETA, 1.0))])
    u = jax.random.uniform(ks[9], (L, LRU_WIDTH), jnp.float32, 0.9, 0.999)
    a0 = u ** (1.0 / LRU_C)
    fan_c = CMP_BLOCK * HEAD_DIM
    return {
        'x': nrm(ks[0], (BATCH, SEQ, D_MODEL), 1.0),
        'w_in': nrm(ks[1], (L, D_MODEL, IN_COLS), D_MODEL ** -0.5) * jnp.asarray(col_scale),
        'b_in': nrm(ks[2], (L, IN_COLS), 0.01),
        'conv_w': nrm(ks[3], (L, CONV_WIDTH, LRU_WIDTH), CONV_WIDTH ** -0.5),
        'conv_b': nrm(ks[4], (L, LRU_WIDTH), 0.01),
        'lru_wa': nrm(ks[5], (L, LRU_BLOCKS, LRU_BLOCK_DIM, LRU_BLOCK_DIM), LRU_BLOCK_DIM ** -0.5),
        'lru_ba': nrm(ks[6], (L, LRU_WIDTH), 0.01),
        'lru_wx': nrm(ks[7], (L, LRU_BLOCKS, LRU_BLOCK_DIM, LRU_BLOCK_DIM), LRU_BLOCK_DIM ** -0.5),
        'lru_bx': nrm(ks[8], (L, LRU_WIDTH), 0.01),
        'lru_lambda': jnp.log(a0) - jnp.log1p(-a0),
        'cmp_pos_k': nrm(ks[10], (L, CMP_BLOCK, HEAD_DIM), 0.02),
        'cmpk_w1': nrm(ks[11], (L, fan_c, HEAD_DIM), fan_c ** -0.5),
        'cmpk_b1': nrm(ks[12], (L, HEAD_DIM), 0.01),
        'cmpk_w2': nrm(ks[13], (L, HEAD_DIM, HEAD_DIM), HEAD_DIM ** -0.5),
        'cmpk_b2': nrm(ks[14], (L, HEAD_DIM), 0.01),
        'cmp_pos_v': nrm(ks[15], (L, CMP_BLOCK, HEAD_DIM), 0.02),
        'cmpv_w1': nrm(ks[16], (L, fan_c, HEAD_DIM), fan_c ** -0.5),
        'cmpv_b1': nrm(ks[17], (L, HEAD_DIM), 0.01),
        'cmpv_w2': nrm(ks[18], (L, HEAD_DIM, HEAD_DIM), HEAD_DIM ** -0.5),
        'cmpv_b2': nrm(ks[19], (L, HEAD_DIM), 0.01),
        'gn_lru_g': 1.0 + nrm(ks[20], (L, LRU_WIDTH), 0.02),
        'gn_nsa_g': 1.0 + nrm(ks[21], (L, NSA_WIDTH), 0.02),
        'w_out': nrm(ks[22], (L, MIX_WIDTH, D_MODEL), BETA * MIX_WIDTH ** -0.5),
        'ln1_g': 1.0 + nrm(ks[23], (L, D_MODEL), 0.02),
        'ln1_b': nrm(ks[24], (L, D_MODEL), 0.02),
        'peer_wq': nrm(ks[25], (L, D_MODEL, PEER_HEADS * 2 * PEER_KEY_DIM), D_MODEL ** -0.5),
        'peer_subkeys': nrm(ks[26], (L, 2, PEER_KEYS, PEER_KEY_DIM), PEER_KEY_DIM ** -0.5),
        'peer_u': nrm(ks[27], (L, N_EXPERTS, D_MODEL), D_MODEL ** -0.5),
        'peer_v': nrm(ks[28], (L, N_EXPERTS, D_MODEL), BETA * PEER_HEADS ** -0.5),
        'ln2_g': 1.0 + nrm(ks[29], (L, D_MODEL), 0.02),
        'ln2_b': nrm(ks[30], (L, D_MODEL), 0.02),
    }

def second_block(x, w_in, b_in, conv_w, conv_b, lru_wa, lru_ba, lru_wx, lru_bx, lru_lambda,
              cmp_pos_k, cmpk_w1, cmpk_b1, cmpk_w2, cmpk_b2,
              cmp_pos_v, cmpv_w1, cmpv_b1, cmpv_w2, cmpv_b2,
              gn_lru_g, gn_nsa_g, w_out, ln1_g, ln1_b,
              peer_wq, peer_subkeys, peer_u, peer_v, ln2_g, ln2_b):
    B, S, _ = x.shape
    offsets = np.cumsum(IN_SPLITS)[:-1].tolist()
    for l in range(DEPTH):
        h = x @ w_in[l] + b_in[l]
        lru_x, lru_gate, q, kc_raw, vc_raw, ks_, vs_, kw_, vw_, gts = jnp.split(h, offsets, axis=-1)
        y_lru = _rg_lru(lru_x, lru_gate, conv_w[l], conv_b[l], lru_wa[l], lru_ba[l],
                        lru_wx[l], lru_bx[l], lru_lambda[l])
        kv = lambda t: t.reshape(B, S, N_KV, HEAD_DIM)
        kc = _compress(kv(kc_raw), cmp_pos_k[l], cmpk_w1[l], cmpk_b1[l], cmpk_w2[l], cmpk_b2[l])
        vc = _compress(kv(vc_raw), cmp_pos_v[l], cmpv_w1[l], cmpv_b1[l], cmpv_w2[l], cmpv_b2[l])
        y_nsa = _nsa(q.reshape(B, S, N_HEADS, HEAD_DIM), kc, vc, kv(ks_), kv(vs_), kv(kw_), kv(vw_),
                     gts.reshape(B, S, N_HEADS, N_BRANCHES))
        mix = jnp.concatenate([_rms_norm(y_lru, gn_lru_g[l]), _rms_norm(y_nsa, gn_nsa_g[l])], axis=-1) @ w_out[l]
        x = _layer_norm(ALPHA * x + mix, ln1_g[l], ln1_b[l])
        x = _layer_norm(ALPHA * x + _peer(x, peer_wq[l], peer_subkeys[l], peer_u[l], peer_v[l]), ln2_g[l], ln2_b[l])
    return x


def setup_inputs(seed=0):
    out = dict(first_inputs(seed))
    for name, value in second_inputs(seed + 1).items():
        if name != "x":
            out[name + "_2"] = value
    return out


def reference(
    x, c, w_ada, b_ada, norm_mix, norm_ffn, w_in, w_gk2, b_gk, q_gain, k_gain, gla_gain, w_out,
    w_router_grp, b_router_grp, w_router_exp, b_router_exp, w_gate, w_up, w_down, w_in_2,
    b_in_2, conv_w_2, conv_b_2, lru_wa_2, lru_ba_2, lru_wx_2, lru_bx_2, lru_lambda_2,
    cmp_pos_k_2, cmpk_w1_2, cmpk_b1_2, cmpk_w2_2, cmpk_b2_2, cmp_pos_v_2, cmpv_w1_2, cmpv_b1_2,
    cmpv_w2_2, cmpv_b2_2, gn_lru_g_2, gn_nsa_g_2, w_out_2, ln1_g_2, ln1_b_2, peer_wq_2,
    peer_subkeys_2, peer_u_2, peer_v_2, ln2_g_2, ln2_b_2,
):
    x = first_block(
        x, c, w_ada, b_ada, norm_mix, norm_ffn, w_in, w_gk2, b_gk, q_gain, k_gain, gla_gain,
        w_out, w_router_grp, b_router_grp, w_router_exp, b_router_exp, w_gate, w_up, w_down,
    )
    return second_block(
        x, w_in_2, b_in_2, conv_w_2, conv_b_2, lru_wa_2, lru_ba_2, lru_wx_2, lru_bx_2,
        lru_lambda_2, cmp_pos_k_2, cmpk_w1_2, cmpk_b1_2, cmpk_w2_2, cmpk_b2_2, cmp_pos_v_2,
        cmpv_w1_2, cmpv_b1_2, cmpv_w2_2, cmpv_b2_2, gn_lru_g_2, gn_nsa_g_2, w_out_2, ln1_g_2,
        ln1_b_2, peer_wq_2, peer_subkeys_2, peer_u_2, peer_v_2, ln2_g_2, ln2_b_2,
    )


_drawn_inputs = setup_inputs


def setup_inputs(seed=0):
    import zlib

    import numpy as np

    out = dict(_drawn_inputs(seed))
    spreads = {}
    factors = {'norm_mix': 2.733,
     'b_gk': 2.932,
     'q_gain': 8.0,
     'k_gain': 4.769,
     'gla_gain': 4.872,
     'b_router_grp': 11.707,
     'b_router_exp': 3.533,
     'lru_ba_2': 28.909,
     'lru_bx_2': 8.0,
     'cmp_pos_k_2': 30.392,
     'cmpk_b1_2': 48.414,
     'cmpk_b2_2': 64.0,
     'cmp_pos_v_2': 4.316,
     'cmpv_b1_2': 6.258,
     'cmpv_b2_2': 4.376,
     'gn_lru_g_2': 14.565,
     'gn_nsa_g_2': 15.355}
    for name, (base, spread) in spreads.items():
        noise = np.random.default_rng([zlib.crc32(name.encode()), seed]).standard_normal(out[name].shape)
        drawn = base * np.exp(spread * noise) if base else spread * noise
        out[name] = __import__('jax').numpy.asarray(drawn.astype(out[name].dtype))
    for name, factor in factors.items():
        out[name] = (out[name] * factor).astype(out[name].dtype)
    return out
```

```python
import math
from contextlib import ExitStack

import numpy as np
import concourse.bass as bass
from concourse import mybir

F32 = mybir.dt.float32
U32 = mybir.dt.uint32
ACT = mybir.ActivationFunctionType
ALU = mybir.AluOpType
AX = mybir.AxisListType

P = 128
D = 1024
KT = D // P
T = 256
TT = T // P
DEPTH = 2
NMOD = 6
SBH, SBD = 8, 64
GH, GDK, GDV, RANK, CHUNK = 4, 64, 128, 16, 64
NCH = T // CHUNK
NG, EPG = 4, 8
NE = NG * EPG
FE = 256
FT = FE // P
EPS = 1e-6
LT = 4
HD, NH, NKV, REP = 64, 8, 2, 4
CB, CS = 32, 16
NC = (T - CB) // CS + 1
NCP = 16
PH, PK, TOPK = 8, 128, 16
LN_EPS = 1e-5
ALPHA = (2 * DEPTH) ** 0.25
NEG = -1e30
SLOT = 1024
RING = 8
TMW = 2 * NKV * HD + NH * 3

W1_IN, W1_OUT = 24, 8
MOE_SLOTS = 6 * NE
W2_IN, W2_OUT, W2_Q = 20, 8, 16
PEER_SLOTS = 2 * PK
MOE_STEP = 4
PEER_STEP = 4

def _layout(items):
    at, out = 0, {}
    for name, n in items:
        out[name] = (at, n)
        at += n
    return out, at


CST, CST_N = _layout([
    ("ident", P), ("ones", P), ("headblk", P), ("sufneg", P), ("negones", P), ("sbmask", 384), ("glamask", P),
    ("iota", P), ("alibi0", NH * P), ("alibi1", NH * T), ("alibic", TT * NH * NCP), ("anyc", TT),
])
C1, C1_N = _layout([
    ("norm_mix", 8), ("norm_ffn", 8), ("b_ada", 48), ("b_gk", 2), ("q_gain", 1), ("k_gain", 1), ("gla_gain", 1),
])
C2, C2_N = _layout([
    ("b_in", W2_IN), ("conv_w", 16), ("conv_b", LT), ("lru_ba", LT), ("lru_bx", LT), ("lam", LT), ("gn_lru", LT),
    ("gn_nsa", LT), ("ln1_g", 8), ("ln1_b", 8), ("ln2_g", 8), ("ln2_b", 8), ("b1k", 1), ("b1v", 1), ("b2k", 1),
    ("pos_k", CB // 2), ("pos_v", CB // 2),
])
CMPW = 16 * HD
X2, X2_N = _layout([("w1k", CMPW), ("w1v", CMPW), ("w2k", 2 * HD), ("w2v", HD), ("wa", LT * P), ("wx", LT * P)])

SEMS = """x_load cst_load col_load row_load slot_done ada_used ada_acc ada_ps ada_col csilu pair_evac x_ready
norm_sq norm_ss norm_rs h_ready
aux1_load glr_mm glr_ev gkz_mm gkz_ev sbv_ev gv_ev qk_sq qk_ss qk_rs qkn z_mm zm_ok ln_ok lf_ok suf_mm arg_ok w_ok pv_mm
outa_ev gl_ln gl_b gl_e1 gl_e2 gl_prod kend_mm kend_ev kv_mm states sc_mm sc_ok o_mm o_ev o_sq o_ss o_rs grs
mixb_ok
rt_load rt_mm rt_cp rt_max rt_exp comb_ok comb_mm combt_ev comb_st comb_ld silu_ok hh_ok y_ev yt_mm
tm_load x2_load x2_z tm_mm tm_ev
xc_ok ri_mm ri_ev lam_e loga th_ok u_in sqrt_ok lru_h gelu_g ylru_ok blk_ok c1_mm c1_ev c2_mm c2_ev
cs_mm cs_max cs_exp cs_ok ct_mm ct_ev att_mm att_max att_exp att_ok att_t att_tev nsa_mm nsa_ev
g_sq g_ss g_rs mix2_ok z1_ok ln_mu ln_c ln_sq ln_ss ln_rs
pq_ok sk_load ps_mm ps_ev pk_exp pk_top pk_t pk_tev pt_a pt_mm g_ev y2t z2_ok pk_ok lf_ok2 gelu_ok pw_ok y2_ev out_st""".split()


def program(nc, a, out, plan=None, dumps=None):
    plan = plan or [("mix", 0), ("moe", 0), ("mix", 1), ("moe", 1), ("nsa", 0), ("peer", 0), ("nsa", 1), ("peer", 1)]
    ctx = ExitStack()
    with ctx:
        def sb(name, shape, dt=F32):
            return ctx.enter_context(nc.sbuf_tensor(name, shape, dt))

        S = {n: ctx.enter_context(nc.semaphore(n)) for n in SEMS}
        slot_ready = [ctx.enter_context(nc.semaphore(f"slot_ready{i}")) for i in range(RING)]
        ada_ready = [ctx.enter_context(nc.semaphore(f"ada_ready{i}")) for i in range(3)]

        x = sb("x", [P, KT, T])
        h = sb("h", [P, KT, T])
        ring = sb("ring", [P, RING, SLOT])
        cst = sb("cst", [P, CST_N])
        col1 = sb("col1", [P, DEPTH, C1_N])
        col2 = sb("col2", [P, DEPTH, C2_N])
        row = sb("row", [1, DEPTH, NG + NE + TMW + HD])
        ccol = sb("ccol", [P, KT])
        csil = sb("csil", [P, KT])
        mod = sb("mod", [P, NMOD * KT])
        ga = sb("ga", [P, 2, KT])
        arena = sb("arena", [P, 32768])
        PS = ctx.enter_context(nc.psum_tensor("PS", [P, 8, 512], F32))
        comb_dram = nc.dram_tensor("comb_scratch", (DEPTH, NE, T), F32, kind="Internal").ap()

        def cc(name):
            o, n = CST[name]
            return cst[:, o:o + n]

        def c1(l, name, j=0, n=None):
            o, m = C1[name]
            return col1[:, l, o + j:o + (m if n is None else j + n)]

        def c2(l, name, j=0, n=None):
            o, m = C2[name]
            return col2[:, l, o + j:o + (m if n is None else j + n)]

        def area(names, at=0):
            got = {}
            for name, dims in names:
                n = int(np.prod(dims))
                v = arena[:, at:at + n]
                if len(dims) == 2:
                    v = v.rearrange("p (a b) -> p a b", b=dims[1])
                if len(dims) == 3:
                    v = v.rearrange("p (a b c) -> p a b c", b=dims[1], c=dims[2])
                got[name] = v
                at += n
            assert at <= 32768, at
            return got

        ident, ones = cc("ident"), cc("ones")
        ADA = area([("acc", (NMOD, D)), ("ring", (3, D))], 32768 - 9 * D)
        M = area([
            ("qk", (8, T)), ("qkn", (8, T)), ("gqk", (4, T)), ("gr", (4, T)), ("sbv", (TT, 512)), ("gv", (TT, 512)),
            ("sq", (8, T)), ("rsq", (8, T)), ("zm", (4, 384)), ("e", (4, 384)), ("lf", (4, 384)), ("w", (4, 384)),
            ("wglr", (KT, RANK)), ("gk2", (2 * P,)), ("glr", (T,)), ("rs", (T,)), ("mixT", (KT, T)),
        ])
        G = area([
            ("gy", (2, T)), ("b0", (8, CHUNK)), ("b1", (8, CHUNK)), ("eb", (8, CHUNK)), ("einv", (8, CHUNK)),
            ("eend", (8, CHUNK)), ("qd", (2, T)), ("ki", (2, T)), ("ke", (2, T)), ("kend", (4, P)), ("sc", (8, P)),
            ("st", (NCH - 1, GH, GDV)),
        ], 21376)
        E = area([
            ("rs", (T,)), ("sq", (8, T)), ("comb", (TT, NE)), ("combT", (T,)), ("combB", (NE, T)), ("sg", (4, T)),
            ("t1", (4, T)), ("hh", (4, T)), ("y", (TT, D)), ("lg", (TT, 40)), ("gm8", (TT, 8)), ("sel", (TT, 8)),
            ("m8", (TT, 8)), ("oh", (TT, NG)), ("tmp", (TT, NE)), ("ew", (TT, 8)), ("o2", (TT, 8)), ("sc", (TT, 8)),
            ("gf", (TT, 8)), ("if", (TT, 8)), ("wr", (KT, NG + NE)), ("gx", (TT, NG)),
        ])
        N = area([
            ("p", (W2_IN, T)), ("wtm", (KT, TMW)), ("x2", (X2_N,)), ("vtm", (TT, 4 * HD)), ("gt", (TT, 3 * NH)),
            ("gth", (TT, 3, NH)), ("xc", (LT, T)), ("r", (LT, T)), ("i", (LT, T)), ("a0", (LT, T)), ("a1", (LT, T)),
            ("u", (LT, T)), ("gg", (LT, T)), ("lam", (6, LT)), ("blk", (2, CB // 2, 2 * NC)), ("gel", (2, 2 * NC)),
            ("gvr", (P,)), ("kc", (2 * NC,)), ("vcz", (4, HD)), ("cs", (TT, NH, 32)), ("ct", (4, P)), ("st", (3, TT * NH)),
            ("s0", (NH, T)), ("pt", (6 * NH, P)),
        ])
        N["mix"] = arena[:, 5120:7168].rearrange("p (a b) -> p a b", b=T)
        N["ynsa"] = N["a0"]
        N["sq"] = N["s0"]
        N["rs"] = N["blk"].rearrange("p a m c -> p (a m c)")[:, 0:2 * T]
        L_ = area([("sq", (KT, T)), ("rs", (T,)), ("y", (TT, D))], 16384)
        Q = area([
            ("sk", (2, PK)), ("pq", (2 * PH, T)), ("s", (TT, 2 * PH, PK)), ("wk", (2 * PH, PK)), ("v", (TT, 2 * PH, TOPK)),
            ("si", (TT, 2 * PH, TOPK)), ("cand", (PH, TOPK * TOPK)), ("wk2", (PH, TOPK * TOPK)), ("cv", (TT, PH * TOPK)),
            ("hl", (2, PH * TOPK)), ("eq", (PH * TOPK, TOPK)), ("ab", (TT, 2, PH * TOPK)), ("sm", (TT, PH)), ("gate", (TT, PH * TOPK)),
            ("iu", (TT, 2 * PH, TOPK)), ("ciu", (TT, PH * TOPK)), ("hlu", (2, PH * TOPK)),
        ])
        for name in ("iu", "ciu", "hlu"):
            Q[name] = Q[name].bitcast(U32)
        GT = arena[:, 0:T * PK].rearrange("p (t b) -> p t b", b=PK)
        hw = h[:].rearrange("p a b -> p (a b)")
        egT = hw[:, 0:3 * T].rearrange("p (a b) -> p a b", b=T)
        OA = hw[:, 3 * T:3 * T + 4 * PK].rearrange("p (a b) -> p a b", b=PK)
        OB = hw[:, 3 * T + 4 * PK:3 * T + 8 * PK].rearrange("p (a b) -> p a b", b=PK)
        gel = hw[:, 0:4 * T].rearrange("p (a b) -> p a b", b=T)
        pw = hw[:, 4 * T:8 * T].rearrange("p (a b) -> p a b", b=T)
        gi = sb("gi", [P, TT, 8], U32)
        ii = sb("ii", [P, TT, 8], U32)

        block = ctx.enter_context(nc.Block())

        def slot_base():
            at, got = 0, {}
            for k, l in plan:
                got[k, l] = at
                at += {"mix": W1_IN + W1_OUT, "moe": MOE_SLOTS, "nsa": W2_IN + W2_OUT, "peer": W2_Q + PEER_SLOTS}[k]
            return got, at

        BASE, _ = slot_base()
        PAIR, at = {}, 0
        for k, l in plan:
            PAIR[k, l] = at
            at += {"mix": 12, "moe": 0, "nsa": 14, "peer": 8}[k]
        SIDX = {s: i for i, s in enumerate(plan)}
        LN = {s: i for i, s in enumerate([s for s in plan if s[0] in ("nsa", "peer")])}
        NORM = {s: i for i, s in enumerate([s for s in plan if s[0] in ("mix", "moe")])}

        def wait_slot(eng, n, i=0, per=0):
            eng.wait_ge(slot_ready[n % RING], 16 * (n // RING + 1) + 16 * per * i)

        UNITS = [(0, 0), (1, 0), (0, 1), (1, 1)]

        def pt_at(br, t):
            return 3 * NH * br + (NH if t else 0), NH * (t + 1)

        def up_done(n0, i, j, first):
            return n0 + 2 if first and j == 0 else n0 + 6 * (MOE_STEP * i + j)

        @block.sync
        def _(sp):
            def load(n, src, i=0, per=0):
                if n >= RING or per:
                    sp.wait_ge(S["slot_done"], n - RING + 1 + RING * per * i)
                sp.dma_start(ring[:, n % RING], src).then_inc(slot_ready[n % RING], 16)

            def moe(l):
                n0 = BASE["moe", l]
                eu, ed = a["w_gu"][l], a["w_down"][l]

                def up(n, e, i=0, per=0):
                    for j in range(4):
                        src = eu[e, j] if isinstance(e, int) else eu[bass.ds(e, 1), j].rearrange("a p n -> p (a n)")
                        load(n + j, src, i, per)

                def down(n, e, i=0, per=0):
                    for j in range(2):
                        src = ed[e, j] if isinstance(e, int) else ed[bass.ds(e, 1), j].rearrange("a p n -> p (a n)")
                        load(n + j, src, i, per)
                n = n0
                for e in range(MOE_STEP):
                    up(n, e)
                    n += 4
                    if e:
                        down(n, e - 1)
                        n += 2
                with sp.Fori(1, NE // MOE_STEP) as i:
                    for j in range(MOE_STEP):
                        m = n + 6 * j - 24
                        up(m, i * MOE_STEP + j, i, 3)
                        down(m + 4, i * MOE_STEP + j - 1, i, 3)
                down(n0 + MOE_SLOTS - 2, NE - 1)

            def peer(l):
                n0 = BASE["peer", l] + W2_Q

                def u(n, b, i=0, per=0):
                    src = a["u_t"][l, b] if isinstance(b, int) else a["u_t"][l, bass.ds(b, 1)].rearrange("a p n -> p (a n)")
                    load(n, src, i, per)

                def v(n, b, i=0, per=0):
                    src = a["v_t"][l, :, b] if isinstance(b, int) else a["v_t"][l, :, bass.ds(b, 1)].rearrange("p a n -> p (a n)")
                    load(n, src, i, per)
                n = n0
                for b in range(PEER_STEP):
                    u(n, b)
                    n += 1
                    if b:
                        v(n, b - 1)
                        n += 1
                with sp.Fori(1, PK // PEER_STEP) as i:
                    for j in range(PEER_STEP):
                        m = n + 2 * j - 8
                        u(m, i * PEER_STEP + j, i, 1)
                        v(m + 1, i * PEER_STEP + j - 1, i, 1)
                v(n0 + PEER_SLOTS - 1, PK - 1)

            sp.dma_start(x[:], a["x_fm"]).then_inc(S["x_load"], 16)
            for kind, l in plan:
                n = BASE[kind, l]
                if kind == "mix":
                    for j in range(W1_IN + W1_OUT):
                        load(n + j, a["w1"][l, j])
                elif kind == "nsa":
                    for j in range(W2_IN + W2_OUT):
                        load(n + j, a["w2"][l, j])
                elif kind == "moe":
                    moe(l)
                else:
                    for j in range(W2_Q):
                        load(n + j, a["w2"][l, W2_IN + W2_OUT + j])
                    peer(l)
            sp.wait_ge(S["x_ready"], len(plan))
            sp.dma_start(out, x[:]).then_inc(S["out_st"], 16)
            n_out = 16
            for k, (src, dst) in enumerate(dumps or []):
                sp.dma_start(dst, src).then_inc(S["out_st"], 16)
                n_out += 16
            sp.wait_ge(S["out_st"], n_out)

        @block.gpsimd
        def _(pool):
            def ada(l):
                wk = a["w_ada"][l].rearrange("(k p) (m n) -> k m p n", p=P, n=D)

                def step(k, first):
                    for m in range(NMOD):
                        if not (first and m < 3):
                            pool.wait_ge(S["ada_used"], l * NMOD * KT + NMOD * k + m - 2)
                        src = wk[k, m] if isinstance(k, int) else wk[bass.ds(k, 1), m].rearrange("a p n -> p (a n)")
                        pool.dma_start(ADA["ring"][:, m % 3], src).then_inc(ada_ready[m % 3], 16)
                step(0, l == 0)
                with pool.Fori(1, KT) as k:
                    step(k, False)

            pool.dma_start(ccol[:], a["c_col"]).then_inc(S["col_load"], 16)
            pool.dma_start(cst[:], a["cst"]).then_inc(S["cst_load"], 16)
            pool.dma_start(col1[:], a["col1"]).then_inc(S["col_load"], 16)
            pool.dma_start(col2[:], a["col2"]).then_inc(S["col_load"], 16)
            pool.dma_start(row[:], a["row"]).then_inc(S["row_load"], 16)
            for kind, l in plan:
                s = SIDX[kind, l]
                if kind == "mix":
                    if s:
                        pool.wait_ge(S["x_ready"], s)
                    pool.dma_start(M["wglr"], a["w_glr"][l]).then_inc(S["aux1_load"], 16)
                    pool.dma_start(M["gk2"][0:RANK, :], a["w_gk2"][l]).then_inc(S["aux1_load"], 16)
                    if l == 0:
                        ada(0)
                if kind in ("nsa", "peer"):
                    if s:
                        pool.wait_ge(S["x_ready"], s)
                    if kind == "nsa":
                        pool.dma_start(N["wtm"], a["w_tm"][l]).then_inc(S["tm_load"], 16)
                        pool.dma_start(N["x2"], a["x2"][l]).then_inc(S["x2_load"], 16)
                    else:
                        pool.dma_start(Q["sk"], a["sk_t"][l]).then_inc(S["sk_load"], 16)
                if kind == "moe":
                    pool.wait_ge(S["x_ready"], s)
                    pool.dma_start(E["wr"], a["w_rt"][l]).then_inc(S["rt_load"], 16)
                    pool.wait_ge(S["combt_ev"], l + 1)
                    pool.dma_start(comb_dram[l], E["combT"][0:NE, :]).then_inc(S["comb_st"], 16)
                    pool.wait_ge(S["comb_st"], 16 * (l + 1))
                    pool.dma_start(E["combB"], comb_dram[l].partition_broadcast(P)).then_inc(S["comb_ld"], 16)
                    if l == 0 and ("mix", 1) in plan:
                        ada(1)

        @block.scalar
        def _(act):
            A = nc.scalar.activation

            def norm(s, sq, rs):
                n = NORM[s]
                if SIDX[s]:
                    act.wait_ge(S["x_ready"], SIDX[s])
                else:
                    act.wait_ge(S["x_load"], 16)
                A(sq, x[:], ACT.Square).then_inc(S["norm_sq"], 1)
                act.wait_ge(S["norm_ss"], n + 1)
                A(rs, PS[:, 7, 0:T], ACT.Ln, scale=1.0 / D, bias=EPS)
                act.drain()
                A(rs, rs, ACT.Exp, scale=-0.5).then_inc(S["norm_rs"], 1)

            def mix(l):
                s, n0, p0 = ("mix", l), BASE["mix", l], PAIR["mix", l]
                norm(s, M["sq"], M["rs"])
                act.wait_ge(S["glr_mm"], l + 1)
                A(M["glr"][0:RANK, :], PS[0:RANK, 4, 0:T], ACT.Copy).then_inc(S["glr_ev"], 1)
                dst = [M["qk"][:, 0:2], M["qk"][:, 2:4], M["qk"][:, 4:6], M["qk"][:, 6:8], M["gqk"][:, 0:2],
                       M["gqk"][:, 2:4], M["gr"][:, 0:2], M["gr"][:, 2:4]]
                for j in range(8):
                    act.wait_ge(S["slot_done"], n0 + 2 * j + 2)
                    A(dst[j], PS[:, (p0 + j) % 4, :].rearrange("p (a b) -> p a b", b=T), ACT.Copy).then_inc(S["pair_evac"], 1)
                    if j == 0:
                        act.wait_ge(S["gkz_mm"], l + 1)
                        for q in range(2):
                            A(G["gy"][:, q], PS[:, 5, T * q:T * q + T], ACT.Identity, bias=c1(l, "b_gk", q, 1)).then_inc(S["gkz_ev"], 1)
                        act.drain()
                        b0 = G["b0"].rearrange("p (q c) t -> p q (c t)", q=2)
                        A(b0, G["gy"], ACT.Abs)
                        act.drain()
                        A(b0, b0, ACT.Exp, scale=-1.0)
                        act.drain()
                        A(b0, b0, ACT.Ln, bias=1.0).then_inc(S["gl_ln"], 1)
                act.drain()
                A(M["sq"], M["qk"], ACT.Square).then_inc(S["qk_sq"], 1)
                A(M["gr"], M["gr"], ACT.Silu).then_inc(S["grs"], 1)
                act.wait_ge(S["slot_done"], n0 + 20)
                A(M["sbv"], PS[:, 4:6, :], ACT.Copy).then_inc(S["sbv_ev"], 1)
                act.wait_ge(S["slot_done"], n0 + 24)
                A(M["gv"], PS[:, 6:8, :], ACT.Copy).then_inc(S["gv_ev"], 1)
                act.wait_ge(S["qk_ss"], l + 1)
                A(M["rsq"], PS[:, 0:4, :].rearrange("p a (b c) -> p (a b) c", c=T), ACT.Ln, scale=1.0 / SBD, bias=EPS)
                act.drain()
                A(M["rsq"], M["rsq"], ACT.Exp, scale=-0.5).then_inc(S["qk_rs"], 1)
                for g in range(2):
                    k = 2 * l + g
                    act.wait_ge(S["zm_ok"], k + 1)
                    if k:
                        act.wait_ge(S["lf_ok"], k)
                    A(M["e"], M["zm"], ACT.Abs)
                    act.drain()
                    A(M["e"], M["e"], ACT.Exp, scale=-1.0)
                    act.drain()
                    A(M["e"], M["e"], ACT.Ln, bias=1.0).then_inc(S["ln_ok"], 1)
                    act.wait_ge(S["arg_ok"], k + 1)
                    A(M["w"], M["zm"], ACT.Exp).then_inc(S["w_ok"], 1)
                    act.wait_ge(S["pv_mm"], k + 1)
                    A(M["mixT"][:, 2 * g:2 * g + 2], PS[:, 0:2, 0:T], ACT.Copy).then_inc(S["outa_ev"], 1)
                act.wait_ge(S["gl_b"], l + 1)
                A(G["eb"], G["b0"], ACT.Exp)
                A(G["einv"], G["b0"], ACT.Exp, scale=-1.0).then_inc(S["gl_e1"], 1)
                A(G["eend"], G["b1"], ACT.Exp).then_inc(S["gl_e2"], 1)
                act.wait_ge(S["kend_mm"], l + 1)
                A(G["kend"].rearrange("p a b -> p (a b)"), PS[:, 4, :], ACT.Copy).then_inc(S["kend_ev"], 1)
                act.wait_ge(S["o_mm"], l + 1)
                o2 = M["qk"][:, 0:4]
                A(o2, PS[:, 2:4, :].rearrange("p a (b c) -> p (a b) c", c=T), ACT.Copy)
                A(M["rsq"][:, 0:4], PS[:, 2:4, :].rearrange("p a (b c) -> p (a b) c", c=T), ACT.Square).then_inc(S["o_sq"], 1)
                act.wait_ge(S["o_ss"], l + 1)
                A(M["rsq"][:, 4:8], PS[:, 0:2, :].rearrange("p a (b c) -> p (a b) c", c=T), ACT.Ln, scale=1.0 / GDV, bias=EPS)
                act.drain()
                A(M["rsq"][:, 4:8], M["rsq"][:, 4:8], ACT.Exp, scale=-0.5).then_inc(S["o_rs"], 1)

            def moe(l):
                norm(("moe", l), E["sq"], E["rs"])
                act.wait_ge(S["rt_max"], l + 1)
                for t in range(TT):
                    A(E["gx"][:, t], E["lg"][:, t, 0:NG], ACT.Exp, bias=E["sc"][:, t, 0:1], accum_out=E["sc"][:, t, 1:2])
                A(E["sc"][:, :, 2:3], E["sc"][:, :, 3:4], ACT.Exp).then_inc(S["rt_exp"], 1)
                act.wait_ge(S["comb_mm"], l + 1)
                A(E["combT"][0:NE, :], PS[0:NE, 6, 0:T], ACT.Copy).then_inc(S["combt_ev"], 1)
                u0, n0 = FT * NE * l, BASE["moe", l]

                def step(i, first):
                    for j in range(FT * MOE_STEP):
                        u = u0 + FT * MOE_STEP * i + j
                        act.wait_ge(S["slot_done"], up_done(n0, i, j // 2, first) + 2 * (j % 2))
                        if not (first and j < 4):
                            act.wait_ge(S["hh_ok"], u - 3)
                        A(E["sg"][:, j % 4], PS[:, 4 + j % 4, 0:T], ACT.Silu).then_inc(S["silu_ok"], 1)
                step(0, True)
                with act.Fori(1, NE // MOE_STEP) as i:
                    step(i, False)
                act.wait_ge(S["slot_done"], n0 + MOE_SLOTS)
                A(E["y"].rearrange("p a (b c) -> p (a b) c", c=512), PS[:, 0:4, :], ACT.Copy).then_inc(S["y_ev"], 1)

            def layer_norm(l, q):
                n = LN["peer" if q else "nsa", l]
                act.wait_ge(S["ln_c"], n + 1)
                A(L_["sq"], x[:], ACT.Square).then_inc(S["ln_sq"], 1)
                act.wait_ge(S["ln_ss"], n + 1)
                A(L_["rs"], PS[:, 7, 0:T], ACT.Ln, scale=1.0 / D, bias=LN_EPS)
                act.drain()
                A(L_["rs"], L_["rs"], ACT.Exp, scale=-0.5).then_inc(S["ln_rs"], 1)

            def bank_pair(b):
                return PS[:, b, :].rearrange("p (a b) -> p a b", b=T)

            def nsa(l):
                n0, p0, s = BASE["nsa", l], PAIR["nsa", l], SIDX["nsa", l]
                if s:
                    act.wait_ge(S["x_ready"], s)
                lam = N["lam"]
                A(lam[:, 0], c2(l, "lam"), ACT.Abs)
                act.drain()
                A(lam[:, 1], lam[:, 0], ACT.Exp, scale=-1.0).then_inc(S["lam_e"], 1)
                for j in range(W2_IN // 2):
                    act.wait_ge(S["slot_done"], n0 + 2 * j + 2)
                    for q in range(2):
                        last = A(N["p"][:, 2 * j + q], PS[:, (p0 + j) % 4, T * q:T * q + T], ACT.Identity, bias=c2(l, "b_in", 2 * j + q, 1))
                    last.then_inc(S["pair_evac"], 1)
                act.wait_ge(S["tm_mm"], l + 1)
                A(N["vtm"], PS[:, 4:6, 0:4 * HD], ACT.Copy)
                A(N["gt"], PS[:, 4:6, 4 * HD:TMW], ACT.Sigmoid).then_inc(S["tm_ev"], 1)
                act.wait_ge(S["c1_mm"], l + 1)
                for q, name in ((0, "b1k"), (1, "b1v")):
                    last = A(N["gel"][0:HD, q], PS[0:HD, q, 0:2 * NC], ACT.Gelu_apprx_tanh, bias=c2(l, name)[0:HD])
                last.then_inc(S["c1_ev"], 1)
                act.wait_ge(S["ri_mm"], l + 1)
                for q, (buf, name) in enumerate((("r", "lru_ba"), ("i", "lru_bx"))):
                    for t in range(LT):
                        last = A(N[buf][:, t], PS[:, 4 + 2 * q + t // 2, T * (t % 2):T * (t % 2) + T], ACT.Sigmoid, bias=c2(l, name, t, 1))
                last.then_inc(S["ri_ev"], 1)
                act.wait_ge(S["c2_mm"], l + 1)
                A(N["kc"], PS[:, 0, 0:2 * NC], ACT.Identity, bias=c2(l, "b2k"))
                for j in range(4):
                    last = A(N["vcz"][32 * j:32 * j + 32, j], PS[32 * j:32 * j + 32, 1, 0:HD], ACT.Copy)
                last.then_inc(S["c2_ev"], 1)
                act.wait_ge(S["loga"], l + 1)
                A(N["a0"], N["r"], ACT.Exp)
                A(N["u"], N["r"], ACT.Tanh).then_inc(S["th_ok"], 1)
                act.wait_ge(S["u_in"], l + 1)
                A(N["u"], N["a1"], ACT.Sqrt).then_inc(S["sqrt_ok"], 1)
                A(N["gg"], N["p"][:, 4:8], ACT.Gelu_apprx_tanh).then_inc(S["gelu_g"], 1)
                act.wait_ge(S["cs_max"], l + 1)
                A(N["cs"][:, :, :, 0:NC], N["cs"][:, :, :, 0:NC], ACT.Exp).then_inc(S["cs_exp"], 1)
                act.wait_ge(S["ct_mm"], l + 1)
                A(N["ct"], PS[:, 2, :].rearrange("p (a b) -> p a b", b=P), ACT.Copy).then_inc(S["ct_ev"], 1)
                for u, (br, t) in enumerate(UNITS):
                    k = 4 * l + u
                    sv = N["s0"].rearrange("p a b -> p (a b)")[:, 0:NH * P * (t + 1)]
                    act.wait_ge(S["att_max"], k + 1)
                    A(sv, sv, ACT.Exp).then_inc(S["att_exp"], 1)
                    act.wait_ge(S["att_t"], k + 1)
                    o, nt = pt_at(br, t)
                    A(N["pt"][:, o:o + nt], PS[:, 0:nt // 4, :].rearrange("p a (b c) -> p (a b) c", c=P), ACT.Copy).then_inc(S["att_tev"], 1)
                act.wait_ge(S["nsa_mm"], l + 1)
                act.wait_ge(S["lru_h"], l + 1)
                for t in range(TT):
                    last = A(N["ynsa"][:, :, P * t:P * t + P], PS[:, t, :].rearrange("p (a b) -> p a b", b=P), ACT.Copy)
                last.then_inc(S["nsa_ev"], 1)
                act.wait_ge(S["ylru_ok"], l + 1)
                act.drain()
                A(N["sq"][:, 0:4], N["u"], ACT.Square)
                A(N["sq"][:, 4:8], N["ynsa"], ACT.Square).then_inc(S["g_sq"], 1)
                act.wait_ge(S["g_ss"], l + 1)
                A(N["rs"], PS[:, 7, :], ACT.Ln, scale=1.0 / 512, bias=LN_EPS)
                act.drain()
                A(N["rs"], N["rs"], ACT.Exp, scale=-0.5).then_inc(S["g_rs"], 1)
                layer_norm(l, 0)

            def peer(l):
                n0, p0 = BASE["peer", l], PAIR["peer", l]
                for j in range(W2_Q // 2):
                    act.wait_ge(S["slot_done"], n0 + 2 * j + 2)
                    A(Q["pq"][:, 2 * j:2 * j + 2], bank_pair((p0 + j) % 4), ACT.Copy).then_inc(S["pair_evac"], 1)
                for t in range(TT):
                    act.wait_ge(S["ps_mm"], 2 * l + t + 1)
                    A(Q["s"][:, t], PS[:, 4:8, :].rearrange("p a (b c) -> p (a b) c", c=PK), ACT.Copy).then_inc(S["ps_ev"], 1)
                act.wait_ge(S["pk_top"], l + 1)
                A(Q["cv"], Q["cv"], ACT.Exp).then_inc(S["pk_exp"], 1)
                act.wait_ge(S["pk_t"], l + 1)
                A(egT, PS[:, 0:2, :].rearrange("p a (b c) -> p (a b) c", c=T)[:, 0:3], ACT.Copy).then_inc(S["pk_tev"], 1)

                def evac(i):
                    for j in range(4):
                        act.wait_ge(S["pt_mm"], T * l + 16 * i + 4 * j + 4)
                        o = GT[:, 4 * j:4 * j + 4] if isinstance(i, int) else GT[:, bass.ds(16 * i + 4 * j, 4)]
                        A(o, PS[:, 4 + j, :].rearrange("p (a b) -> p a b", b=PK), ACT.Copy).then_inc(S["g_ev"], 1)
                evac(0)
                with act.Fori(1, T // 16) as i:
                    evac(i)
                n0 += W2_Q

                def step(i, first):
                    for j in range(PEER_STEP):
                        act.wait_ge(S["slot_done"], n0 + 1 if first and j == 0 else n0 + 2 * (PEER_STEP * i + j))
                        if not first:
                            act.wait_ge(S["pw_ok"], PK * l + PEER_STEP * i + j - 3)
                        A(gel[:, j], PS[:, 4 + j, 0:T], ACT.Gelu_apprx_tanh).then_inc(S["gelu_ok"], 1)
                act.wait_ge(S["pt_mm"], T * (l + 1))
                act.drain()
                step(0, True)
                with act.Fori(1, PK // PEER_STEP) as i:
                    step(i, False)
                act.wait_ge(S["slot_done"], n0 + PEER_SLOTS)
                A(L_["y"].rearrange("p a (b c) -> p (a b) c", c=512), PS[:, 0:4, :], ACT.Copy).then_inc(S["y2_ev"], 1)
                layer_norm(l, 1)

            act.wait_ge(S["col_load"], 48)
            A(csil[:], ccol[:], ACT.Silu).then_inc(S["csilu"], 1)
            fns = {"mix": mix, "moe": moe, "nsa": nsa, "peer": peer}
            for kind, l in plan:
                fns[kind](l)

        @block.vector
        def _(dve):
            V = nc.vector

            def ada_step(l, k):
                for m in range(NMOD):
                    if m == 0:
                        dve.drain()
                    dve.wait_ge(ada_ready[m % 3], 16 * (2 * KT * l + 2 * k + m // 3 + 1))
                    ck = csil[:, k:k + 1] if isinstance(k, int) else csil[:, bass.ds(k, 1)]
                    V.scalar_tensor_tensor(ADA["acc"][:, m], ADA["ring"][:, m % 3], ck, ADA["acc"][:, m],
                                           ALU.mult, ALU.add).then_inc(S["ada_used"], 1)

            def ada_clear(l):
                V.memset(ADA["acc"], 0.0)

            def ada_cols(l):
                dve.wait_ge(S["ada_ps"], l + 1)
                V.tensor_tensor(mod[:], PS[:, 6, 0:NMOD * KT], c1(l, "b_ada"), ALU.add)
                dve.drain()
                for q, name in ((0, "norm_mix"), (1, "norm_ffn")):
                    V.scalar_tensor_tensor(ga[:, q], mod[:, 24 * q + 8:24 * q + 16], 1.0, c1(l, name), ALU.add, ALU.mult)
                dve.drain()

            def norm(s, rs, q):
                dve.wait_ge(S["norm_rs"], NORM[s] + 1)
                V.tensor_tensor(h[:], x[:], rs.unsqueeze(1).to_broadcast([P, KT, T]), ALU.mult)
                dve.drain()
                for k in range(KT):
                    last = V.tensor_scalar(h[:, k], h[:, k], ga[:, q, k:k + 1], mod[:, 24 * q + k:24 * q + k + 1],
                                           ALU.mult, ALU.add)
                last.then_inc(S["h_ready"], 1)

            def mix(l):
                s, n0, p0 = ("mix", l), BASE["mix", l], PAIR["mix", l]
                if l == 0:
                    ada_clear(0)
                    dve.wait_ge(S["csilu"], 1)
                    for k in range(KT):
                        ada_step(0, k)
                    dve.drain().then_inc(S["ada_acc"], 1)
                ada_cols(l)
                norm(s, M["rs"], 0)
                dve.wait_ge(S["gl_ln"], l + 1)
                b0, b1 = G["b0"], G["b1"]
                V.scalar_tensor_tensor(b1.rearrange("p (q c) t -> p q (c t)", q=2), G["gy"], 0.0,
                                       b0.rearrange("p (q c) t -> p q (c t)", q=2), ALU.min, ALU.subtract)
                dve.drain()
                V.tensor_scalar(b0, b1, 1.0 / 16.0, None, ALU.mult)
                d, src, dst = 1, b0, b1
                while d < CHUNK:
                    dve.drain()
                    V.tensor_tensor(dst[:, :, d:], src[:, :, d:], src[:, :, :CHUNK - d], ALU.add)
                    last = V.tensor_copy(dst[:, :, :d], src[:, :, :d])
                    src, dst, d = dst, src, 2 * d
                assert src is b0
                dve.drain()
                V.tensor_tensor(b1, b0[:, :, CHUNK - 1:CHUNK].to_broadcast([P, 8, CHUNK]), b0, ALU.subtract).then_inc(S["gl_b"], 1)
                V.memset(G["st"], 0.0)
                dve.wait_ge(S["qk_rs"], l + 1)
                V.scalar_tensor_tensor(M["qkn"][:, 0:4], M["qk"][:, 0:4], c1(l, "q_gain"), M["rsq"][:, 0:4], ALU.mult, ALU.mult)
                V.scalar_tensor_tensor(M["qkn"][:, 4:8], M["qk"][:, 4:8], c1(l, "k_gain"), M["rsq"][:, 4:8],
                                       ALU.mult, ALU.mult).then_inc(S["qkn"], 1)
                sbm = cc("sbmask").unsqueeze(1).to_broadcast([P, 4, 384])
                for g in range(2):
                    k = 2 * l + g
                    dve.wait_ge(S["z_mm"], k + 1)
                    if k:
                        dve.wait_ge(S["w_ok"], k)
                    V.scalar_tensor_tensor(M["zm"], PS[:, 0:4, 0:384], SBD ** -0.5, sbm, ALU.mult, ALU.add).then_inc(S["zm_ok"], 1)
                    dve.wait_ge(S["ln_ok"], k + 1)
                    if k:
                        dve.wait_ge(S["suf_mm"], k)
                    V.scalar_tensor_tensor(M["lf"], M["zm"], 0.0, M["e"], ALU.max, ALU.add).then_inc(S["lf_ok"], 1)
                    dve.wait_ge(S["suf_mm"], k + 1)
                    V.tensor_tensor(M["zm"], PS[:, 4:8, 0:384], M["zm"], ALU.add).then_inc(S["arg_ok"], 1)
                dve.wait_ge(S["gl_e1"], l + 1)
                ch = lambda v: v.rearrange("p (q c) t -> p q (c t)", q=2)
                V.scalar_tensor_tensor(G["qd"], M["gqk"][:, 0:2], GDK ** -0.5, ch(G["eb"]), ALU.mult, ALU.mult)
                V.tensor_tensor(G["ki"], M["gqk"][:, 2:4], ch(G["einv"]), ALU.mult)
                dve.wait_ge(S["gl_e2"], l + 1)
                V.tensor_tensor(G["ke"], M["gqk"][:, 2:4], ch(G["eend"]), ALU.mult).then_inc(S["gl_prod"], 1)
                dve.wait_ge(S["kv_mm"], l + 1)
                st = G["st"]
                for c in range(NCH - 1):
                    for hh in range(GH):
                        o, q = GDK * (hh % 2), hh // 2
                        kv = PS[o:o + GDK, 5 + c, P * q:P * q + P]
                        if c == 0:
                            last = V.tensor_copy(st[o:o + GDK, 0, hh], kv)
                        else:
                            last = V.scalar_tensor_tensor(st[o:o + GDK, c, hh], st[o:o + GDK, c - 1, hh],
                                                          G["eb"][o:o + GDK, 4 * q + c, CHUNK - 1:CHUNK], kv, ALU.mult, ALU.add)
                    if c < NCH - 2:
                        dve.drain()
                last.then_inc(S["states"], 1)
                dve.wait_ge(S["sc_mm"], l + 1)
                V.tensor_tensor(G["sc"], PS[:, 0:2, :].rearrange("p a (b c) -> p (a b) c", c=P),
                                cc("glamask").unsqueeze(1).to_broadcast([P, 8, P]), ALU.mult).then_inc(S["sc_ok"], 1)
                dve.wait_ge(S["o_rs"], l + 1)
                dve.wait_ge(S["grs"], l + 1)
                o2 = M["qk"][:, 0:4]
                V.scalar_tensor_tensor(o2, o2, c1(l, "gla_gain"), M["rsq"][:, 4:8], ALU.mult, ALU.mult)
                dve.drain()
                V.tensor_tensor(M["mixT"][:, 4:8], o2, M["gr"], ALU.mult).then_inc(S["mixb_ok"], 1)
                for j in range(4):
                    dve.wait_ge(S["slot_done"], n0 + W1_IN + 2 * j + 2)
                    for q in range(2):
                        k = 2 * j + q
                        last = V.scalar_tensor_tensor(x[:, k], PS[:, (p0 + 8 + j) % 4, T * q:T * q + T],
                                                      mod[:, 16 + k:17 + k], x[:, k], ALU.mult, ALU.add)
                    last.then_inc(S["pair_evac"], 1)
                dve.drain().then_inc(S["x_ready"], 1)

            def moe(l):
                norm(("moe", l), E["rs"], 1)
                lg, sc = E["lg"], E["sc"]
                V.memset(lg[:, :, NG:8], NEG)
                dve.wait_ge(S["rt_mm"], l + 1)
                rt = PS[:, 6, 0:TT * 64].rearrange("p (a b) -> p a b", b=64)
                V.tensor_copy(lg[:, :, 0:NG], rt[:, :, 0:NG])
                V.tensor_copy(lg[:, :, 8:8 + NE], rt[:, :, NG:NG + NE])
                dve.drain()
                for t in range(TT):
                    V.max(E["gm8"][:, t], lg[:, t, 0:8])
                dve.drain()
                for t in range(TT):
                    V.max_index(gi[:, t], E["gm8"][:, t], lg[:, t, 0:8])
                V.tensor_scalar(sc[:, :, 0:1], E["gm8"][:, :, 0:1], -1.0, None, ALU.mult)
                dve.drain()
                V.tensor_copy(E["gf"], gi[:])
                dve.drain()
                io = lambda n: cc("iota")[:, 0:n].unsqueeze(1).to_broadcast([P, TT, n])
                V.tensor_tensor(E["oh"], io(NG), E["gf"][:, :, 0:1].to_broadcast([P, TT, NG]), ALU.is_equal)
                dve.drain()
                for t in range(TT):
                    ohb = E["oh"][:, t].unsqueeze(2).to_broadcast([P, NG, EPG])
                    V.tensor_tensor(E["tmp"][:, t].rearrange("p (g e) -> p g e", g=NG),
                                    lg[:, t, 8:8 + NE].rearrange("p (g e) -> p g e", g=NG), ohb, ALU.mult)
                dve.drain()
                for t in range(TT):
                    V.tensor_reduce(E["sel"][:, t], E["tmp"][:, t].rearrange("p (g e) -> p e g", g=NG), AX.X, ALU.add)
                dve.drain()
                for t in range(TT):
                    V.max(E["m8"][:, t], E["sel"][:, t])
                dve.drain()
                for t in range(TT):
                    V.max_index(ii[:, t], E["m8"][:, t], E["sel"][:, t])
                V.tensor_tensor(sc[:, :, 3:4], E["m8"][:, :, 1:2], E["m8"][:, :, 0:1], ALU.subtract)
                dve.drain()
                V.tensor_copy(E["if"], ii[:]).then_inc(S["rt_max"], 1)
                dve.wait_ge(S["rt_exp"], l + 1)
                V.tensor_scalar(sc[:, :, 4:5], sc[:, :, 2:3], 1.0, None, ALU.add)
                dve.drain()
                V.tensor_tensor(sc[:, :, 4:5], sc[:, :, 4:5], sc[:, :, 1:2], ALU.mult)
                dve.drain()
                V.reciprocal(sc[:, :, 5:6], sc[:, :, 4:5])
                dve.drain()
                V.tensor_tensor(sc[:, :, 6:7], sc[:, :, 5:6], sc[:, :, 2:3], ALU.mult)
                V.tensor_tensor(E["ew"], io(EPG), E["if"][:, :, 0:1].to_broadcast([P, TT, EPG]), ALU.is_equal)
                V.tensor_tensor(E["o2"], io(EPG), E["if"][:, :, 1:2].to_broadcast([P, TT, EPG]), ALU.is_equal)
                dve.drain()
                V.tensor_tensor(E["ew"], E["ew"], sc[:, :, 5:6].to_broadcast([P, TT, EPG]), ALU.mult)
                V.tensor_tensor(E["o2"], E["o2"], sc[:, :, 6:7].to_broadcast([P, TT, EPG]), ALU.mult)
                dve.drain()
                V.tensor_tensor(E["ew"], E["ew"], E["o2"], ALU.add)
                dve.drain()
                for t in range(TT):
                    last = V.tensor_tensor(E["comb"][:, t].rearrange("p (g e) -> p g e", g=NG),
                                           E["oh"][:, t].unsqueeze(2).to_broadcast([P, NG, EPG]),
                                           E["ew"][:, t].unsqueeze(1).to_broadcast([P, NG, EPG]), ALU.mult)
                last.then_inc(S["comb_ok"], 1)
                with_ada = l == 0 and ("mix", 1) in plan
                if with_ada:
                    ada_clear(1)
                dve.wait_ge(S["comb_ld"], 16 * (l + 1))
                u0 = FT * NE * l

                def step(i, first):
                    for j in range(FT * MOE_STEP):
                        u = u0 + FT * MOE_STEP * i + j
                        dve.wait_ge(S["silu_ok"], u + 1)
                        if not (first and j < 4):
                            dve.wait_ge(S["slot_done"], BASE["moe", l] + 6 * (MOE_STEP * i + j // 2) - 2)
                        V.tensor_tensor(E["t1"][:, j % 4], E["sg"][:, j % 4], PS[:, 4 + j % 4, T:2 * T], ALU.mult)
                        dve.drain()
                        e = MOE_STEP * i + j // 2
                        cb = E["combB"][:, e] if isinstance(e, int) else E["combB"][:, bass.ds(e, 1)].rearrange("p a n -> p (a n)")
                        V.tensor_tensor(E["hh"][:, j % 4], E["t1"][:, j % 4], cb, ALU.mult).then_inc(S["hh_ok"], 1)
                    if with_ada:
                        ada_step(1, i)
                step(0, True)
                with dve.Fori(1, NE // MOE_STEP) as i:
                    step(i, False)
                if with_ada:
                    dve.drain().then_inc(S["ada_acc"], 1)
                dve.wait_ge(S["yt_mm"], l + 1)
                for k in range(KT):
                    last = V.scalar_tensor_tensor(x[:, k], PS[:, 4 + k // 2, T * (k % 2):T * (k % 2) + T],
                                                  mod[:, 40 + k:41 + k], x[:, k], ALU.mult, ALU.add)
                last.then_inc(S["x_ready"], 1)

            def layer_norm(l, q):
                n = LN["peer" if q else "nsa", l]
                dve.wait_ge(S["ln_mu"], n + 1)
                V.scalar_tensor_tensor(x[:], PS[:, 6, 0:T].unsqueeze(1).to_broadcast([P, KT, T]), -1.0 / D, x[:],
                                       ALU.mult, ALU.add).then_inc(S["ln_c"], 1)
                dve.wait_ge(S["ln_rs"], n + 1)
                V.tensor_tensor(x[:], x[:], L_["rs"].unsqueeze(1).to_broadcast([P, KT, T]), ALU.mult)
                dve.drain()
                for k in range(KT):
                    last = V.tensor_scalar(x[:, k], x[:, k], c2(l, f"ln{q + 1}_g", k, 1), c2(l, f"ln{q + 1}_b", k, 1), ALU.mult, ALU.add)
                last.then_inc(S["x_ready"], 1)

            def nsa(l):
                n0, p0 = BASE["nsa", l], PAIR["nsa", l]
                p, xc, lam = N["p"], N["xc"], N["lam"]
                dve.wait_ge(S["lam_e"], l + 1)
                V.tensor_scalar(lam[:, 2], lam[:, 1], 2.0, None, ALU.add)
                V.memset(N["gvr"], 0.0)
                V.memset(N["vcz"], 0.0)
                V.memset(N["cs"], 0.0).then_inc(S["x2_z"], 1)
                dve.drain()
                V.reciprocal(lam[:, 3], lam[:, 2])
                dve.drain()
                V.tensor_tensor(lam[:, 2], lam[:, 1], lam[:, 3], ALU.mult)
                dve.drain()
                V.tensor_tensor(lam[:, 3], lam[:, 2], lam[:, 2], ALU.mult)
                dve.drain()
                V.tensor_scalar(lam[:, 4], lam[:, 3], 1.0 / 19, None, ALU.mult)
                for c in range(17, 1, -2):
                    dve.drain()
                    V.scalar_tensor_tensor(lam[:, 4], lam[:, 4], 1.0 / c, lam[:, 3], ALU.add, ALU.mult)
                dve.drain()
                V.scalar_tensor_tensor(lam[:, 4], lam[:, 4], 1.0, lam[:, 2], ALU.add, ALU.mult)
                V.tensor_scalar(lam[:, 5], c2(l, "lam"), 0.0, 8.0, ALU.min, ALU.mult)
                dve.drain()
                V.scalar_tensor_tensor(lam[:, 4], lam[:, 4], -16.0, lam[:, 5], ALU.mult, ALU.add)
                dve.wait_ge(S["pair_evac"], p0 + 2)
                for t in range(LT):
                    V.tensor_scalar(xc[:, t], p[:, t], c2(l, "conv_w", 3 * LT + t, 1), c2(l, "conv_b", t, 1), ALU.mult, ALU.add)
                for k in range(3):
                    d = 3 - k
                    dve.drain()
                    for t in range(LT):
                        last = V.scalar_tensor_tensor(xc[:, t, d:], p[:, t, 0:T - d], c2(l, "conv_w", k * LT + t, 1), xc[:, t, d:],
                                                      ALU.mult, ALU.add)
                last.then_inc(S["xc_ok"], 1)
                dve.wait_ge(S["pair_evac"], p0 + 8)
                for q, name in ((0, "pos_k"), (1, "pos_v")):
                    for g in range(NKV):
                        for o in range(2):
                            r = slice(HD * o, HD * o + HD)
                            src = p[r, 12 + 2 * q + g, :]
                            win = src[:, o:o + 1].copy()
                            win = bass.AP(win.tensor, win.offset, [win.ap[0], (2, CB // 2), (CS, NC)])
                            pos = c2(l, name)[r].unsqueeze(2).to_broadcast([HD, CB // 2, NC])
                            last = V.tensor_tensor(N["blk"][r, q, :, NC * g:NC * g + NC], win, pos, ALU.add)
                last.then_inc(S["blk_ok"], 1)
                dve.wait_ge(S["c1_ev"], l + 1)
                for j in range(4):
                    g = j // 2
                    last = V.tensor_copy(N["gvr"][0:HD, 32 * j:32 * j + NC], N["gel"][0:HD, 1, NC * g:NC * g + NC])
                last.then_inc(S["att_ok"], 1)
                dve.wait_ge(S["tm_ev"], l + 1)
                for br in range(3):
                    for par in range(2):
                        V.tensor_copy(N["gth"][:, :, br, 4 * par:4 * par + 4], N["gt"][:, :, 3 * par + br:3 * par + br + 19:6])
                dve.wait_ge(S["ri_ev"], l + 1)
                for t in range(LT):
                    last = V.tensor_scalar(N["r"][:, t], N["r"][:, t], lam[:, 4, t:t + 1], None, ALU.mult)
                last.then_inc(S["loga"], 1)
                V.tensor_tensor(N["i"], N["i"], xc, ALU.mult)
                dve.wait_ge(S["th_ok"], l + 1)
                V.tensor_scalar(N["a1"], N["u"], -1.0, 1.0, ALU.mult, ALU.add)
                dve.drain()
                V.reciprocal(N["a1"], N["a1"])
                dve.drain()
                V.scalar_tensor_tensor(N["a1"], N["u"], -2.0, N["a1"], ALU.mult, ALU.mult)
                dve.drain()
                V.tensor_scalar(N["a1"], N["a1"], 1e-30, None, ALU.max).then_inc(S["u_in"], 1)
                cs, st = N["cs"], N["st"]
                dve.wait_ge(S["cs_mm"], l + 1)
                for t in range(TT):
                    for par in range(2):
                        o = CST["alibic"][0] + (t * NH + 4 * par) * NCP
                        al = cst[:, o:o + 4 * NCP].rearrange("p (a b) -> p a b", b=NCP)[:, :, 0:NC]
                        src = PS[:, 2 + par, 64 * t:64 * t + 64].rearrange("p (a b) -> p a b", b=NCP)[:, :, 0:NC]
                        V.scalar_tensor_tensor(cs[:, t, 4 * par:4 * par + 4, 0:NC], src, HD ** -0.5, al, ALU.mult, ALU.add)
                csv = cs.rearrange("p t h c -> p (t h) c")[:, :, 0:NC]
                bc = lambda v, n: v.unsqueeze(2).to_broadcast([P, v.shape[1], n])
                dve.drain()
                V.tensor_reduce(st[:, 0], csv, AX.X, ALU.max)
                dve.drain()
                V.tensor_tensor(csv, csv, bc(st[:, 0], NC), ALU.subtract).then_inc(S["cs_max"], 1)
                dve.wait_ge(S["cs_exp"], l + 1)
                V.tensor_reduce(st[:, 1], csv, AX.X, ALU.add)
                dve.drain()
                V.reciprocal(st[:, 2], st[:, 1])
                dve.drain()
                for t in range(TT):
                    V.scalar_tensor_tensor(st[:, 2, NH * t:NH * t + NH], st[:, 2, NH * t:NH * t + NH], cc("anyc")[:, t:t + 1],
                                           N["gth"][:, t, 0], ALU.mult, ALU.mult)
                dve.drain()
                V.tensor_tensor(csv, csv, bc(st[:, 2], NC), ALU.mult).then_inc(S["cs_ok"], 1)
                for u, (br, t) in enumerate(UNITS):
                    k, nk = 4 * l + u, P * (t + 1)
                    sv = N["s0"].rearrange("p a b -> p (a b)")[:, 0:NH * nk].rearrange("p (a b) -> p a b", b=nk)
                    dve.wait_ge(S["att_mm"], k + 1)
                    if u:
                        dve.wait_ge(S["att_t"], k)
                    V.scalar_tensor_tensor(sv.rearrange("p a b -> p (a b)"), PS[:, 4:6 + 2 * t, :].rearrange("p a b -> p (a b)"), HD ** -0.5, cc(f"alibi{t}"),
                                           ALU.mult, ALU.add)
                    dve.drain()
                    V.tensor_reduce(st[:, 0, 0:NH], sv, AX.X, ALU.max)
                    dve.drain()
                    V.tensor_tensor(sv, sv, bc(st[:, 0, 0:NH], nk), ALU.subtract).then_inc(S["att_max"], 1)
                    dve.wait_ge(S["att_exp"], k + 1)
                    V.tensor_reduce(st[:, 1, 0:NH], sv, AX.X, ALU.add)
                    dve.drain()
                    V.reciprocal(st[:, 2, 0:NH], st[:, 1, 0:NH])
                    dve.drain()
                    V.tensor_tensor(st[:, 2, 0:NH], st[:, 2, 0:NH], N["gth"][:, t, 1 + br], ALU.mult)
                    dve.drain()
                    V.tensor_tensor(sv, sv, bc(st[:, 2, 0:NH], nk), ALU.mult).then_inc(S["lf_ok2"], 1)
                dve.wait_ge(S["sqrt_ok"], l + 1)
                V.tensor_tensor(N["u"], N["u"], N["i"], ALU.mult)
                a0, a1, tmp, d = N["a0"], N["a1"], N["xc"], 1
                while d < T:
                    dve.drain()
                    V.tensor_tensor(tmp[:, :, d:], a0[:, :, d:], N["u"][:, :, 0:T - d], ALU.mult)
                    if 2 * d < T:
                        V.tensor_tensor(a1[:, :, 2 * d:], a0[:, :, 2 * d:], a0[:, :, d:T - d], ALU.mult)
                    dve.drain()
                    V.tensor_tensor(N["u"][:, :, d:], N["u"][:, :, d:], tmp[:, :, d:], ALU.add)
                    a0, a1, d = a1, a0, 2 * d
                dve.drain().then_inc(S["lru_h"], 1)
                dve.wait_ge(S["gelu_g"], l + 1)
                V.tensor_tensor(N["u"], N["u"], N["gg"], ALU.mult).then_inc(S["ylru_ok"], 1)
                dve.wait_ge(S["g_rs"], l + 1)
                for t in range(LT):
                    V.scalar_tensor_tensor(N["mix"][:, t], N["u"][:, t], c2(l, "gn_lru", t, 1), N["rs"][:, 0:T], ALU.mult, ALU.mult)
                for t in range(LT):
                    last = V.scalar_tensor_tensor(N["mix"][:, 4 + t], N["ynsa"][:, t], c2(l, "gn_nsa", t, 1), N["rs"][:, T:2 * T],
                                                  ALU.mult, ALU.mult)
                last.then_inc(S["mix2_ok"], 1)
                for j in range(4):
                    dve.wait_ge(S["slot_done"], n0 + W2_IN + 2 * j + 2)
                    V.scalar_tensor_tensor(x[:, 2 * j:2 * j + 2], x[:, 2 * j:2 * j + 2], ALPHA,
                                           PS[:, (p0 + 10 + j) % 4, :].rearrange("p (a b) -> p a b", b=T), ALU.mult, ALU.add)\
                        .then_inc(S["pair_evac"], 1)
                dve.drain().then_inc(S["z1_ok"], 1)
                layer_norm(l, 0)

            def peer(l):
                n0 = BASE["peer", l] + W2_Q
                v, iu, wk = Q["v"], Q["iu"], Q["wk"]

                def top16(val, idx, src, work, n):
                    for r in range(n):
                        V.max(val[:, r, 0:8], src[:, r])
                    dve.drain()
                    for r in range(n):
                        V.max_index(idx[:, r, 0:8], val[:, r, 0:8], src[:, r])
                        V.match_replace(work[:, r], val[:, r, 0:8], src[:, r], -3e38)
                    dve.drain()
                    for r in range(n):
                        V.max(val[:, r, 8:16], work[:, r])
                    dve.drain()
                    for r in range(n):
                        V.max_index(idx[:, r, 8:16], val[:, r, 8:16], work[:, r])
                    dve.drain()

                hk = lambda w: w.rearrange("p (h k) -> p h k", k=TOPK)
                for t in range(TT):
                    dve.wait_ge(S["ps_ev"], 2 * l + t + 1)
                    top16(v[:, t], iu[:, t], Q["s"][:, t], wk, 2 * PH)
                    V.tensor_copy(Q["si"][:, t], iu[:, t])
                    vv = v[:, t].rearrange("p (h c) k -> p h c k", c=2)
                    V.tensor_tensor(Q["cand"].rearrange("p h (i j) -> p h i j", j=TOPK),
                                    vv[:, :, 0].unsqueeze(3).to_broadcast([P, PH, TOPK, TOPK]),
                                    vv[:, :, 1].unsqueeze(2).to_broadcast([P, PH, TOPK, TOPK]), ALU.add)
                    dve.drain()
                    top16(hk(Q["cv"][:, t]), hk(Q["ciu"][:, t]), Q["cand"], Q["wk2"], PH)
                    V.tensor_copy(Q["sm"][:, t], hk(Q["cv"][:, t])[:, :, 0])
                    V.tensor_scalar(Q["hlu"][:, 0], Q["ciu"][:, t], 4, None, ALU.logical_shift_right)
                    V.tensor_scalar(Q["hlu"][:, 1], Q["ciu"][:, t], 15, None, ALU.bitwise_and)
                    dve.drain()
                    V.tensor_copy(Q["hl"], Q["hlu"])
                    V.tensor_tensor(hk(Q["cv"][:, t]), hk(Q["cv"][:, t]), Q["sm"][:, t].unsqueeze(2).to_broadcast([P, PH, TOPK]), ALU.subtract)
                    dve.drain()
                    for c in range(2):
                        V.tensor_tensor(Q["eq"], Q["hl"][:, c].unsqueeze(2).to_broadcast([P, PH * TOPK, TOPK]),
                                        cc("iota")[:, 0:TOPK].unsqueeze(1).to_broadcast([P, PH * TOPK, TOPK]), ALU.is_equal)
                        dve.drain()
                        eq4 = Q["eq"].rearrange("p (h k) j -> p h k j", k=TOPK)
                        si = Q["si"][:, t].rearrange("p (h c) k -> p h c k", c=2)[:, :, c]
                        V.tensor_tensor(eq4, eq4, si.unsqueeze(2).to_broadcast([P, PH, TOPK, TOPK]), ALU.mult)
                        dve.drain()
                        V.tensor_reduce(Q["ab"][:, t, c], Q["eq"], AX.X, ALU.add)
                        dve.drain()
                dve.drain().then_inc(S["pk_top"], 1)
                dve.wait_ge(S["pk_exp"], l + 1)
                for t in range(TT):
                    V.tensor_reduce(Q["sm"][:, t], hk(Q["cv"][:, t]), AX.X, ALU.add)
                dve.drain()
                V.reciprocal(Q["sm"], Q["sm"])
                dve.drain()
                for t in range(TT):
                    last = V.tensor_tensor(hk(Q["gate"][:, t]), hk(Q["cv"][:, t]), Q["sm"][:, t].unsqueeze(2).to_broadcast([P, PH, TOPK]), ALU.mult)
                last.then_inc(S["pk_ok"], 1)
                dve.wait_ge(S["pk_tev"], l + 1)

                def onehots(i, first):
                    for j in range(16):
                        if not (first and j < 4):
                            dve.wait_ge(S["pt_mm"], T * l + 16 * i + j - 3)
                        col = lambda m: egT[:, m, j:j + 1] if isinstance(i, int) else egT[:, m, bass.ds(16 * i + j, 1)]
                        V.tensor_scalar(OA[:, j % 4], cc("iota"), col(0), col(2), ALU.is_equal, ALU.mult)
                        V.tensor_scalar(OB[:, j % 4], cc("iota"), col(1), None, ALU.is_equal).then_inc(S["pt_a"], 1)
                onehots(0, True)
                with dve.Fori(1, T // 16) as i:
                    onehots(i, False)
                dve.wait_ge(S["g_ev"], T // 4 * (l + 1))

                def step(i, first):
                    for j in range(PEER_STEP):
                        b = PEER_STEP * i + j
                        dve.wait_ge(S["gelu_ok"], PK * l + b + 1)
                        if not first:
                            dve.wait_ge(S["slot_done"], n0 + 2 * b - 5)
                        g = GT[:, :, b] if isinstance(b, int) else GT[:, :, bass.ds(b, 1)].rearrange("p t a -> p (t a)")
                        V.tensor_tensor(pw[:, j], gel[:, j], g, ALU.mult).then_inc(S["pw_ok"], 1)
                step(0, True)
                with dve.Fori(1, PK // PEER_STEP) as i:
                    step(i, False)
                dve.wait_ge(S["y2t"], l + 1)
                V.scalar_tensor_tensor(x[:], x[:], ALPHA, PS[:, 4:8, :].rearrange("p a (b c) -> p (a b) c", c=T), ALU.mult, ALU.add)\
                    .then_inc(S["z2_ok"], 1)
                layer_norm(l, 1)

            fns = {"mix": mix, "moe": moe, "nsa": nsa, "peer": peer}
            dve.wait_ge(S["cst_load"], 16)
            for kind, l in plan:
                fns[kind](l)

        @block.tensor
        def _(pe):
            mm = nc.tensor.matmul

            def norm(s, sq):
                pe.wait_ge(S["norm_sq"], NORM[s] + 1)
                for k in range(KT):
                    last = mm(PS[:, 7, 0:T], ones, sq[:, k], start=k == 0, stop=k == KT - 1)
                last.then_inc(S["norm_ss"], 1)

            def pairs(n0, p0, n, rhs):
                for j in range(n):
                    if p0 + j >= 4:
                        pe.wait_ge(S["pair_evac"], p0 + j - 3)
                    for q in range(2):
                        s = n0 + 2 * j + q
                        wait_slot(pe, s)
                        for k in range(KT):
                            last = mm(PS[:, (p0 + j) % 4, T * q:T * q + T], ring[:, s % RING, P * k:P * k + P], rhs[:, k],
                                      start=k == 0, stop=k == KT - 1)
                        last.then_inc(S["slot_done"], 1)
                    yield j

            def token_major(n0, banks, w):
                for i in range(4):
                    s = n0 + i
                    wait_slot(pe, s)
                    for q in range(2):
                        for t in range(TT):
                            last = mm(PS[:, banks + t, :], h[:, 2 * i + q, P * t:P * t + P], ring[:, s % RING, 512 * q:512 * q + 512],
                                      start=i + q == 0, stop=i == 3 and q == 1)
                    last.then_inc(S["slot_done"], 1)

            def mix(l):
                s, n0, p0 = ("mix", l), BASE["mix", l], PAIR["mix", l]
                pe.wait_ge(S["ada_acc"], l + 1)
                if SIDX[s]:
                    pe.wait_ge(S["x_ready"], SIDX[s])
                for j in range(NMOD * KT):
                    last = mm(PS[:, 6, j:j + 1], ADA["acc"][:, j // KT, P * (j % KT):P * (j % KT) + P], ones[:, 0:1], start=True, stop=True)
                last.then_inc(S["ada_ps"], 1)
                norm(s, M["sq"])
                pe.wait_ge(S["h_ready"], NORM[s] + 1)
                pe.wait_ge(S["aux1_load"], 32 * (l + 1))
                for k in range(KT):
                    last = mm(PS[0:RANK, 4, 0:T], M["wglr"][:, k], h[:, k], start=k == 0, stop=k == KT - 1)
                last.then_inc(S["glr_mm"], 1)
                for j in pairs(n0, p0, 8, h):
                    if j == 0:
                        pe.wait_ge(S["glr_ev"], l + 1)
                        for q in range(2):
                            last = mm(PS[:, 5, T * q:T * q + T], M["gk2"][0:RANK, P * q:P * q + P], M["glr"][0:RANK, :], start=True, stop=True)
                        last.then_inc(S["gkz_mm"], 1)
                pe.wait_ge(S["gkz_ev"], 2 * (l + 1))
                token_major(n0 + 16, 4, None)
                token_major(n0 + 20, 6, None)
                pe.wait_ge(S["qk_sq"], l + 1)
                for j in range(4):
                    last = mm(PS[:, j, :], cc("headblk"), M["sq"][:, 2 * j:2 * j + 2], start=True, stop=True)
                last.then_inc(S["qk_ss"], 1)
                pe.wait_ge(S["qkn"], l + 1)
                q_, k_, v_ = M["qkn"][:, 0:4], M["qkn"][:, 4:8], M["sbv"]
                for g in range(2):
                    k = 2 * l + g
                    if g:
                        pe.wait_ge(S["outa_ev"], k)
                    for i in range(4):
                        hh = 4 * g + i
                        o, t = SBD * (hh % 2), hh // 2
                        mm(PS[:, i, 0:T], k_[o:o + SBD, t, 0:P], q_[o:o + SBD, t, :], start=True, stop=True)
                        last = mm(PS[:, i, T:T + P], k_[o:o + SBD, t, P:T], q_[o:o + SBD, t, P:T], start=True, stop=True)
                    last.then_inc(S["z_mm"], 1)
                    pe.wait_ge(S["lf_ok"], k + 1)
                    if not g:
                        pe.wait_ge(S["gv_ev"], l + 1)
                    if k:
                        pe.wait_ge(S["arg_ok"], k)
                    for i in range(4):
                        mm(PS[:, 4 + i, 0:384], cc("sufneg"), M["lf"][:, i], start=True, stop=False)
                        last = mm(PS[:, 4 + i, P:T], cc("negones"), M["lf"][:, i, T:T + P], start=False, stop=True)
                    last.then_inc(S["suf_mm"], 1)
                    pe.wait_ge(S["w_ok"], k + 1)
                    for i in range(4):
                        hh = 4 * g + i
                        o, b = SBD * (hh % 2), i // 2
                        mm(PS[o:o + SBD, b, 0:T], v_[:, 0, SBD * hh:SBD * hh + SBD], M["w"][:, i, 0:T], start=True, stop=False)
                        last = mm(PS[o:o + SBD, b, P:T], v_[:, 1, SBD * hh:SBD * hh + SBD], M["w"][:, i, T:T + P], start=False, stop=True)
                    last.then_inc(S["pv_mm"], 1)
                pe.wait_ge(S["gl_prod"], l + 1)
                for t in range(TT):
                    for q in range(2):
                        last = nc.tensor.transpose(PS[:, 4, P * (2 * t + q):P * (2 * t + q) + P], G["ke"][:, q, P * t:P * t + P], ident)
                last.then_inc(S["kend_mm"], 1)
                pe.wait_ge(S["outa_ev"], 2 * (l + 1))
                for hh in range(GH):
                    o, q = GDK * (hh % 2), hh // 2
                    for t in range(TT):
                        r = 4 * (hh % 2) + hh // 2 * 2 + t
                        last = mm(PS[:, r // 4, P * (r % 4):P * (r % 4) + P], G["ki"][o:o + GDK, q, P * t:P * t + P],
                                  G["qd"][o:o + GDK, q, P * t:P * t + P], start=True, stop=True)
                last.then_inc(S["sc_mm"], 1)
                pe.wait_ge(S["kend_ev"], l + 1)
                for c in range(NCH - 1):
                    r0, t = CHUNK * (c % 2), c // 2
                    for hh in range(GH):
                        o, q = GDK * (hh % 2), hh // 2
                        last = mm(PS[o:o + GDK, 5 + c, P * q:P * q + P],
                                  G["kend"][r0:r0 + CHUNK, 2 * t + q, o:o + GDK], M["gv"][r0:r0 + CHUNK, t, GDV * hh:GDV * hh + GDV],
                                  start=True, stop=True)
                last.then_inc(S["kv_mm"], 1)
                pe.wait_ge(S["states"], l + 1)
                pe.wait_ge(S["sc_ok"], l + 1)
                for hh in range(GH):
                    o, q = GDK * (hh % 2), hh // 2
                    for t in range(TT):
                        r = 2 * hh + t
                        b, c0 = 2 + r // 4, P * (r % 4)
                        chunks = [c for c in (2 * t, 2 * t + 1) if c]
                        rs = 4 * (hh % 2) + hh // 2 * 2 + t
                        mm(PS[:, b, c0:c0 + P], M["gv"][:, t, GDV * hh:GDV * hh + GDV], G["sc"][:, rs], start=True, stop=False)
                        for c in chunks:
                            last = mm(PS[:, b, c0 + CHUNK * (c % 2):c0 + CHUNK * (c % 2) + CHUNK], G["st"][:, c - 1, hh],
                                      G["qd"][:, q, CHUNK * c:CHUNK * c + CHUNK], start=False, stop=c == chunks[-1])
                last.then_inc(S["o_mm"], 1)
                pe.wait_ge(S["o_sq"], l + 1)
                for b in range(2):
                    last = mm(PS[:, b, :], ones, M["rsq"][:, 2 * b:2 * b + 2], start=True, stop=True)
                last.then_inc(S["o_ss"], 1)
                pe.wait_ge(S["mixb_ok"], l + 1)
                for _ in pairs(n0 + W1_IN, p0 + 8, 4, M["mixT"]):
                    pass

            def moe(l):
                s, n0 = ("moe", l), BASE["moe", l]
                norm(s, E["sq"])
                pe.wait_ge(S["h_ready"], NORM[s] + 1)
                pe.wait_ge(S["rt_load"], 16 * (l + 1))
                pe.wait_ge(S["row_load"], 16)
                for t in range(TT):
                    for k in range(KT):
                        mm(PS[:, 6, 64 * t:64 * t + NG + NE], h[:, k, P * t:P * t + P], E["wr"][:, k], start=k == 0, stop=False)
                    last = mm(PS[:, 6, 64 * t:64 * t + NG + NE], ones[0:1, :], row[:, l, 0:NG + NE], start=False, stop=True)
                last.then_inc(S["rt_mm"], 1)
                pe.wait_ge(S["comb_ok"], l + 1)
                for t in range(TT):
                    last = nc.tensor.transpose(PS[0:NE, 6, P * t:P * t + P], E["comb"][:, t], ident)
                last.then_inc(S["comb_mm"], 1)
                pe.wait_ge(S["combt_ev"], l + 1)

                def up(n, j, u, i=0, per=0, waits=True):
                    for f in range(FT):
                        b = 4 + (2 * j + f) % 4
                        if waits:
                            pe.wait_ge(S["hh_ok"], u + f - 3)
                        for q in range(2):
                            m = n + 2 * f + q
                            wait_slot(pe, m, i, per)
                            for k in range(KT):
                                last = mm(PS[:, b, T * q:T * q + T], ring[:, m % RING, P * k:P * k + P], h[:, k],
                                          start=k == 0, stop=k == KT - 1)
                            last.then_inc(S["slot_done"], 1)

                def down(n, j, u, i=0, per=0, start=False, stop=False):
                    pe.wait_ge(S["hh_ok"], u)
                    for f in range(FT):
                        wait_slot(pe, n + f, i, per)
                        for t in range(TT):
                            for q in range(2):
                                last = mm(PS[:, 2 * t + q, :], E["hh"][:, (2 * j + f) % 4, P * t:P * t + P],
                                          ring[:, (n + f) % RING, 512 * q:512 * q + 512], start=start and f == 0, stop=stop and f == FT - 1)
                        last.then_inc(S["slot_done"], 1)

                n, u0 = n0, FT * NE * l
                for e in range(MOE_STEP):
                    up(n, e, u0 + FT * e, waits=e >= 2)
                    n += 4
                    if e:
                        down(n, e - 1, u0 + FT * e, start=e == 1)
                        n += 2
                with pe.Fori(1, NE // MOE_STEP) as i:
                    for j in range(MOE_STEP):
                        m, u = n + 6 * j - 24, u0 + FT * (MOE_STEP * i + j)
                        up(m, j, u, i, 3)
                        down(m + 4, j - 1 + MOE_STEP, u, i, 3)
                down(n0 + MOE_SLOTS - 2, MOE_STEP - 1, u0 + FT * NE, stop=True)
                pe.wait_ge(S["y_ev"], l + 1)
                for k in range(KT):
                    for t in range(TT):
                        last = nc.tensor.transpose(PS[:, 4 + k // 2, T * (k % 2) + P * t:T * (k % 2) + P * t + P],
                                                   E["y"][:, t, P * k:P * k + P], ident)
                last.then_inc(S["yt_mm"], 1)

            def layer_norm(l, q):
                n = LN["peer" if q else "nsa", l]
                pe.wait_ge(S["z2_ok" if q else "z1_ok"], l + 1)
                for k in range(KT):
                    last = mm(PS[:, 6, 0:T], ones, x[:, k], start=k == 0, stop=k == KT - 1)
                last.then_inc(S["ln_mu"], 1)
                pe.wait_ge(S["ln_sq"], n + 1)
                for k in range(KT):
                    last = mm(PS[:, 7, 0:T], ones, L_["sq"][:, k], start=k == 0, stop=k == KT - 1)
                last.then_inc(S["ln_ss"], 1)

            def nsa(l):
                n0, p0, s = BASE["nsa", l], PAIR["nsa", l], SIDX["nsa", l]
                if s:
                    pe.wait_ge(S["x_ready"], s)
                else:
                    pe.wait_ge(S["x_load"], 16)
                for _ in pairs(n0, p0, W2_IN // 2, x):
                    pass
                pe.wait_ge(S["tm_load"], 16 * (l + 1))
                pe.wait_ge(S["row_load"], 16)
                for t in range(TT):
                    for k in range(KT):
                        mm(PS[:, 4 + t, 0:TMW], x[:, k, P * t:P * t + P], N["wtm"][:, k], start=k == 0, stop=False)
                    last = mm(PS[:, 4 + t, 0:TMW], ones[0:1, :], row[:, l, NG + NE:NG + NE + TMW], start=False, stop=True)
                last.then_inc(S["tm_mm"], 1)
                pe.wait_ge(S["x2_load"], 16 * (l + 1))
                pe.wait_ge(S["pair_evac"], p0 + 10)
                pe.wait_ge(S["blk_ok"], l + 1)

                def w(name, rows=P):
                    o, n = X2[name]
                    return N["x2"][0:rows, o:o + n]
                for q, name in ((0, "w1k"), (1, "w1v")):
                    for m in range(CB // 2):
                        last = mm(PS[0:HD, q, 0:2 * NC], w(name)[:, HD * m:HD * m + HD], N["blk"][:, q, m], start=m == 0, stop=m == CB // 2 - 1)
                last.then_inc(S["c1_mm"], 1)
                pe.wait_ge(S["xc_ok"], l + 1)
                pe.wait_ge(S["tm_ev"], l + 1)
                for q, name in ((0, "wa"), (1, "wx")):
                    for t in range(LT):
                        last = mm(PS[:, 4 + 2 * q + t // 2, T * (t % 2):T * (t % 2) + T], w(name)[:, P * t:P * t + P], N["xc"][:, t],
                                  start=True, stop=True)
                last.then_inc(S["ri_mm"], 1)
                pe.wait_ge(S["att_ok"], l + 1)
                pe.wait_ge(S["x2_z"], l + 1)
                mm(PS[:, 0, 0:2 * NC], w("w2k", HD), N["gel"][0:HD, 0], start=True, stop=True)
                mm(PS[:, 1, 0:HD], N["gvr"][0:HD, :], w("w2v", HD), start=True, stop=False)
                mm(PS[:, 1, 0:HD], ones[0:1, :], row[:, l, NG + NE + TMW:], start=False, stop=True).then_inc(S["c2_mm"], 1)
                pe.wait_ge(S["c2_ev"], l + 1)
                q_ = N["p"][:, 8:12]
                for hh in range(NH):
                    o, j = HD * (hh % 2), hh // 2
                    for t in range(TT):
                        g = hh // REP
                        last = mm(PS[:, 2 + hh % 2, 64 * t + NCP * j:64 * t + NCP * j + NC], q_[o:o + HD, j, P * t:P * t + P],
                                  N["kc"][o:o + HD, NC * g:NC * g + NC], start=True, stop=True)
                last.then_inc(S["cs_mm"], 1)

                def scores(u):
                    br, t = UNITS[u]
                    for hh in range(NH):
                        o, j, g, nk = HD * (hh % 2), hh // 2, hh // REP, P * (t + 1)
                        c0 = (4 * (hh % 2) + j) * nk
                        last = mm(PS[:, 4 + c0 // 512, c0 % 512:c0 % 512 + nk], q_[o:o + HD, j, P * t:P * t + P],
                                  N["p"][o:o + HD, 16 + 2 * br + g, 0:nk], start=True, stop=True)
                    last.then_inc(S["att_mm"], 1)

                pe.wait_ge(S["ri_ev"], l + 1)
                scores(0)
                pe.wait_ge(S["cs_ok"], l + 1)
                for t in range(TT):
                    for par in range(2):
                        last = nc.tensor.transpose(PS[:, 2, P * (2 * t + par):P * (2 * t + par) + P],
                                                   N["cs"][:, t, 4 * par:4 * par + 4].rearrange("p a b -> p (a b)"), ident)
                last.then_inc(S["ct_mm"], 1)
                pe.wait_ge(S["ct_ev"], l + 1)
                for u, (br, t) in enumerate(UNITS):
                    k = 4 * l + u
                    pe.wait_ge(S["lf_ok2"], k + 1)
                    if u + 1 < len(UNITS):
                        scores(u + 1)
                    if u:
                        pe.wait_ge(S["att_tev"], k)
                    sv = N["s0"].rearrange("p a b -> p (a b)")
                    for hp in range(NH):
                        for kt in range(t + 1):
                            i = hp * (t + 1) + kt
                            last = nc.tensor.transpose(PS[:, i // 4, P * (i % 4):P * (i % 4) + P], sv[:, P * i:P * i + P], ident)
                    last.then_inc(S["att_t"], 1)
                pe.wait_ge(S["att_tev"], 4 * (l + 1))
                for t in range(TT):
                    for hh in range(NH):
                        par, j, g = hh % 2, hh // 2, hh // REP
                        dst = PS[HD * par:HD * par + HD, t, P * j:P * j + P]
                        mm(dst, N["vcz"][:, j], N["ct"][:, 2 * t + par], start=True, stop=False)
                        for br in range(2):
                            at_, _ = pt_at(br, t)
                            for kt in range(t + 1):
                                last = mm(dst, N["vtm"][:, kt, HD * (2 * br + g):HD * (2 * br + g) + HD],
                                          N["pt"][:, at_ + (4 * par + j) * (t + 1) + kt], start=False, stop=br == 1 and kt == t)
                last.then_inc(S["nsa_mm"], 1)
                pe.wait_ge(S["g_sq"], l + 1)
                for q in range(2):
                    for t in range(LT):
                        last = mm(PS[:, 7, T * q:T * q + T], ones, N["sq"][:, 4 * q + t], start=t == 0, stop=t == LT - 1)
                last.then_inc(S["g_ss"], 1)
                pe.wait_ge(S["mix2_ok"], l + 1)
                for _ in pairs(n0 + W2_IN, p0 + 10, 4, N["mix"]):
                    pass
                layer_norm(l, 0)

            def peer(l):
                n0, p0, s = BASE["peer", l], PAIR["peer", l], SIDX["peer", l]
                if s:
                    pe.wait_ge(S["x_ready"], s)
                else:
                    pe.wait_ge(S["x_load"], 16)
                for _ in pairs(n0, p0, W2_Q // 2, x):
                    pass
                pe.wait_ge(S["sk_load"], 16 * (l + 1))
                pe.wait_ge(S["pair_evac"], p0 + 8)
                for t in range(TT):
                    if t:
                        pe.wait_ge(S["ps_ev"], 2 * l + 1)
                    for r in range(2 * PH):
                        last = mm(PS[:, 4 + r // 4, P * (r % 4):P * (r % 4) + P], Q["pq"][:, r, P * t:P * t + P], Q["sk"][:, r % 2],
                                  start=True, stop=True)
                    last.then_inc(S["ps_mm"], 1)
                pe.wait_ge(S["pk_ok"], l + 1)
                for m in range(3):
                    for t in range(TT):
                        c0 = T * m + P * t
                        src = Q["gate"][:, t] if m == 2 else Q["ab"][:, t, m]
                        last = nc.tensor.transpose(PS[:, c0 // 512, c0 % 512:c0 % 512 + P], src, ident)
                last.then_inc(S["pk_t"], 1)
                pe.wait_ge(S["ps_ev"], 2 * (l + 1))

                def outer(i, first):
                    for j in range(16):
                        if not first and j % 4 == 0:
                            pe.wait_ge(S["g_ev"], T // 4 * l + 4 * i + j // 4 - 3)
                        pe.wait_ge(S["pt_a"], T * l + 16 * i + j + 1)
                        mm(PS[:, 4 + j // 4, P * (j % 4):P * (j % 4) + P], OA[:, j % 4], OB[:, j % 4], start=True, stop=True)\
                            .then_inc(S["pt_mm"], 1)
                outer(0, True)
                with pe.Fori(1, T // 16) as i:
                    outer(i, False)
                pe.wait_ge(S["g_ev"], T // 4 * (l + 1))
                n0 += W2_Q

                def up(n, j, b, i=0, per=0, waits=True):
                    if waits:
                        pe.wait_ge(S["gelu_ok"], PK * l + b - 3)
                    wait_slot(pe, n, i, per)
                    for k in range(KT):
                        last = mm(PS[:, 4 + j % 4, 0:T], ring[:, n % RING, P * k:P * k + P], x[:, k], start=k == 0, stop=k == KT - 1)
                    last.then_inc(S["slot_done"], 1)

                def down(n, j, b, i=0, per=0, start=False, stop=False):
                    pe.wait_ge(S["pw_ok"], PK * l + b + 1)
                    wait_slot(pe, n, i, per)
                    for t in range(TT):
                        for q in range(2):
                            last = mm(PS[:, 2 * t + q, :], pw[:, j % 4, P * t:P * t + P], ring[:, n % RING, 512 * q:512 * q + 512],
                                      start=start, stop=stop)
                    last.then_inc(S["slot_done"], 1)
                n = n0
                for b in range(PEER_STEP):
                    up(n, b, b, waits=False)
                    n += 1
                    if b:
                        down(n, b - 1, b - 1, start=b == 1)
                        n += 1
                with pe.Fori(1, PK // PEER_STEP) as i:
                    for j in range(PEER_STEP):
                        m, b = n + 2 * j - 8, PEER_STEP * i + j
                        up(m, j, b, i, 1)
                        down(m + 1, j + PEER_STEP - 1, b - 1, i, 1)
                down(n0 + PEER_SLOTS - 1, PEER_STEP - 1, PK - 1, stop=True)
                pe.wait_ge(S["y2_ev"], l + 1)
                for k in range(KT):
                    for t in range(TT):
                        last = nc.tensor.transpose(PS[:, 4 + k // 2, T * (k % 2) + P * t:T * (k % 2) + P * t + P],
                                                   L_["y"][:, t, P * k:P * k + P], ident)
                last.then_inc(S["y2t"], 1)
                layer_norm(l, 1)

            pe.wait_ge(S["cst_load"], 16)
            fns = {"mix": mix, "moe": moe, "nsa": nsa, "peer": peer}
            for kind, l in plan:
                fns[kind](l)


def _cst():
    c = np.zeros((P, CST_N), np.float32)

    def put(name, v):
        o, n = CST[name]
        c[:, o:o + n] = v.reshape(P, n)
    i, j = np.arange(P)[:, None], np.arange(P)[None, :]
    put("ident", (i == j).astype(np.float32))
    put("ones", np.ones((P, P), np.float32))
    put("headblk", (i // 64 == j // 64).astype(np.float32))
    put("sufneg", -(i >= j).astype(np.float32))
    put("negones", -np.ones((P, P), np.float32))
    before = np.where(i < j, 0.0, NEG)
    put("sbmask", np.concatenate([before, np.zeros((P, P)), before], 1))
    put("glamask", ((i // CHUNK == j // CHUNK) & (i <= j)).astype(np.float32))
    put("iota", np.broadcast_to(np.arange(P, dtype=np.float32), (P, P)))
    slopes = np.array([2.0 ** (-8.0 * (k + 1) / NH) for k in range(NH)], np.float32)
    slopes = np.concatenate([slopes[0::2], slopes[1::2]])
    for t in range(TT):
        q = P * t + np.arange(P)[:, None, None]
        k = np.arange(P * (t + 1))[None, None, :]
        put(f"alibi{t}", np.where(k <= q, -slopes[None, :, None] * np.abs(q - k), NEG).astype(np.float32))
    q = (P * np.arange(TT)[None, :] + np.arange(P)[:, None])[:, :, None, None]
    e = np.arange(NCP) * CS + CB - 1
    e = np.where(np.arange(NCP) < NC, e, 1 << 20)[None, None, None, :]
    put("alibic", np.where(e <= q, -slopes[None, None, :, None] * np.abs(q - e), NEG).astype(np.float32))
    put("anyc", (q[:, :, 0, 0] >= CB - 1).astype(np.float32))
    return c


def _cols(items, table, width):
    c = np.zeros((P, DEPTH, width), np.float32)
    for name, v in items.items():
        o, n = table[name]
        c[:, :, o:o + n] = v
    return c


def _tiles(w):
    L, _, n = w.shape
    return w.reshape(L, KT, P, n // P, P).transpose(0, 3, 2, 1, 4).reshape(L, n // P, P, SLOT)


def _rows(w):
    L = w.shape[0]
    return w.reshape(L, 4, 2, P, 512).transpose(0, 1, 3, 2, 4).reshape(L, 4, P, SLOT)


def _col(v):
    return v.reshape(v.shape[0], -1, P).transpose(2, 0, 1)


def kernel(**inputs):
    import concourse.bacc as _bacc
    from concourse.bass_utils import run_bass_kernel_spmd as _run
    i = {k: np.asarray(v) for k, v in inputs.items()}
    L = DEPTH
    w_in = i["w_in"]
    dup = lambda v: np.concatenate([v, v], -1)
    fm = np.concatenate([w_in[:, :, 0:1024], w_in[:, :, 1536:2048], w_in[:, :, 2560:3072]], 2)
    a = {
        "x_fm": i["x"][0].reshape(T, KT, P).transpose(2, 1, 0),
        "c_col": i["c"][0].reshape(KT, P).T,
        "cst": _cst(),
        "w_ada": i["w_ada"],
        "w1": np.concatenate([_tiles(fm), _rows(w_in[:, :, 1024:1536]), _rows(w_in[:, :, 2048:2560]), _tiles(i["w_out"])], 1),
        "w_glr": w_in[:, :, 3072:].reshape(L, KT, P, RANK).transpose(0, 2, 1, 3),
        "w_gk2": i["w_gk2"],
        "col1": _cols({
            "norm_mix": _col(i["norm_mix"]), "norm_ffn": _col(i["norm_ffn"]), "b_ada": _col(i["b_ada"]), "b_gk": _col(i["b_gk"]),
            "q_gain": _col(dup(i["q_gain"])), "k_gain": _col(dup(i["k_gain"])), "gla_gain": _col(i["gla_gain"]),
        }, C1, C1_N),
        "w_rt": np.concatenate([i["w_router_grp"], i["w_router_exp"]], 2).reshape(L, KT, P, NG + NE).transpose(0, 2, 1, 3),
    }
    gu = np.stack([i["w_gate"].reshape(L, NE, D, FE), i["w_up"].reshape(L, NE, D, FE)], 2)
    a["w_gu"] = gu.reshape(L, NE, 2, KT, P, FT, P).transpose(0, 1, 5, 2, 4, 3, 6).reshape(L, NE, 4, P, SLOT)
    a["w_down"] = i["w_down"].reshape(L, NE, FT, P, D)
    u = i["peer_u_2"].reshape(L, PK, PK, KT, P)
    a["u_t"] = u.transpose(0, 2, 4, 3, 1).reshape(L, PK, P, SLOT)
    a["v_t"] = i["peer_v_2"].reshape(L, PK, PK, D)
    w2, b2 = i["w_in_2"], i["b_in_2"]

    def fm2(w):
        t = [w[..., 0:1536]]
        for o in (1536, 1664, 1792, 2048):
            for g in range(NKV):
                t.append(dup(w[..., o + HD * g:o + HD * g + HD]))
        return np.concatenate(t, -1)

    def tm2(w):
        return np.concatenate([w[..., 1920:2048], w[..., 2176:2328]], -1)
    a["w2"] = np.concatenate([_tiles(fm2(w2)), _tiles(i["w_out_2"]), _tiles(i["peer_wq_2"])], 1)
    a["w_tm"] = tm2(w2).reshape(L, KT, P, TMW).transpose(0, 2, 1, 3)
    a["row"] = np.concatenate([i["b_router_grp"], i["b_router_exp"], tm2(b2), i["cmpv_b2_2"]], -1)[None]
    pad = lambda v: np.concatenate([v, np.zeros_like(v)], -1)
    pos = lambda v: v.reshape(L, CB // 2, 2 * HD).transpose(2, 0, 1)
    a["col2"] = _cols({
        "b_in": _col(fm2(b2)), "conv_w": i["conv_w_2"].reshape(L, 4, LT, P).transpose(3, 0, 1, 2).reshape(P, L, 16),
        "conv_b": _col(i["conv_b_2"]), "lru_ba": _col(i["lru_ba_2"]), "lru_bx": _col(i["lru_bx_2"]), "lam": _col(i["lru_lambda_2"]),
        "gn_lru": _col(i["gn_lru_g_2"]), "gn_nsa": _col(i["gn_nsa_g_2"]), "ln1_g": _col(i["ln1_g_2"]), "ln1_b": _col(i["ln1_b_2"]),
        "ln2_g": _col(i["ln2_g_2"]), "ln2_b": _col(i["ln2_b_2"]), "b1k": _col(pad(i["cmpk_b1_2"])), "b1v": _col(pad(i["cmpv_b1_2"])),
        "b2k": _col(dup(i["cmpk_b2_2"])), "pos_k": pos(i["cmp_pos_k_2"]), "pos_v": pos(i["cmp_pos_v_2"]),
    }, C2, C2_N)
    x2 = np.zeros((L, P, X2_N), np.float32)

    def put(name, v, rows=P):
        o, n = X2[name]
        x2[:, :rows, o:o + n] = v.reshape(L, rows, n)
    w1 = lambda v: v.reshape(L, 16, P, HD).transpose(0, 2, 1, 3)
    put("w1k", w1(i["cmpk_w1_2"]))
    put("w1v", w1(i["cmpv_w1_2"]))
    put("w2k", dup(i["cmpk_w2_2"]), HD)
    put("w2v", i["cmpv_w2_2"], HD)
    for name in ("wa", "wx"):
        blk = np.zeros((L, P, LT, P), np.float32)
        w = i[f"lru_{name}_2"]
        for t in range(LT):
            for q in range(2):
                blk[:, 64 * q:64 * q + 64, t, 64 * q:64 * q + 64] = w[:, 2 * t + q]
        put(name, blk)
    a["x2"] = x2
    a["sk_t"] = i["peer_subkeys_2"].transpose(0, 3, 1, 2)
    nc = _bacc.Bacc("TRN2", target_bir_lowering=False, num_devices=1)
    a = {k: np.ascontiguousarray(v) for k, v in a.items()}
    aps = {k: nc.dram_tensor(f"in_{k}", v.shape, F32, kind="ExternalInput").ap() for k, v in a.items()}
    out = nc.dram_tensor("out_fm", (P, KT, T), F32, kind="ExternalOutput").ap()
    program(nc, aps, out)
    r = _run(nc, [{f"in_{k}": v for k, v in a.items()}], core_ids=[0])
    return r.results[0]["out_fm"].transpose(2, 1, 0).reshape(1, T, D)
```

```python
import math
from contextlib import ExitStack

import numpy as np
import concourse.bass as bass
from concourse import mybir

F32 = mybir.dt.float32
U32 = mybir.dt.uint32
F32R = mybir.dt.float32r
ACT = mybir.ActivationFunctionType
ALU = mybir.AluOpType
AX = mybir.AxisListType

P = 128
D = 1024
KT = D // P
T = 256
TT = T // P
DEPTH = 2
NMOD = 6
SBH, SBD = 8, 64
GH, GDK, GDV, RANK, CHUNK = 4, 64, 128, 16, 64
NCH = T // CHUNK
NG, EPG = 4, 8
NE = NG * EPG
FE = 256
FT = FE // P
EPS = 1e-6
LT = 4
HD, NH, NKV, REP = 64, 8, 2, 4
CB, CS = 32, 16
NC = (T - CB) // CS + 1
NCP = 16
PH, PK, TOPK = 8, 128, 16
LN_EPS = 1e-5
ALPHA = (2 * DEPTH) ** 0.25
NEG = -1e30
SLOT = 1024
RING = 4
TMW = 2 * NKV * HD + NH * 3

W1_IN, W1_OUT = 24, 8
MOE_SLOTS = 6 * NE
W2_IN, W2_OUT, W2_Q = 20, 8, 16
PEER_SLOTS = 2 * PK
MOE_STEP = 4
PEER_STEP = 4

def _layout(items):
    at, out = 0, {}
    for name, n in items:
        out[name] = (at, n)
        at += n
    return out, at


CST, CST_N = _layout([
    ("ident", P), ("ones", P), ("headblk", P), ("sufneg", P), ("negones", P), ("glamask", P), ("iota", P), ("anyc", TT),
])
TAB, TAB_N = _layout([("sbmask", 384), ("alibi0", NH * P), ("alibi1", NH * T), ("alibic", TT * NH * NCP)])
C1, C1_N = _layout([
    ("norm_mix", 8), ("norm_ffn", 8), ("b_ada", 48), ("b_gk", 2), ("q_gain", 1), ("k_gain", 1), ("gla_gain", 1),
])
C2, C2_N = _layout([
    ("b_in", W2_IN), ("conv_w", 16), ("conv_b", LT), ("lru_ba", LT), ("lru_bx", LT), ("lam", LT), ("gn_lru", LT),
    ("gn_nsa", LT), ("ln1_g", 8), ("ln1_b", 8), ("ln2_g", 8), ("ln2_b", 8), ("b1k", 1), ("b1v", 1), ("b2k", 1),
    ("pos_k", CB // 2), ("pos_v", CB // 2),
])
CMPW = 16 * HD
X2, X2_N = _layout([("w1k", CMPW), ("w1v", CMPW), ("w2k", 2 * HD), ("w2v", HD), ("wa", LT * P), ("wx", LT * P)])

SEMS = """x_load cst_load col_load row_load slot_done ada_used ada_acc ada_ps ada_col csilu pair_evac x_ready norm_sq
norm_ss norm_rs h_ready aux1_load glr_mm glr_ev gkz_mm gkz_ev sbv_ev gv_ev qk_sq qk_ss qk_rs qkn z_mm zm_ok
ln_ok lf_ok suf_mm arg_ok w_ok pv_mm outa_ev gl_ln gl_b gl_e1 gl_e2 gl_prod kend_mm kend_ev kv_mm states sc_mm
sc_ok o_mm o_sq o_ss o_rs grs mixb_ok rt_load rt_mm rt_max rt_exp comb_ok comb_mm combt_ev comb_st comb_ld
silu_ok hh_ok y_ev yt_mm tm_load x2_load pads_zero tm_mm tm_ev xc_ok ri_mm ri_ev lam_e loga th_ok u_in sqrt_ok
lru_h gelu_g ylru_ok blk_ok c1_mm c1_ev c2_mm c2_ev cs_mm cs_max cs_exp cs_ok ct_mm ct_ev att_mm att_max
att_exp gvr_ok att_t att_tev nsa_mm nsa_ev g_sq g_ss g_rs mix2_ok z1_ok ln_mu ln_c ln_sq ln_ss ln_rs sk_load
ps_mm ps_ev pk_exp pk_top pk_t pk_tev pt_a pt_mm g_ev y2t z2_ok pk_ok p_ok gelu_ok pw_ok tab_load hi_done
lo_done hs_ok xs_ok y2_ev out_st""".split()


def program(nc, a, out, plan=None, dumps=None):
    plan = plan or [("mix", 0), ("moe", 0), ("mix", 1), ("moe", 1), ("nsa", 0), ("peer", 0), ("nsa", 1), ("peer", 1)]
    ctx = ExitStack()
    with ctx:
        def sb(name, shape, dt=F32):
            return ctx.enter_context(nc.sbuf_tensor(name, shape, dt))

        S = {n: ctx.enter_context(nc.semaphore(n)) for n in SEMS}
        slot_ready = [ctx.enter_context(nc.semaphore(f"slot_ready{i}")) for i in range(RING)]
        ada_ready = [ctx.enter_context(nc.semaphore(f"ada_ready{i}")) for i in range(3)]

        place = {}
        for name in ("arena", "x", "h"):
            at = -(-nc.sbuf_base // 32) * 32
            place[name] = (at, sb(name, [P, 32768] if name == "arena" else [P, KT, T]))
        arena, x, h = (place[n][1] for n in ("arena", "x", "h"))

        def rounded(name, base, at, dims):
            return nc.alloc_sbuf_tensor_at(name, [P, *dims], F32R, offset=place[base][0] + 4 * at)

        ring = sb("ring", [P, RING, SLOT])
        w_hi = sb("w_hi", [P, RING, SLOT], F32R)
        w_lo = sb("w_lo", [P, RING, SLOT], F32R)
        pb = sb("pb", [P, 2, T])
        pw_hi = sb("pw_hi", [P, 2, T], F32R)
        pw_lo = sb("pw_lo", [P, 2, T], F32R)
        cst = sb("cst", [P, CST_N])
        col1 = sb("col1", [P, DEPTH, C1_N])
        col2 = sb("col2", [P, DEPTH, C2_N])
        row = sb("row", [1, DEPTH, NG + NE + TMW + HD])
        ccol = sb("ccol", [P, KT])
        csil = sb("csil", [P, KT])
        mod = sb("mod", [P, NMOD * KT])
        ga = sb("ga", [P, 2, KT])
        PS = ctx.enter_context(nc.psum_tensor("PS", [P, 8, 512], F32))
        comb_dram = nc.dram_tensor("comb_scratch", (DEPTH, NE, T), F32, kind="Internal").ap()

        def cc(name):
            o, n = CST[name]
            return cst[:, o:o + n]

        def c1(l, name, j=0, n=None):
            o, m = C1[name]
            return col1[:, l, o + j:o + (m if n is None else j + n)]

        def c2(l, name, j=0, n=None):
            o, m = C2[name]
            return col2[:, l, o + j:o + (m if n is None else j + n)]

        def area(names, at=0):
            got = {}
            for name, dims in names:
                n = int(np.prod(dims))
                v = arena[:, at:at + n]
                if len(dims) == 2:
                    v = v.rearrange("p (a b) -> p a b", b=dims[1])
                if len(dims) == 3:
                    v = v.rearrange("p (a b c) -> p a b c", b=dims[1], c=dims[2])
                got[name] = v
                at += n
            assert at <= 32768, at
            return got

        ident, ones = cc("ident"), cc("ones")
        ADA = area([("acc", (NMOD, D)), ("ring", (3, D))], 32768 - 9 * D)
        M = area([
            ("qk", (8, T)), ("qkn", (8, T)), ("gqk", (4, T)), ("gr", (4, T)), ("sbv", (TT, 512)), ("gv", (TT, 512)),
            ("sq", (8, T)), ("rsq", (8, T)), ("zm", (4, 384)), ("e", (4, 384)), ("lf", (4, 384)), ("w", (4, 384)),
            ("wglr", (KT, RANK)), ("gk2", (2 * P,)), ("glr", (T,)), ("rs", (T,)), ("mixT", (KT, T)),
            ("sbmask", (384,)),
        ])
        G = area([
            ("gy", (2, T)), ("b0", (8, CHUNK)), ("b1", (8, CHUNK)), ("eb", (8, CHUNK)), ("einv", (8, CHUNK)),
            ("eend", (8, CHUNK)), ("qd", (2, T)), ("ki", (2, T)), ("ke", (2, T)), ("kend", (4, P)), ("sc", (8, P)),
            ("st", (NCH - 1, GH, GDV)),
        ], 21760)
        E = area([
            ("rs", (T,)), ("sq", (8, T)), ("comb", (TT, NE)), ("combT", (T,)), ("combB", (NE, T)), ("sg", (4, T)),
            ("t1", (4, T)), ("hh_hi", (4, T)), ("hh_lo", (4, T)), ("h_hi", (KT, T)), ("h_lo", (KT, T)), ("y", (TT, D)), ("lg", (TT, 40)), ("gm8", (TT, 8)), ("sel", (TT, 8)),
            ("m8", (TT, 8)), ("oh", (TT, NG)), ("tmp", (TT, NE)), ("ew", (TT, 8)), ("o2", (TT, 8)), ("sc", (TT, 8)),
            ("gf", (TT, 8)), ("if", (TT, 8)), ("wr", (KT, NG + NE)), ("gx", (TT, NG)),
        ])
        N = area([
            ("p", (W2_IN, T)), ("wtm", (KT, TMW)), ("x2", (X2_N,)), ("vtm", (TT, 4 * HD)), ("gt", (TT, 3 * NH)),
            ("gth", (TT, 3, NH)), ("xc", (LT, T)), ("r", (LT, T)), ("i", (LT, T)), ("a0", (LT, T)), ("a1", (LT, T)),
            ("u", (LT, T)), ("gg", (LT, T)), ("lam", (6, LT)), ("blk", (2, CB // 2, 2 * NC)), ("gel", (2, 2 * NC)),
            ("gvr", (P,)), ("kc", (2 * NC,)), ("vcz", (4, HD)), ("cs", (TT, NH, 32)), ("ct", (4, P)), ("st", (3, TT * NH)),
            ("s0", (NH, T)), ("pt", (6 * NH, P)),
            ("tab", (TAB_N - 384,)),
        ])
        N["mix"] = arena[:, 5120:7168].rearrange("p (a b) -> p a b", b=T)
        N["ynsa"] = N["a0"]
        N["sq"] = N["s0"]
        N["rs"] = N["blk"].rearrange("p a m c -> p (a m c)")[:, 0:2 * T]
        L_ = area([("sq", (KT, T)), ("rs", (T,)), ("y", (TT, D))], 16384)
        Q = area([
            ("sk", (2, PK)), ("pq", (2 * PH, T)), ("s", (TT, 2 * PH, PK)), ("wk", (2 * PH, PK)), ("v", (TT, 2 * PH, TOPK)),
            ("si", (TT, 2 * PH, TOPK)), ("cand", (PH, TOPK * TOPK)), ("wk2", (PH, TOPK * TOPK)), ("cv", (TT, PH * TOPK)),
            ("hl", (2, PH * TOPK)), ("eq", (PH * TOPK, TOPK)), ("ab", (TT, 2, PH * TOPK)), ("sm", (TT, PH)), ("gate", (TT, PH * TOPK)),
            ("iu", (TT, 2 * PH, TOPK)), ("ciu", (TT, PH * TOPK)), ("hlu", (2, PH * TOPK)),
        ])
        for name in ("iu", "ciu", "hlu"):
            Q[name] = Q[name].bitcast(U32)
        GT = arena[:, 0:T * PK].rearrange("p (t b) -> p t b", b=PK)
        hw = h[:].rearrange("p a b -> p (a b)")
        egT = hw[:, 0:3 * T].rearrange("p (a b) -> p a b", b=T)
        OA = hw[:, 3 * T:3 * T + 4 * PK].rearrange("p (a b) -> p a b", b=PK)
        OB = hw[:, 3 * T + 4 * PK:3 * T + 8 * PK].rearrange("p (a b) -> p a b", b=PK)
        for name in ("hh_hi", "hh_lo", "h_hi", "h_lo"):
            E[name] = rounded(name, "arena", E[name].offset, E[name].shape[1:])
        x_hi, x_lo = rounded("x_hi", "h", 0, [KT, T])[:], rounded("x_lo", "x", 0, [KT, T])[:]
        gi = sb("gi", [P, TT, 8], U32)
        ii = sb("ii", [P, TT, 8], U32)

        block = ctx.enter_context(nc.Block())

        def slot_base():
            at, got = 0, {}
            for k, l in plan:
                got[k, l] = at
                at += {"mix": W1_IN + W1_OUT, "moe": MOE_SLOTS, "nsa": W2_IN + W2_OUT, "peer": W2_Q + PEER_SLOTS}[k]
            return got, at

        BASE, _ = slot_base()
        BASE_SPLIT = {s: BASE[s] + (W2_Q if s[0] == "peer" else 0) for s in plan if s[0] in ("moe", "peer")}

        def i_pos(i):
            return not isinstance(i, int)

        def after_split(n):
            for s, b in BASE_SPLIT.items():
                if b <= n < b + (MOE_SLOTS if s[0] == "moe" else PEER_SLOTS):
                    return s
            return None
        PAIR, at = {}, 0
        for k, l in plan:
            PAIR[k, l] = at
            at += {"mix": 12, "moe": 0, "nsa": 14, "peer": 8}[k]
        SIDX = {s: i for i, s in enumerate(plan)}
        TABS = {s: i for i, s in enumerate([s for s in plan if s[0] in ("mix", "nsa")])}
        SPLIT, at = {}, 0
        for k, l in plan:
            SPLIT[k, l] = at
            at += {"moe": MOE_SLOTS, "peer": PEER_SLOTS}.get(k, 0)
        LN = {s: i for i, s in enumerate([s for s in plan if s[0] in ("nsa", "peer")])}
        NORM = {s: i for i, s in enumerate([s for s in plan if s[0] in ("mix", "moe")])}

        def wait_slot(eng, n, i=0, per=0):
            eng.wait_ge(slot_ready[n % RING], 16 * (n // RING + 1) + 16 * per * i)

        UNITS = [(0, 0), (1, 0), (0, 1), (1, 1)]

        def pt_at(br, t):
            return 3 * NH * br + (NH if t else 0), NH * (t + 1)

        def up_done(n0, i, j, first):
            return n0 + 2 if first and j == 0 else n0 + 6 * (MOE_STEP * i + j)

        @block.sync
        def _(sp):
            def load(n, src, i=0, per=0, split=None):
                if split and (per or n - RING >= BASE_SPLIT[split]):
                    sp.wait_ge(S["lo_done"], SPLIT[split] + n - RING - BASE_SPLIT[split] + 1 + RING * per * i)
                elif after_split(n - RING):
                    kind = after_split(n - RING)
                    sp.wait_ge(S["lo_done"], SPLIT[kind] + n - RING - BASE_SPLIT[kind] + 1)
                elif n >= RING:
                    sp.wait_ge(S["slot_done"], n - RING + 1)
                sp.dma_start(ring[:, n % RING], src).then_inc(slot_ready[n % RING], 16)

            def moe(l):
                n0 = BASE["moe", l]
                eu, ed = a["w_gu"][l], a["w_down"][l]

                def up(n, e, i=0, per=0):
                    for j in range(4):
                        src = eu[e, j] if isinstance(e, int) else eu[bass.ds(e, 1), j].rearrange("a p n -> p (a n)")
                        load(n + j, src, i, per, ("moe", l))

                def down(n, e, i=0, per=0):
                    for j in range(2):
                        src = ed[e, j] if isinstance(e, int) else ed[bass.ds(e, 1), j].rearrange("a p n -> p (a n)")
                        load(n + j, src, i, per, ("moe", l))
                n = n0
                for e in range(MOE_STEP):
                    up(n, e)
                    n += 4
                    if e:
                        down(n, e - 1)
                        n += 2
                with sp.Fori(1, NE // MOE_STEP) as i:
                    for j in range(MOE_STEP):
                        m = n + 6 * j - 24
                        up(m, i * MOE_STEP + j, i, 6)
                        down(m + 4, i * MOE_STEP + j - 1, i, 6)
                down(n0 + MOE_SLOTS - 2, NE - 1)

            def peer(l):
                n0 = BASE["peer", l] + W2_Q

                def u(n, b, i=0, per=0):
                    src = a["u_t"][l, b] if isinstance(b, int) else a["u_t"][l, bass.ds(b, 1)].rearrange("a p n -> p (a n)")
                    load(n, src, i, per, ("peer", l))

                def v(n, b, i=0, per=0):
                    src = a["v_t"][l, :, b] if isinstance(b, int) else a["v_t"][l, :, bass.ds(b, 1)].rearrange("p a n -> p (a n)")
                    load(n, src, i, per, ("peer", l))
                n = n0
                for b in range(PEER_STEP):
                    u(n, b)
                    n += 1
                    if b:
                        v(n, b - 1)
                        n += 1
                with sp.Fori(1, PK // PEER_STEP) as i:
                    for j in range(PEER_STEP):
                        m = n + 2 * j - 8
                        u(m, i * PEER_STEP + j, i, 2)
                        v(m + 1, i * PEER_STEP + j - 1, i, 2)
                v(n0 + PEER_SLOTS - 1, PK - 1)

            sp.dma_start(x[:], a["x_fm"]).then_inc(S["x_load"], 16)
            for kind, l in plan:
                n = BASE[kind, l]
                if kind == "mix":
                    for j in range(W1_IN + W1_OUT):
                        load(n + j, a["w1"][l, j])
                elif kind == "nsa":
                    for j in range(W2_IN + W2_OUT):
                        load(n + j, a["w2"][l, j])
                elif kind == "moe":
                    moe(l)
                else:
                    for j in range(W2_Q):
                        load(n + j, a["w2"][l, W2_IN + W2_OUT + j])
                    peer(l)
            sp.wait_ge(S["x_ready"], len(plan))
            sp.dma_start(out, x[:]).then_inc(S["out_st"], 16)
            n_out = 16
            for k, (src, dst) in enumerate(dumps or []):
                sp.dma_start(dst, src).then_inc(S["out_st"], 16)
                n_out += 16
            sp.wait_ge(S["out_st"], n_out)

        @block.gpsimd
        def _(pool):
            def ada(l):
                wk = a["w_ada"][l].rearrange("(k p) (m n) -> k m p n", p=P, n=D)

                def step(k, first):
                    for m in range(NMOD):
                        if not (first and m < 3):
                            pool.wait_ge(S["ada_used"], l * NMOD * KT + NMOD * k + m - 2)
                        src = wk[k, m] if isinstance(k, int) else wk[bass.ds(k, 1), m].rearrange("a p n -> p (a n)")
                        pool.dma_start(ADA["ring"][:, m % 3], src).then_inc(ada_ready[m % 3], 16)
                step(0, False)
                with pool.Fori(1, KT) as k:
                    step(k, False)

            def ada_half(q):
                wk = a["w_ada"][0].rearrange("(k p) (m n) -> k m p n", p=P, n=D)

                def step(k, first):
                    for m in range(3):
                        if not first:
                            pool.wait_ge(S["ada_used"], 3 * KT * q + 3 * k + m - 2)
                        src = wk[k, 3 * q + m] if isinstance(k, int) else wk[bass.ds(k, 1), 3 * q + m].rearrange("a p n -> p (a n)")
                        pool.dma_start(ADA["ring"][:, m], src).then_inc(ada_ready[m], 16)
                step(0, q == 0)
                with pool.Fori(1, KT) as k:
                    step(k, False)

            pool.dma_start(ccol[:], a["c_col"]).then_inc(S["col_load"], 16)
            pool.dma_start(cst[:], a["cst"]).then_inc(S["cst_load"], 16)
            pool.dma_start(col1[:], a["col1"]).then_inc(S["col_load"], 16)
            pool.dma_start(col2[:], a["col2"]).then_inc(S["col_load"], 16)
            pool.dma_start(row[:], a["row"]).then_inc(S["row_load"], 16)
            for kind, l in plan:
                s = SIDX[kind, l]
                if kind == "mix":
                    if s:
                        pool.wait_ge(S["x_ready"], s)
                    if l == 0:
                        ada_half(0)
                    pool.dma_start(M["wglr"], a["w_glr"][l]).then_inc(S["aux1_load"], 16)
                    pool.dma_start(M["gk2"][0:RANK, :], a["w_gk2"][l]).then_inc(S["aux1_load"], 16)
                    pool.dma_start(M["sbmask"], a["tab"][:, 0:384]).then_inc(S["tab_load"], 16)
                    if l == 0:
                        ada_half(1)
                if kind in ("nsa", "peer"):
                    if s:
                        pool.wait_ge(S["x_ready"], s)
                    if kind == "nsa":
                        pool.dma_start(N["wtm"], a["w_tm"][l]).then_inc(S["tm_load"], 16)
                        pool.dma_start(N["x2"], a["x2"][l]).then_inc(S["x2_load"], 16)
                        pool.dma_start(N["tab"], a["tab"][:, 384:]).then_inc(S["tab_load"], 16)
                    else:
                        pool.dma_start(Q["sk"], a["sk_t"][l]).then_inc(S["sk_load"], 16)
                if kind == "moe":
                    pool.wait_ge(S["x_ready"], s)
                    pool.dma_start(E["wr"], a["w_rt"][l]).then_inc(S["rt_load"], 16)
                    pool.wait_ge(S["combt_ev"], l + 1)
                    pool.dma_start(comb_dram[l], E["combT"][0:NE, :]).then_inc(S["comb_st"], 16)
                    pool.wait_ge(S["comb_st"], 16 * (l + 1))
                    pool.dma_start(E["combB"], comb_dram[l].partition_broadcast(P)).then_inc(S["comb_ld"], 16)
                    if l == 0 and ("mix", 1) in plan:
                        ada(1)

        @block.scalar
        def _(act):
            A = nc.scalar.activation

            def norm(s, sq, rs):
                n = NORM[s]
                if SIDX[s]:
                    act.wait_ge(S["x_ready"], SIDX[s])
                else:
                    act.wait_ge(S["x_load"], 16)
                A(sq, x[:], ACT.Square).then_inc(S["norm_sq"], 1)
                act.wait_ge(S["norm_ss"], n + 1)
                A(rs, PS[:, 7, 0:T], ACT.Ln, scale=1.0 / D, bias=EPS)
                act.drain()
                A(rs, rs, ACT.Exp, scale=-0.5).then_inc(S["norm_rs"], 1)

            def split_hi(s, n, i=0, per=0):
                m = BASE_SPLIT[s] + n
                wait_slot(act, m, i, per)
                if i_pos(i) or m >= RING:
                    act.wait_ge(S["slot_done"], m - RING + 1 + RING * per * i)
                A(w_hi[:, m % RING], ring[:, m % RING], ACT.Copy).then_inc(S["hi_done"], 1)

            def mix(l):
                s, n0, p0 = ("mix", l), BASE["mix", l], PAIR["mix", l]
                norm(s, M["sq"], M["rs"])
                act.wait_ge(S["glr_mm"], l + 1)
                A(M["glr"][0:RANK, :], PS[0:RANK, 4, 0:T], ACT.Copy).then_inc(S["glr_ev"], 1)
                dst = [M["qk"][:, 0:2], M["qk"][:, 2:4], M["qk"][:, 4:6], M["qk"][:, 6:8], M["gqk"][:, 0:2],
                       M["gqk"][:, 2:4], M["gr"][:, 0:2], M["gr"][:, 2:4]]
                for j in range(8):
                    act.wait_ge(S["slot_done"], n0 + 2 * j + 2)
                    A(dst[j], PS[:, (p0 + j) % 4, :].rearrange("p (a b) -> p a b", b=T), ACT.Copy).then_inc(S["pair_evac"], 1)
                    if j == 0:
                        act.wait_ge(S["gkz_mm"], l + 1)
                        for q in range(2):
                            A(G["gy"][:, q], PS[:, 5, T * q:T * q + T], ACT.Identity, bias=c1(l, "b_gk", q, 1)).then_inc(S["gkz_ev"], 1)
                        act.drain()
                        b0 = G["b0"].rearrange("p (q c) t -> p q (c t)", q=2)
                        A(b0, G["gy"], ACT.Abs)
                        act.drain()
                        A(b0, b0, ACT.Exp, scale=-1.0)
                        act.drain()
                        A(b0, b0, ACT.Ln, bias=1.0).then_inc(S["gl_ln"], 1)
                act.drain()
                A(M["sq"], M["qk"], ACT.Square).then_inc(S["qk_sq"], 1)
                A(M["gr"], M["gr"], ACT.Silu).then_inc(S["grs"], 1)
                act.wait_ge(S["slot_done"], n0 + 20)
                A(M["sbv"], PS[:, 4:6, :], ACT.Copy).then_inc(S["sbv_ev"], 1)
                act.wait_ge(S["slot_done"], n0 + 24)
                A(M["gv"], PS[:, 6:8, :], ACT.Copy).then_inc(S["gv_ev"], 1)
                act.wait_ge(S["qk_ss"], l + 1)
                A(M["rsq"], PS[:, 0:4, :].rearrange("p a (b c) -> p (a b) c", c=T), ACT.Ln, scale=1.0 / SBD, bias=EPS)
                act.drain()
                A(M["rsq"], M["rsq"], ACT.Exp, scale=-0.5).then_inc(S["qk_rs"], 1)
                for g in range(2):
                    k = 2 * l + g
                    act.wait_ge(S["zm_ok"], k + 1)
                    if k:
                        act.wait_ge(S["lf_ok"], k)
                    A(M["e"], M["zm"], ACT.Abs)
                    act.drain()
                    A(M["e"], M["e"], ACT.Exp, scale=-1.0)
                    act.drain()
                    A(M["e"], M["e"], ACT.Ln, bias=1.0).then_inc(S["ln_ok"], 1)
                    act.wait_ge(S["arg_ok"], k + 1)
                    A(M["w"], M["zm"], ACT.Exp).then_inc(S["w_ok"], 1)
                    act.wait_ge(S["pv_mm"], k + 1)
                    A(M["mixT"][:, 2 * g:2 * g + 2], PS[:, 0:2, 0:T], ACT.Copy).then_inc(S["outa_ev"], 1)
                act.wait_ge(S["gl_b"], l + 1)
                A(G["eb"], G["b0"], ACT.Exp)
                A(G["einv"], G["b0"], ACT.Exp, scale=-1.0).then_inc(S["gl_e1"], 1)
                A(G["eend"], G["b1"], ACT.Exp).then_inc(S["gl_e2"], 1)
                act.wait_ge(S["kend_mm"], l + 1)
                A(G["kend"].rearrange("p a b -> p (a b)"), PS[:, 4, :], ACT.Copy).then_inc(S["kend_ev"], 1)
                act.wait_ge(S["o_mm"], l + 1)
                o2 = M["qk"][:, 0:4]
                A(o2, PS[:, 2:4, :].rearrange("p a (b c) -> p (a b) c", c=T), ACT.Copy)
                A(M["rsq"][:, 0:4], PS[:, 2:4, :].rearrange("p a (b c) -> p (a b) c", c=T), ACT.Square).then_inc(S["o_sq"], 1)
                act.wait_ge(S["o_ss"], l + 1)
                A(M["rsq"][:, 4:8], PS[:, 0:2, :].rearrange("p a (b c) -> p (a b) c", c=T), ACT.Ln, scale=1.0 / GDV, bias=EPS)
                act.drain()
                A(M["rsq"][:, 4:8], M["rsq"][:, 4:8], ACT.Exp, scale=-0.5).then_inc(S["o_rs"], 1)

            def moe(l):
                norm(("moe", l), E["sq"], E["rs"])
                act.wait_ge(S["rt_max"], l + 1)
                for t in range(TT):
                    A(E["gx"][:, t], E["lg"][:, t, 0:NG], ACT.Exp, bias=E["sc"][:, t, 0:1], accum_out=E["sc"][:, t, 1:2])
                A(E["sc"][:, :, 2:3], E["sc"][:, :, 3:4], ACT.Exp).then_inc(S["rt_exp"], 1)
                act.wait_ge(S["comb_mm"], l + 1)
                A(E["combT"][0:NE, :], PS[0:NE, 6, 0:T], ACT.Copy).then_inc(S["combt_ev"], 1)
                u0, n0 = FT * NE * l, BASE["moe", l]

                def step(i, first):
                    for j in range(FT * MOE_STEP):
                        u = u0 + FT * MOE_STEP * i + j
                        for c in range(3):
                            split_hi(("moe", l), 3 * j + c, i, 6)
                        act.wait_ge(S["slot_done"], up_done(n0, i, j // 2, first) + 2 * (j % 2))
                        if not (first and j < 4):
                            act.wait_ge(S["hh_ok"], u - 3)
                        A(E["sg"][:, j % 4], PS[:, 4 + j % 4, 0:T], ACT.Silu).then_inc(S["silu_ok"], 1)
                step(0, True)
                with act.Fori(1, NE // MOE_STEP) as i:
                    step(i, False)
                act.wait_ge(S["slot_done"], n0 + MOE_SLOTS)
                A(E["y"].rearrange("p a (b c) -> p (a b) c", c=512), PS[:, 0:4, :], ACT.Copy).then_inc(S["y_ev"], 1)

            def layer_norm(l, q):
                n = LN["peer" if q else "nsa", l]
                act.wait_ge(S["ln_c"], n + 1)
                A(L_["sq"], x[:], ACT.Square).then_inc(S["ln_sq"], 1)
                act.wait_ge(S["ln_ss"], n + 1)
                A(L_["rs"], PS[:, 7, 0:T], ACT.Ln, scale=1.0 / D, bias=LN_EPS)
                act.drain()
                A(L_["rs"], L_["rs"], ACT.Exp, scale=-0.5).then_inc(S["ln_rs"], 1)

            def bank_pair(b):
                return PS[:, b, :].rearrange("p (a b) -> p a b", b=T)

            def nsa(l):
                n0, p0, s = BASE["nsa", l], PAIR["nsa", l], SIDX["nsa", l]
                if s:
                    act.wait_ge(S["x_ready"], s)
                lam = N["lam"]
                A(lam[:, 0], c2(l, "lam"), ACT.Abs)
                act.drain()
                A(lam[:, 1], lam[:, 0], ACT.Exp, scale=-1.0).then_inc(S["lam_e"], 1)
                for j in range(W2_IN // 2):
                    act.wait_ge(S["slot_done"], n0 + 2 * j + 2)
                    for q in range(2):
                        last = A(N["p"][:, 2 * j + q], PS[:, (p0 + j) % 4, T * q:T * q + T], ACT.Identity, bias=c2(l, "b_in", 2 * j + q, 1))
                    last.then_inc(S["pair_evac"], 1)
                act.wait_ge(S["tm_mm"], l + 1)
                A(N["vtm"], PS[:, 4:6, 0:4 * HD], ACT.Copy)
                A(N["gt"], PS[:, 4:6, 4 * HD:TMW], ACT.Sigmoid).then_inc(S["tm_ev"], 1)
                act.wait_ge(S["c1_mm"], l + 1)
                for q, name in ((0, "b1k"), (1, "b1v")):
                    last = A(N["gel"][0:HD, q], PS[0:HD, q, 0:2 * NC], ACT.Gelu_apprx_tanh, bias=c2(l, name)[0:HD])
                last.then_inc(S["c1_ev"], 1)
                act.wait_ge(S["ri_mm"], l + 1)
                for q, (buf, name) in enumerate((("r", "lru_ba"), ("i", "lru_bx"))):
                    for t in range(LT):
                        last = A(N[buf][:, t], PS[:, 4 + 2 * q + t // 2, T * (t % 2):T * (t % 2) + T], ACT.Sigmoid, bias=c2(l, name, t, 1))
                last.then_inc(S["ri_ev"], 1)
                act.wait_ge(S["c2_mm"], l + 1)
                A(N["kc"], PS[:, 0, 0:2 * NC], ACT.Identity, bias=c2(l, "b2k"))
                for j in range(4):
                    last = A(N["vcz"][32 * j:32 * j + 32, j], PS[32 * j:32 * j + 32, 1, 0:HD], ACT.Copy)
                last.then_inc(S["c2_ev"], 1)
                act.wait_ge(S["loga"], l + 1)
                A(N["a0"], N["r"], ACT.Exp)
                A(N["u"], N["r"], ACT.Tanh).then_inc(S["th_ok"], 1)
                act.wait_ge(S["u_in"], l + 1)
                A(N["u"], N["a1"], ACT.Sqrt).then_inc(S["sqrt_ok"], 1)
                A(N["gg"], N["p"][:, 4:8], ACT.Gelu_apprx_tanh).then_inc(S["gelu_g"], 1)
                act.wait_ge(S["cs_max"], l + 1)
                A(N["cs"][:, :, :, 0:NC], N["cs"][:, :, :, 0:NC], ACT.Exp).then_inc(S["cs_exp"], 1)
                act.wait_ge(S["ct_mm"], l + 1)
                A(N["ct"], PS[:, 2, :].rearrange("p (a b) -> p a b", b=P), ACT.Copy).then_inc(S["ct_ev"], 1)
                for u, (br, t) in enumerate(UNITS):
                    k = 4 * l + u
                    sv = N["s0"].rearrange("p a b -> p (a b)")[:, 0:NH * P * (t + 1)]
                    act.wait_ge(S["att_max"], k + 1)
                    A(sv, sv, ACT.Exp).then_inc(S["att_exp"], 1)
                    act.wait_ge(S["att_t"], k + 1)
                    o, nt = pt_at(br, t)
                    A(N["pt"][:, o:o + nt], PS[:, 0:nt // 4, :].rearrange("p a (b c) -> p (a b) c", c=P), ACT.Copy).then_inc(S["att_tev"], 1)
                act.wait_ge(S["nsa_mm"], l + 1)
                act.wait_ge(S["lru_h"], l + 1)
                for t in range(TT):
                    last = A(N["ynsa"][:, :, P * t:P * t + P], PS[:, t, :].rearrange("p (a b) -> p a b", b=P), ACT.Copy)
                last.then_inc(S["nsa_ev"], 1)
                act.wait_ge(S["ylru_ok"], l + 1)
                act.drain()
                A(N["sq"][:, 0:4], N["u"], ACT.Square)
                A(N["sq"][:, 4:8], N["ynsa"], ACT.Square).then_inc(S["g_sq"], 1)
                act.wait_ge(S["g_ss"], l + 1)
                A(N["rs"], PS[:, 7, :], ACT.Ln, scale=1.0 / 512, bias=LN_EPS)
                act.drain()
                A(N["rs"], N["rs"], ACT.Exp, scale=-0.5).then_inc(S["g_rs"], 1)
                layer_norm(l, 0)

            def peer(l):
                n0, p0 = BASE["peer", l], PAIR["peer", l]
                for j in range(PH + 1):
                    if j < PH:
                        act.wait_ge(S["slot_done"], n0 + 2 * j + 2)
                        A(Q["pq"][:, 2 * j:2 * j + 2], bank_pair((p0 + j) % 4), ACT.Copy).then_inc(S["pair_evac"], 1)
                    if j:
                        hd = j - 1
                        act.wait_ge(S["ps_mm"], PH * l + hd + 1)
                        A(Q["s"][:, :, 2 * hd:2 * hd + 2], PS[:, 4 + hd % 4, :].rearrange("p (t c k) -> p t c k", t=TT, c=2),
                          ACT.Copy).then_inc(S["ps_ev"], 1)
                act.wait_ge(S["pk_top"], l + 1)
                A(Q["cv"], Q["cv"], ACT.Exp).then_inc(S["pk_exp"], 1)
                act.wait_ge(S["pk_t"], l + 1)
                A(egT, PS[:, 0:2, :].rearrange("p a (b c) -> p (a b) c", c=T)[:, 0:3], ACT.Copy).then_inc(S["pk_tev"], 1)

                def evac(i):
                    for j in range(4):
                        act.wait_ge(S["pt_mm"], T * l + 16 * i + 4 * j + 4)
                        o = GT[:, 4 * j:4 * j + 4] if isinstance(i, int) else GT[:, bass.ds(16 * i + 4 * j, 4)]
                        A(o, PS[:, 4 + j, :].rearrange("p (a b) -> p a b", b=PK), ACT.Copy).then_inc(S["g_ev"], 1)
                evac(0)
                with act.Fori(1, T // 16) as i:
                    evac(i)
                n0 += W2_Q

                def step(i, first):
                    for j in range(PEER_STEP):
                        for c in range(2):
                            split_hi(("peer", l), 2 * j + c, i, 2)
                        act.wait_ge(S["slot_done"], n0 + 1 if first and j == 0 else n0 + 2 * (PEER_STEP * i + j))
                        if not (first and j < 2):
                            act.wait_ge(S["pw_ok"], PK * l + PEER_STEP * i + j - 1)
                        A(pb[:, j % 2], PS[:, 4 + j, 0:T], ACT.Gelu_apprx_tanh).then_inc(S["gelu_ok"], 1)
                step(0, True)
                with act.Fori(1, PK // PEER_STEP) as i:
                    step(i, False)
                act.wait_ge(S["slot_done"], n0 + PEER_SLOTS)
                A(L_["y"].rearrange("p a (b c) -> p (a b) c", c=512), PS[:, 0:4, :], ACT.Copy).then_inc(S["y2_ev"], 1)
                layer_norm(l, 1)

            act.wait_ge(S["col_load"], 48)
            A(csil[:], ccol[:], ACT.Silu).then_inc(S["csilu"], 1)
            fns = {"mix": mix, "moe": moe, "nsa": nsa, "peer": peer}
            for kind, l in plan:
                fns[kind](l)

        @block.vector
        def _(dve):
            V = nc.vector

            def ada_step(l, k):
                for m in range(NMOD):
                    if m == 0:
                        dve.drain()
                    dve.wait_ge(ada_ready[m % 3], 16 * (2 * KT * l + 2 * k + m // 3 + 1))
                    ck = csil[:, k:k + 1] if isinstance(k, int) else csil[:, bass.ds(k, 1)]
                    V.scalar_tensor_tensor(ADA["acc"][:, m], ADA["ring"][:, m % 3], ck, ADA["acc"][:, m],
                                           ALU.mult, ALU.add).then_inc(S["ada_used"], 1)

            def ada_clear(l):
                V.memset(ADA["acc"], 0.0)

            def ada_half(q):
                for k in range(KT):
                    for m in range(3):
                        dve.wait_ge(ada_ready[m], 16 * (KT * q + k + 1))
                        if m == 0:
                            dve.drain()
                        V.scalar_tensor_tensor(ADA["acc"][:, 3 * q + m], ADA["ring"][:, m], csil[:, k:k + 1], ADA["acc"][:, 3 * q + m],
                                               ALU.mult, ALU.add).then_inc(S["ada_used"], 1)
                dve.drain().then_inc(S["ada_acc"], 1)

            def ada_cols(l, q0, q1):
                dve.wait_ge(S["ada_ps"], 2 * l + q0 + 1)
                V.tensor_tensor(mod[:, 24 * q0:24 * q1], PS[:, 6, 24 * q0:24 * q1], c1(l, "b_ada", 24 * q0, 24 * (q1 - q0)),
                                ALU.add).then_inc(S["ada_col"], 1)
                dve.drain()
                for q, name in ((0, "norm_mix"), (1, "norm_ffn")):
                    if q0 <= q < q1:
                        V.scalar_tensor_tensor(ga[:, q], mod[:, 24 * q + 8:24 * q + 16], 1.0, c1(l, name), ALU.add, ALU.mult)
                dve.drain()

            def norm(s, rs, q):
                dve.wait_ge(S["norm_rs"], NORM[s] + 1)
                V.tensor_tensor(h[:], x[:], rs.unsqueeze(1).to_broadcast([P, KT, T]), ALU.mult)
                dve.drain()
                for k in range(KT):
                    last = V.tensor_scalar(h[:, k], h[:, k], ga[:, q, k:k + 1], mod[:, 24 * q + k:24 * q + k + 1],
                                           ALU.mult, ALU.add)
                last.then_inc(S["h_ready"], 1)

            def split_lo(s, n, i=0, per=0):
                m = BASE_SPLIT[s] + n
                dve.wait_ge(S["hi_done"], SPLIT[s] + n + 1 + RING * per * i)
                V.tensor_tensor(w_lo[:, m % RING], ring[:, m % RING], w_hi[:, m % RING].bitcast(F32), ALU.subtract)\
                    .then_inc(S["lo_done"], 1)

            def mix(l):
                s, n0, p0 = ("mix", l), BASE["mix", l], PAIR["mix", l]
                if l == 0:
                    ada_clear(0)
                    dve.wait_ge(S["csilu"], 1)
                    ada_half(0)
                    ada_cols(0, 0, 1)
                    norm(s, M["rs"], 0)
                    ada_half(1)
                    ada_cols(0, 1, 2)
                else:
                    ada_cols(1, 0, 2)
                    norm(s, M["rs"], 0)
                dve.wait_ge(S["gl_ln"], l + 1)
                b0, b1 = G["b0"], G["b1"]
                V.scalar_tensor_tensor(b1.rearrange("p (q c) t -> p q (c t)", q=2), G["gy"], 0.0,
                                       b0.rearrange("p (q c) t -> p q (c t)", q=2), ALU.min, ALU.subtract)
                dve.drain()
                V.tensor_scalar(b0, b1, 1.0 / 16.0, None, ALU.mult)
                d, src, dst = 1, b0, b1
                while d < CHUNK:
                    dve.drain()
                    V.tensor_tensor(dst[:, :, d:], src[:, :, d:], src[:, :, :CHUNK - d], ALU.add)
                    last = V.tensor_copy(dst[:, :, :d], src[:, :, :d])
                    src, dst, d = dst, src, 2 * d
                assert src is b0
                dve.drain()
                V.tensor_tensor(b1, b0[:, :, CHUNK - 1:CHUNK].to_broadcast([P, 8, CHUNK]), b0, ALU.subtract).then_inc(S["gl_b"], 1)
                V.memset(G["st"], 0.0)
                dve.wait_ge(S["qk_rs"], l + 1)
                V.scalar_tensor_tensor(M["qkn"][:, 0:4], M["qk"][:, 0:4], c1(l, "q_gain"), M["rsq"][:, 0:4], ALU.mult, ALU.mult)
                V.scalar_tensor_tensor(M["qkn"][:, 4:8], M["qk"][:, 4:8], c1(l, "k_gain"), M["rsq"][:, 4:8],
                                       ALU.mult, ALU.mult).then_inc(S["qkn"], 1)
                sbm = M["sbmask"].unsqueeze(1).to_broadcast([P, 4, 384])
                dve.wait_ge(S["tab_load"], 16 * (TABS["mix", l] + 1))
                for g in range(2):
                    k = 2 * l + g
                    dve.wait_ge(S["z_mm"], k + 1)
                    if k:
                        dve.wait_ge(S["w_ok"], k)
                    V.scalar_tensor_tensor(M["zm"], PS[:, 0:4, 0:384], SBD ** -0.5, sbm, ALU.mult, ALU.add).then_inc(S["zm_ok"], 1)
                    dve.wait_ge(S["ln_ok"], k + 1)
                    if k:
                        dve.wait_ge(S["suf_mm"], k)
                    V.scalar_tensor_tensor(M["lf"], M["zm"], 0.0, M["e"], ALU.max, ALU.add).then_inc(S["lf_ok"], 1)
                    dve.wait_ge(S["suf_mm"], k + 1)
                    V.tensor_tensor(M["zm"], PS[:, 4:8, 0:384], M["zm"], ALU.add).then_inc(S["arg_ok"], 1)
                dve.wait_ge(S["gl_e1"], l + 1)
                ch = lambda v: v.rearrange("p (q c) t -> p q (c t)", q=2)
                V.scalar_tensor_tensor(G["qd"], M["gqk"][:, 0:2], GDK ** -0.5, ch(G["eb"]), ALU.mult, ALU.mult)
                V.tensor_tensor(G["ki"], M["gqk"][:, 2:4], ch(G["einv"]), ALU.mult)
                dve.wait_ge(S["gl_e2"], l + 1)
                V.tensor_tensor(G["ke"], M["gqk"][:, 2:4], ch(G["eend"]), ALU.mult).then_inc(S["gl_prod"], 1)
                dve.wait_ge(S["kv_mm"], l + 1)
                st = G["st"]
                for c in range(NCH - 1):
                    for hh in range(GH):
                        o, q = GDK * (hh % 2), hh // 2
                        kv = PS[o:o + GDK, 5 + c, P * q:P * q + P]
                        if c == 0:
                            last = V.tensor_copy(st[o:o + GDK, 0, hh], kv)
                        else:
                            last = V.scalar_tensor_tensor(st[o:o + GDK, c, hh], st[o:o + GDK, c - 1, hh],
                                                          G["eb"][o:o + GDK, 4 * q + c, CHUNK - 1:CHUNK], kv, ALU.mult, ALU.add)
                    if c < NCH - 2:
                        dve.drain()
                last.then_inc(S["states"], 1)
                dve.wait_ge(S["sc_mm"], l + 1)
                V.tensor_tensor(G["sc"], PS[:, 0:2, :].rearrange("p a (b c) -> p (a b) c", c=P),
                                cc("glamask").unsqueeze(1).to_broadcast([P, 8, P]), ALU.mult).then_inc(S["sc_ok"], 1)
                dve.wait_ge(S["o_rs"], l + 1)
                dve.wait_ge(S["grs"], l + 1)
                o2 = M["qk"][:, 0:4]
                V.scalar_tensor_tensor(o2, o2, c1(l, "gla_gain"), M["rsq"][:, 4:8], ALU.mult, ALU.mult)
                dve.drain()
                V.tensor_tensor(M["mixT"][:, 4:8], o2, M["gr"], ALU.mult).then_inc(S["mixb_ok"], 1)
                for j in range(4):
                    dve.wait_ge(S["slot_done"], n0 + W1_IN + 2 * j + 2)
                    for q in range(2):
                        k = 2 * j + q
                        last = V.scalar_tensor_tensor(x[:, k], PS[:, (p0 + 8 + j) % 4, T * q:T * q + T],
                                                      mod[:, 16 + k:17 + k], x[:, k], ALU.mult, ALU.add)
                    last.then_inc(S["pair_evac"], 1)
                dve.drain().then_inc(S["x_ready"], 1)

            def moe(l):
                norm(("moe", l), E["rs"], 1)
                dve.drain()
                V.tensor_copy(E["h_hi"][:], h[:])
                dve.drain()
                V.tensor_tensor(E["h_lo"][:], h[:], E["h_hi"][:].bitcast(F32), ALU.subtract).then_inc(S["hs_ok"], 1)
                lg, sc = E["lg"], E["sc"]
                V.memset(lg[:, :, NG:8], NEG)
                dve.wait_ge(S["rt_mm"], l + 1)
                rt = PS[:, 6, 0:TT * 64].rearrange("p (a b) -> p a b", b=64)
                V.tensor_copy(lg[:, :, 0:NG], rt[:, :, 0:NG])
                V.tensor_copy(lg[:, :, 8:8 + NE], rt[:, :, NG:NG + NE])
                dve.drain()
                for t in range(TT):
                    V.max(E["gm8"][:, t], lg[:, t, 0:8])
                dve.drain()
                for t in range(TT):
                    V.max_index(gi[:, t], E["gm8"][:, t], lg[:, t, 0:8])
                V.tensor_scalar(sc[:, :, 0:1], E["gm8"][:, :, 0:1], -1.0, None, ALU.mult)
                dve.drain()
                V.tensor_copy(E["gf"], gi[:])
                dve.drain()
                io = lambda n: cc("iota")[:, 0:n].unsqueeze(1).to_broadcast([P, TT, n])
                V.tensor_tensor(E["oh"], io(NG), E["gf"][:, :, 0:1].to_broadcast([P, TT, NG]), ALU.is_equal)
                dve.drain()
                for t in range(TT):
                    ohb = E["oh"][:, t].unsqueeze(2).to_broadcast([P, NG, EPG])
                    V.tensor_tensor(E["tmp"][:, t].rearrange("p (g e) -> p g e", g=NG),
                                    lg[:, t, 8:8 + NE].rearrange("p (g e) -> p g e", g=NG), ohb, ALU.mult)
                dve.drain()
                for t in range(TT):
                    V.tensor_reduce(E["sel"][:, t], E["tmp"][:, t].rearrange("p (g e) -> p e g", g=NG), AX.X, ALU.add)
                dve.drain()
                for t in range(TT):
                    V.max(E["m8"][:, t], E["sel"][:, t])
                dve.drain()
                for t in range(TT):
                    V.max_index(ii[:, t], E["m8"][:, t], E["sel"][:, t])
                V.tensor_tensor(sc[:, :, 3:4], E["m8"][:, :, 1:2], E["m8"][:, :, 0:1], ALU.subtract)
                dve.drain()
                V.tensor_copy(E["if"], ii[:]).then_inc(S["rt_max"], 1)
                dve.wait_ge(S["rt_exp"], l + 1)
                V.tensor_scalar(sc[:, :, 4:5], sc[:, :, 2:3], 1.0, None, ALU.add)
                dve.drain()
                V.tensor_tensor(sc[:, :, 4:5], sc[:, :, 4:5], sc[:, :, 1:2], ALU.mult)
                dve.drain()
                V.reciprocal(sc[:, :, 5:6], sc[:, :, 4:5])
                dve.drain()
                V.tensor_tensor(sc[:, :, 6:7], sc[:, :, 5:6], sc[:, :, 2:3], ALU.mult)
                V.tensor_tensor(E["ew"], io(EPG), E["if"][:, :, 0:1].to_broadcast([P, TT, EPG]), ALU.is_equal)
                V.tensor_tensor(E["o2"], io(EPG), E["if"][:, :, 1:2].to_broadcast([P, TT, EPG]), ALU.is_equal)
                dve.drain()
                V.tensor_tensor(E["ew"], E["ew"], sc[:, :, 5:6].to_broadcast([P, TT, EPG]), ALU.mult)
                V.tensor_tensor(E["o2"], E["o2"], sc[:, :, 6:7].to_broadcast([P, TT, EPG]), ALU.mult)
                dve.drain()
                V.tensor_tensor(E["ew"], E["ew"], E["o2"], ALU.add)
                dve.drain()
                for t in range(TT):
                    last = V.tensor_tensor(E["comb"][:, t].rearrange("p (g e) -> p g e", g=NG),
                                           E["oh"][:, t].unsqueeze(2).to_broadcast([P, NG, EPG]),
                                           E["ew"][:, t].unsqueeze(1).to_broadcast([P, NG, EPG]), ALU.mult)
                last.then_inc(S["comb_ok"], 1)
                with_ada = l == 0 and ("mix", 1) in plan
                if with_ada:
                    ada_clear(1)
                dve.wait_ge(S["comb_ld"], 16 * (l + 1))
                u0 = FT * NE * l

                def step(i, first):
                    for j in range(FT * MOE_STEP):
                        u = u0 + FT * MOE_STEP * i + j
                        for c in range(3):
                            split_lo(("moe", l), 3 * j + c, i, 6)
                        dve.wait_ge(S["silu_ok"], u + 1)
                        if not (first and j < 4):
                            dve.wait_ge(S["slot_done"], BASE["moe", l] + 6 * (MOE_STEP * i + j // 2) - 2)
                        V.tensor_tensor(E["t1"][:, j % 4], E["sg"][:, j % 4], PS[:, 4 + j % 4, T:2 * T], ALU.mult)
                        dve.drain()
                        e = MOE_STEP * i + j // 2
                        cb = E["combB"][:, e] if isinstance(e, int) else E["combB"][:, bass.ds(e, 1)].rearrange("p a n -> p (a n)")
                        t1, hi, lo = E["t1"][:, j % 4], E["hh_hi"][:, j % 4], E["hh_lo"][:, j % 4]
                        V.tensor_tensor(t1, t1, cb, ALU.mult)
                        dve.drain()
                        V.tensor_copy(hi, t1)
                        dve.drain()
                        V.tensor_tensor(lo, t1, hi.bitcast(F32), ALU.subtract).then_inc(S["hh_ok"], 1)
                    if with_ada:
                        ada_step(1, i)
                step(0, True)
                with dve.Fori(1, NE // MOE_STEP) as i:
                    step(i, False)
                if with_ada:
                    dve.drain().then_inc(S["ada_acc"], 1)
                dve.wait_ge(S["yt_mm"], l + 1)
                for k in range(KT):
                    last = V.scalar_tensor_tensor(x[:, k], PS[:, 4 + k // 2, T * (k % 2):T * (k % 2) + T],
                                                  mod[:, 40 + k:41 + k], x[:, k], ALU.mult, ALU.add)
                last.then_inc(S["x_ready"], 1)

            def layer_norm(l, q):
                n = LN["peer" if q else "nsa", l]
                dve.wait_ge(S["ln_mu"], n + 1)
                V.scalar_tensor_tensor(x[:], PS[:, 6, 0:T].unsqueeze(1).to_broadcast([P, KT, T]), -1.0 / D, x[:],
                                       ALU.mult, ALU.add).then_inc(S["ln_c"], 1)
                dve.wait_ge(S["ln_rs"], n + 1)
                V.tensor_tensor(x[:], x[:], L_["rs"].unsqueeze(1).to_broadcast([P, KT, T]), ALU.mult)
                dve.drain()
                for k in range(KT):
                    last = V.tensor_scalar(x[:, k], x[:, k], c2(l, f"ln{q + 1}_g", k, 1), c2(l, f"ln{q + 1}_b", k, 1), ALU.mult, ALU.add)
                last.then_inc(S["x_ready"], 1)

            def nsa(l):
                n0, p0 = BASE["nsa", l], PAIR["nsa", l]
                p, xc, lam = N["p"], N["xc"], N["lam"]
                dve.wait_ge(S["lam_e"], l + 1)
                V.tensor_scalar(lam[:, 2], lam[:, 1], 2.0, None, ALU.add)
                V.memset(N["gvr"], 0.0)
                V.memset(N["vcz"], 0.0)
                V.memset(N["cs"], 0.0).then_inc(S["pads_zero"], 1)
                dve.drain()
                V.reciprocal(lam[:, 3], lam[:, 2])
                dve.drain()
                V.tensor_tensor(lam[:, 2], lam[:, 1], lam[:, 3], ALU.mult)
                dve.drain()
                V.tensor_tensor(lam[:, 3], lam[:, 2], lam[:, 2], ALU.mult)
                dve.drain()
                V.tensor_scalar(lam[:, 4], lam[:, 3], 1.0 / 19, None, ALU.mult)
                for c in range(17, 1, -2):
                    dve.drain()
                    V.scalar_tensor_tensor(lam[:, 4], lam[:, 4], 1.0 / c, lam[:, 3], ALU.add, ALU.mult)
                dve.drain()
                V.scalar_tensor_tensor(lam[:, 4], lam[:, 4], 1.0, lam[:, 2], ALU.add, ALU.mult)
                V.tensor_scalar(lam[:, 5], c2(l, "lam"), 0.0, 8.0, ALU.min, ALU.mult)
                dve.drain()
                V.scalar_tensor_tensor(lam[:, 4], lam[:, 4], -16.0, lam[:, 5], ALU.mult, ALU.add)
                dve.wait_ge(S["pair_evac"], p0 + 2)
                for t in range(LT):
                    V.tensor_scalar(xc[:, t], p[:, t], c2(l, "conv_w", 3 * LT + t, 1), c2(l, "conv_b", t, 1), ALU.mult, ALU.add)
                for k in range(3):
                    d = 3 - k
                    dve.drain()
                    for t in range(LT):
                        last = V.scalar_tensor_tensor(xc[:, t, d:], p[:, t, 0:T - d], c2(l, "conv_w", k * LT + t, 1), xc[:, t, d:],
                                                      ALU.mult, ALU.add)
                last.then_inc(S["xc_ok"], 1)
                dve.wait_ge(S["pair_evac"], p0 + 8)
                for q, name in ((0, "pos_k"), (1, "pos_v")):
                    for g in range(NKV):
                        for o in range(2):
                            r = slice(HD * o, HD * o + HD)
                            src = p[r, 12 + 2 * q + g, :]
                            win = src[:, o:o + 1].copy()
                            win = bass.AP(win.tensor, win.offset, [win.ap[0], (2, CB // 2), (CS, NC)])
                            pos = c2(l, name)[r].unsqueeze(2).to_broadcast([HD, CB // 2, NC])
                            last = V.tensor_tensor(N["blk"][r, q, :, NC * g:NC * g + NC], win, pos, ALU.add)
                last.then_inc(S["blk_ok"], 1)
                dve.wait_ge(S["c1_ev"], l + 1)
                for j in range(4):
                    g = j // 2
                    last = V.tensor_copy(N["gvr"][0:HD, 32 * j:32 * j + NC], N["gel"][0:HD, 1, NC * g:NC * g + NC])
                last.then_inc(S["gvr_ok"], 1)
                dve.wait_ge(S["tm_ev"], l + 1)
                for br in range(3):
                    for par in range(2):
                        V.tensor_copy(N["gth"][:, :, br, 4 * par:4 * par + 4], N["gt"][:, :, 3 * par + br:3 * par + br + 19:6])
                dve.wait_ge(S["ri_ev"], l + 1)
                for t in range(LT):
                    last = V.tensor_scalar(N["r"][:, t], N["r"][:, t], lam[:, 4, t:t + 1], None, ALU.mult)
                last.then_inc(S["loga"], 1)
                V.tensor_tensor(N["i"], N["i"], xc, ALU.mult)
                dve.wait_ge(S["th_ok"], l + 1)
                V.tensor_scalar(N["a1"], N["u"], -1.0, 1.0, ALU.mult, ALU.add)
                dve.drain()
                V.reciprocal(N["a1"], N["a1"])
                dve.drain()
                V.scalar_tensor_tensor(N["a1"], N["u"], -2.0, N["a1"], ALU.mult, ALU.mult)
                dve.drain()
                V.tensor_scalar(N["a1"], N["a1"], 1e-30, None, ALU.max).then_inc(S["u_in"], 1)
                cs, st = N["cs"], N["st"]
                dve.wait_ge(S["tab_load"], 16 * (TABS["nsa", l] + 1))
                dve.wait_ge(S["cs_mm"], l + 1)
                for t in range(TT):
                    for par in range(2):
                        o = TAB["alibic"][0] - 384 + (t * NH + 4 * par) * NCP
                        al = N["tab"][:, o:o + 4 * NCP].rearrange("p (a b) -> p a b", b=NCP)[:, :, 0:NC]
                        src = PS[:, 2 + par, 64 * t:64 * t + 64].rearrange("p (a b) -> p a b", b=NCP)[:, :, 0:NC]
                        V.scalar_tensor_tensor(cs[:, t, 4 * par:4 * par + 4, 0:NC], src, HD ** -0.5, al, ALU.mult, ALU.add)
                csv = cs.rearrange("p t h c -> p (t h) c")[:, :, 0:NC]
                bc = lambda v, n: v.unsqueeze(2).to_broadcast([P, v.shape[1], n])
                dve.drain()
                V.tensor_reduce(st[:, 0], csv, AX.X, ALU.max)
                dve.drain()
                V.tensor_tensor(csv, csv, bc(st[:, 0], NC), ALU.subtract).then_inc(S["cs_max"], 1)
                dve.wait_ge(S["cs_exp"], l + 1)
                V.tensor_reduce(st[:, 1], csv, AX.X, ALU.add)
                dve.drain()
                V.reciprocal(st[:, 2], st[:, 1])
                dve.drain()
                for t in range(TT):
                    V.scalar_tensor_tensor(st[:, 2, NH * t:NH * t + NH], st[:, 2, NH * t:NH * t + NH], cc("anyc")[:, t:t + 1],
                                           N["gth"][:, t, 0], ALU.mult, ALU.mult)
                dve.drain()
                V.tensor_tensor(csv, csv, bc(st[:, 2], NC), ALU.mult).then_inc(S["cs_ok"], 1)
                for u, (br, t) in enumerate(UNITS):
                    k, nk = 4 * l + u, P * (t + 1)
                    sv = N["s0"].rearrange("p a b -> p (a b)")[:, 0:NH * nk].rearrange("p (a b) -> p a b", b=nk)
                    dve.wait_ge(S["att_mm"], k + 1)
                    if u:
                        dve.wait_ge(S["att_t"], k)
                    V.scalar_tensor_tensor(sv.rearrange("p a b -> p (a b)"), PS[:, 4:6 + 2 * t, :].rearrange("p a b -> p (a b)"), HD ** -0.5,
                                           N["tab"][:, NH * P * t:NH * P * t + NH * nk],
                                           ALU.mult, ALU.add)
                    dve.drain()
                    V.tensor_reduce(st[:, 0, 0:NH], sv, AX.X, ALU.max)
                    dve.drain()
                    V.tensor_tensor(sv, sv, bc(st[:, 0, 0:NH], nk), ALU.subtract).then_inc(S["att_max"], 1)
                    dve.wait_ge(S["att_exp"], k + 1)
                    V.tensor_reduce(st[:, 1, 0:NH], sv, AX.X, ALU.add)
                    dve.drain()
                    V.reciprocal(st[:, 2, 0:NH], st[:, 1, 0:NH])
                    dve.drain()
                    V.tensor_tensor(st[:, 2, 0:NH], st[:, 2, 0:NH], N["gth"][:, t, 1 + br], ALU.mult)
                    dve.drain()
                    V.tensor_tensor(sv, sv, bc(st[:, 2, 0:NH], nk), ALU.mult).then_inc(S["p_ok"], 1)
                dve.wait_ge(S["sqrt_ok"], l + 1)
                V.tensor_tensor(N["u"], N["u"], N["i"], ALU.mult)
                a0, a1, tmp, d = N["a0"], N["a1"], N["xc"], 1
                while d < T:
                    dve.drain()
                    V.tensor_tensor(tmp[:, :, d:], a0[:, :, d:], N["u"][:, :, 0:T - d], ALU.mult)
                    if 2 * d < T:
                        V.tensor_tensor(a1[:, :, 2 * d:], a0[:, :, 2 * d:], a0[:, :, d:T - d], ALU.mult)
                    dve.drain()
                    V.tensor_tensor(N["u"][:, :, d:], N["u"][:, :, d:], tmp[:, :, d:], ALU.add)
                    a0, a1, d = a1, a0, 2 * d
                dve.drain().then_inc(S["lru_h"], 1)
                dve.wait_ge(S["gelu_g"], l + 1)
                V.tensor_tensor(N["u"], N["u"], N["gg"], ALU.mult).then_inc(S["ylru_ok"], 1)
                dve.wait_ge(S["g_rs"], l + 1)
                for t in range(LT):
                    V.scalar_tensor_tensor(N["mix"][:, t], N["u"][:, t], c2(l, "gn_lru", t, 1), N["rs"][:, 0:T], ALU.mult, ALU.mult)
                for t in range(LT):
                    last = V.scalar_tensor_tensor(N["mix"][:, 4 + t], N["ynsa"][:, t], c2(l, "gn_nsa", t, 1), N["rs"][:, T:2 * T],
                                                  ALU.mult, ALU.mult)
                last.then_inc(S["mix2_ok"], 1)
                for j in range(4):
                    dve.wait_ge(S["slot_done"], n0 + W2_IN + 2 * j + 2)
                    V.scalar_tensor_tensor(x[:, 2 * j:2 * j + 2], x[:, 2 * j:2 * j + 2], ALPHA,
                                           PS[:, (p0 + 10 + j) % 4, :].rearrange("p (a b) -> p a b", b=T), ALU.mult, ALU.add)\
                        .then_inc(S["pair_evac"], 1)
                dve.drain().then_inc(S["z1_ok"], 1)
                layer_norm(l, 0)

            def peer(l):
                n0 = BASE["peer", l] + W2_Q
                v, iu, wk = Q["v"], Q["iu"], Q["wk"]

                def top16(rows):
                    for val, _, src, _ in rows:
                        V.max(val[:, 0:8], src)
                    dve.drain()
                    for val, idx, src, work in rows:
                        V.max_index(idx[:, 0:8], val[:, 0:8], src)
                        V.match_replace(work, val[:, 0:8], src, -3e38)
                    dve.drain()
                    for val, _, _, work in rows:
                        V.max(val[:, 8:16], work)
                    dve.drain()
                    for val, idx, _, work in rows:
                        V.max_index(idx[:, 8:16], val[:, 8:16], work)

                hk = lambda w: w.rearrange("p (h k) -> p h k", k=TOPK)
                for hd in range(PH):
                    dve.wait_ge(S["ps_ev"], PH * l + hd + 1)
                    top16([(v[:, t, 2 * hd + c], iu[:, t, 2 * hd + c], Q["s"][:, t, 2 * hd + c], wk[:, 2 * t + c])
                           for t in range(TT) for c in range(2)])
                    for t in range(TT):
                        V.tensor_tensor(Q["cand"][:, 2 * (hd % 2) + t].rearrange("p (i j) -> p i j", j=TOPK),
                                        v[:, t, 2 * hd].unsqueeze(2).to_broadcast([P, TOPK, TOPK]),
                                        v[:, t, 2 * hd + 1].unsqueeze(1).to_broadcast([P, TOPK, TOPK]), ALU.add)
                    dve.drain()
                    top16([(hk(Q["cv"][:, t])[:, hd], hk(Q["ciu"][:, t])[:, hd], Q["cand"][:, 2 * (hd % 2) + t], Q["wk2"][:, 2 * (hd % 2) + t])
                           for t in range(TT)])
                dve.drain()
                for t in range(TT):
                    V.tensor_copy(Q["si"][:, t], iu[:, t])
                    V.tensor_copy(Q["sm"][:, t], hk(Q["cv"][:, t])[:, :, 0])
                    V.tensor_scalar(Q["hlu"][:, 0], Q["ciu"][:, t], 4, None, ALU.logical_shift_right)
                    V.tensor_scalar(Q["hlu"][:, 1], Q["ciu"][:, t], 15, None, ALU.bitwise_and)
                    dve.drain()
                    V.tensor_copy(Q["hl"], Q["hlu"])
                    V.tensor_tensor(hk(Q["cv"][:, t]), hk(Q["cv"][:, t]), Q["sm"][:, t].unsqueeze(2).to_broadcast([P, PH, TOPK]), ALU.subtract)
                    dve.drain()
                    for c in range(2):
                        V.tensor_tensor(Q["eq"], Q["hl"][:, c].unsqueeze(2).to_broadcast([P, PH * TOPK, TOPK]),
                                        cc("iota")[:, 0:TOPK].unsqueeze(1).to_broadcast([P, PH * TOPK, TOPK]), ALU.is_equal)
                        dve.drain()
                        eq4 = Q["eq"].rearrange("p (h k) j -> p h k j", k=TOPK)
                        si = Q["si"][:, t].rearrange("p (h c) k -> p h c k", c=2)[:, :, c]
                        V.tensor_tensor(eq4, eq4, si.unsqueeze(2).to_broadcast([P, PH, TOPK, TOPK]), ALU.mult)
                        dve.drain()
                        V.tensor_reduce(Q["ab"][:, t, c], Q["eq"], AX.X, ALU.add)
                        dve.drain()
                dve.drain().then_inc(S["pk_top"], 1)
                dve.wait_ge(S["pk_exp"], l + 1)
                for t in range(TT):
                    V.tensor_reduce(Q["sm"][:, t], hk(Q["cv"][:, t]), AX.X, ALU.add)
                dve.drain()
                V.reciprocal(Q["sm"], Q["sm"])
                dve.drain()
                for t in range(TT):
                    last = V.tensor_tensor(hk(Q["gate"][:, t]), hk(Q["cv"][:, t]), Q["sm"][:, t].unsqueeze(2).to_broadcast([P, PH, TOPK]), ALU.mult)
                last.then_inc(S["pk_ok"], 1)
                dve.wait_ge(S["pk_tev"], l + 1)

                def onehots(i, first):
                    for j in range(16):
                        if not (first and j < 4):
                            dve.wait_ge(S["pt_mm"], T * l + 16 * i + j - 3)
                        col = lambda m: egT[:, m, j:j + 1] if isinstance(i, int) else egT[:, m, bass.ds(16 * i + j, 1)]
                        V.tensor_scalar(OA[:, j % 4], cc("iota"), col(0), col(2), ALU.is_equal, ALU.mult)
                        V.tensor_scalar(OB[:, j % 4], cc("iota"), col(1), None, ALU.is_equal).then_inc(S["pt_a"], 1)
                onehots(0, True)
                with dve.Fori(1, T // 16) as i:
                    onehots(i, False)
                dve.wait_ge(S["g_ev"], T // 4 * (l + 1))
                dve.wait_ge(S["pt_mm"], T * (l + 1))
                V.tensor_copy(x_hi, x[:])
                dve.drain()
                V.tensor_tensor(x_lo, x[:], x_hi.bitcast(F32), ALU.subtract).then_inc(S["xs_ok"], 1)

                def step(i, first):
                    for j in range(PEER_STEP):
                        b = PEER_STEP * i + j
                        for c in range(2):
                            split_lo(("peer", l), 2 * j + c, i, 2)
                        dve.wait_ge(S["gelu_ok"], PK * l + b + 1)
                        if not (first and j < 2):
                            dve.wait_ge(S["slot_done"], n0 + 2 * b - 1)
                        g = GT[:, :, b] if isinstance(b, int) else GT[:, :, bass.ds(b, 1)].rearrange("p t a -> p (t a)")
                        f, hi, lo = pb[:, j % 2], pw_hi[:, j % 2], pw_lo[:, j % 2]
                        V.tensor_tensor(f, f, g, ALU.mult)
                        dve.drain()
                        V.tensor_copy(hi, f)
                        dve.drain()
                        V.tensor_tensor(lo, f, hi.bitcast(F32), ALU.subtract).then_inc(S["pw_ok"], 1)
                step(0, True)
                with dve.Fori(1, PK // PEER_STEP) as i:
                    step(i, False)
                dve.wait_ge(S["y2t"], l + 1)
                V.tensor_tensor(x[:], x_hi.bitcast(F32), x_lo.bitcast(F32), ALU.add)
                dve.drain()
                V.scalar_tensor_tensor(x[:], x[:], ALPHA, PS[:, 4:8, :].rearrange("p a (b c) -> p (a b) c", c=T), ALU.mult, ALU.add)\
                    .then_inc(S["z2_ok"], 1)
                layer_norm(l, 1)

            fns = {"mix": mix, "moe": moe, "nsa": nsa, "peer": peer}
            dve.wait_ge(S["cst_load"], 16)
            for kind, l in plan:
                fns[kind](l)

        @block.tensor
        def _(pe):
            mm = nc.tensor.matmul

            def mm3(dst, w, m, start, stop):
                mm(dst, w[0], m[0], start=start, stop=False)
                mm(dst, w[0], m[1], start=False, stop=False)
                return mm(dst, w[1], m[0], start=False, stop=stop)

            def wait_split(s, m, i=0, per=0):
                pe.wait_ge(S["lo_done"], SPLIT[s] + m - BASE_SPLIT[s] + 1 + RING * per * i)

            def parts(m, c0, c1):
                return w_hi[:, m % RING, c0:c1], w_lo[:, m % RING, c0:c1]

            def norm(s, sq):
                pe.wait_ge(S["norm_sq"], NORM[s] + 1)
                for k in range(KT):
                    last = mm(PS[:, 7, 0:T], ones, sq[:, k], start=k == 0, stop=k == KT - 1)
                last.then_inc(S["norm_ss"], 1)

            def pairs(n0, p0, n, rhs):
                for j in range(n):
                    if p0 + j >= 4:
                        pe.wait_ge(S["pair_evac"], p0 + j - 3)
                    for q in range(2):
                        s = n0 + 2 * j + q
                        wait_slot(pe, s)
                        for k in range(KT):
                            last = mm(PS[:, (p0 + j) % 4, T * q:T * q + T], ring[:, s % RING, P * k:P * k + P], rhs[:, k],
                                      start=k == 0, stop=k == KT - 1)
                        last.then_inc(S["slot_done"], 1)
                    yield j

            def token_major(n0, banks):
                for i in range(4):
                    s = n0 + i
                    wait_slot(pe, s)
                    for q in range(2):
                        for t in range(TT):
                            last = mm(PS[:, banks + t, :], h[:, 2 * i + q, P * t:P * t + P], ring[:, s % RING, 512 * q:512 * q + 512],
                                      start=i + q == 0, stop=i == 3 and q == 1)
                    last.then_inc(S["slot_done"], 1)

            def mix(l):
                s, n0, p0 = ("mix", l), BASE["mix", l], PAIR["mix", l]
                def ada_cols(q0, q1):
                    pe.wait_ge(S["ada_acc"], 2 * l + q0 + 1)
                    for j in range(24 * q0, 24 * q1):
                        last = mm(PS[:, 6, j:j + 1], ADA["acc"][:, j // KT, P * (j % KT):P * (j % KT) + P], ones[:, 0:1], start=True, stop=True)
                    last.then_inc(S["ada_ps"], 1)
                if SIDX[s]:
                    pe.wait_ge(S["x_ready"], SIDX[s])
                ada_cols(0, 2 if l else 1)
                norm(s, M["sq"])
                pe.wait_ge(S["h_ready"], NORM[s] + 1)
                pe.wait_ge(S["aux1_load"], 32 * (l + 1))
                for k in range(KT):
                    last = mm(PS[0:RANK, 4, 0:T], M["wglr"][:, k], h[:, k], start=k == 0, stop=k == KT - 1)
                last.then_inc(S["glr_mm"], 1)
                for j in pairs(n0, p0, 8, h):
                    if j == 0:
                        pe.wait_ge(S["glr_ev"], l + 1)
                        for q in range(2):
                            last = mm(PS[:, 5, T * q:T * q + T], M["gk2"][0:RANK, P * q:P * q + P], M["glr"][0:RANK, :], start=True, stop=True)
                        last.then_inc(S["gkz_mm"], 1)
                pe.wait_ge(S["gkz_ev"], 2 * (l + 1))
                token_major(n0 + 16, 4)
                if l == 0:
                    ada_cols(1, 2)
                pe.wait_ge(S["ada_col"], l + 2)
                token_major(n0 + 20, 6)
                pe.wait_ge(S["qk_sq"], l + 1)
                for j in range(4):
                    last = mm(PS[:, j, :], cc("headblk"), M["sq"][:, 2 * j:2 * j + 2], start=True, stop=True)
                last.then_inc(S["qk_ss"], 1)
                pe.wait_ge(S["qkn"], l + 1)
                q_, k_, v_ = M["qkn"][:, 0:4], M["qkn"][:, 4:8], M["sbv"]
                for g in range(2):
                    k = 2 * l + g
                    if g:
                        pe.wait_ge(S["outa_ev"], k)
                    for i in range(4):
                        hh = 4 * g + i
                        o, t = SBD * (hh % 2), hh // 2
                        mm(PS[:, i, 0:T], k_[o:o + SBD, t, 0:P], q_[o:o + SBD, t, :], start=True, stop=True)
                        last = mm(PS[:, i, T:T + P], k_[o:o + SBD, t, P:T], q_[o:o + SBD, t, P:T], start=True, stop=True)
                    last.then_inc(S["z_mm"], 1)
                    pe.wait_ge(S["lf_ok"], k + 1)
                    if not g:
                        pe.wait_ge(S["gv_ev"], l + 1)
                    if k:
                        pe.wait_ge(S["arg_ok"], k)
                    for i in range(4):
                        mm(PS[:, 4 + i, 0:384], cc("sufneg"), M["lf"][:, i], start=True, stop=False)
                        last = mm(PS[:, 4 + i, P:T], cc("negones"), M["lf"][:, i, T:T + P], start=False, stop=True)
                    last.then_inc(S["suf_mm"], 1)
                    pe.wait_ge(S["w_ok"], k + 1)
                    for i in range(4):
                        hh = 4 * g + i
                        o, b = SBD * (hh % 2), i // 2
                        mm(PS[o:o + SBD, b, 0:T], v_[:, 0, SBD * hh:SBD * hh + SBD], M["w"][:, i, 0:T], start=True, stop=False)
                        last = mm(PS[o:o + SBD, b, P:T], v_[:, 1, SBD * hh:SBD * hh + SBD], M["w"][:, i, T:T + P], start=False, stop=True)
                    last.then_inc(S["pv_mm"], 1)
                pe.wait_ge(S["gl_prod"], l + 1)
                for t in range(TT):
                    for q in range(2):
                        last = nc.tensor.transpose(PS[:, 4, P * (2 * t + q):P * (2 * t + q) + P], G["ke"][:, q, P * t:P * t + P], ident)
                last.then_inc(S["kend_mm"], 1)
                pe.wait_ge(S["outa_ev"], 2 * (l + 1))
                for hh in range(GH):
                    o, q = GDK * (hh % 2), hh // 2
                    for t in range(TT):
                        r = 4 * (hh % 2) + hh // 2 * 2 + t
                        last = mm(PS[:, r // 4, P * (r % 4):P * (r % 4) + P], G["ki"][o:o + GDK, q, P * t:P * t + P],
                                  G["qd"][o:o + GDK, q, P * t:P * t + P], start=True, stop=True)
                last.then_inc(S["sc_mm"], 1)
                pe.wait_ge(S["kend_ev"], l + 1)
                for c in range(NCH - 1):
                    r0, t = CHUNK * (c % 2), c // 2
                    for hh in range(GH):
                        o, q = GDK * (hh % 2), hh // 2
                        last = mm(PS[o:o + GDK, 5 + c, P * q:P * q + P],
                                  G["kend"][r0:r0 + CHUNK, 2 * t + q, o:o + GDK], M["gv"][r0:r0 + CHUNK, t, GDV * hh:GDV * hh + GDV],
                                  start=True, stop=True)
                last.then_inc(S["kv_mm"], 1)
                pe.wait_ge(S["states"], l + 1)
                pe.wait_ge(S["sc_ok"], l + 1)
                for hh in range(GH):
                    o, q = GDK * (hh % 2), hh // 2
                    for t in range(TT):
                        r = 2 * hh + t
                        b, c0 = 2 + r // 4, P * (r % 4)
                        chunks = [c for c in (2 * t, 2 * t + 1) if c]
                        rs = 4 * (hh % 2) + hh // 2 * 2 + t
                        mm(PS[:, b, c0:c0 + P], M["gv"][:, t, GDV * hh:GDV * hh + GDV], G["sc"][:, rs], start=True, stop=False)
                        for c in chunks:
                            last = mm(PS[:, b, c0 + CHUNK * (c % 2):c0 + CHUNK * (c % 2) + CHUNK], G["st"][:, c - 1, hh],
                                      G["qd"][:, q, CHUNK * c:CHUNK * c + CHUNK], start=False, stop=c == chunks[-1])
                last.then_inc(S["o_mm"], 1)
                pe.wait_ge(S["o_sq"], l + 1)
                for b in range(2):
                    last = mm(PS[:, b, :], ones, M["rsq"][:, 2 * b:2 * b + 2], start=True, stop=True)
                last.then_inc(S["o_ss"], 1)
                pe.wait_ge(S["mixb_ok"], l + 1)
                for _ in pairs(n0 + W1_IN, p0 + 8, 4, M["mixT"]):
                    pass

            def moe(l):
                s, n0 = ("moe", l), BASE["moe", l]
                norm(s, E["sq"])
                pe.wait_ge(S["h_ready"], NORM[s] + 1)
                pe.wait_ge(S["rt_load"], 16 * (l + 1))
                pe.wait_ge(S["row_load"], 16)
                for t in range(TT):
                    for k in range(KT):
                        mm(PS[:, 6, 64 * t:64 * t + NG + NE], h[:, k, P * t:P * t + P], E["wr"][:, k], start=k == 0, stop=False)
                    last = mm(PS[:, 6, 64 * t:64 * t + NG + NE], ones[0:1, :], row[:, l, 0:NG + NE], start=False, stop=True)
                last.then_inc(S["rt_mm"], 1)
                pe.wait_ge(S["comb_ok"], l + 1)
                for t in range(TT):
                    last = nc.tensor.transpose(PS[0:NE, 6, P * t:P * t + P], E["comb"][:, t], ident)
                last.then_inc(S["comb_mm"], 1)
                pe.wait_ge(S["combt_ev"], l + 1)

                def up(n, j, u, i=0, per=0, waits=True):
                    for f in range(FT):
                        b = 4 + (2 * j + f) % 4
                        if waits:
                            pe.wait_ge(S["hh_ok"], u + f - 3)
                        for q in range(2):
                            m = n + 2 * f + q
                            wait_split(("moe", l), m, i, per)
                            for k in range(KT):
                                last = mm3(PS[:, b, T * q:T * q + T], parts(m, P * k, P * k + P), (E["h_hi"][:, k], E["h_lo"][:, k]),
                                           k == 0, k == KT - 1)
                            last.then_inc(S["slot_done"], 1)

                def down(n, j, u, i=0, per=0, start=False, stop=False):
                    pe.wait_ge(S["hh_ok"], u)
                    for f in range(FT):
                        wait_split(("moe", l), n + f, i, per)
                        for t in range(TT):
                            for q in range(2):
                                r = (2 * j + f) % 4
                                last = mm3(PS[:, 2 * t + q, :], (E["hh_hi"][:, r, P * t:P * t + P], E["hh_lo"][:, r, P * t:P * t + P]),
                                           parts(n + f, 512 * q, 512 * q + 512), start and f == 0, stop and f == FT - 1)
                        last.then_inc(S["slot_done"], 1)

                pe.wait_ge(S["hs_ok"], l + 1)
                n, u0 = n0, FT * NE * l
                for e in range(MOE_STEP):
                    up(n, e, u0 + FT * e, waits=e >= 2)
                    n += 4
                    if e:
                        down(n, e - 1, u0 + FT * e, start=e == 1)
                        n += 2
                with pe.Fori(1, NE // MOE_STEP) as i:
                    for j in range(MOE_STEP):
                        m, u = n + 6 * j - 24, u0 + FT * (MOE_STEP * i + j)
                        up(m, j, u, i, 6)
                        down(m + 4, j - 1 + MOE_STEP, u, i, 6)
                down(n0 + MOE_SLOTS - 2, MOE_STEP - 1, u0 + FT * NE, stop=True)
                pe.wait_ge(S["y_ev"], l + 1)
                for k in range(KT):
                    for t in range(TT):
                        last = nc.tensor.transpose(PS[:, 4 + k // 2, T * (k % 2) + P * t:T * (k % 2) + P * t + P],
                                                   E["y"][:, t, P * k:P * k + P], ident)
                last.then_inc(S["yt_mm"], 1)

            def layer_norm(l, q):
                n = LN["peer" if q else "nsa", l]
                pe.wait_ge(S["z2_ok" if q else "z1_ok"], l + 1)
                for k in range(KT):
                    last = mm(PS[:, 6, 0:T], ones, x[:, k], start=k == 0, stop=k == KT - 1)
                last.then_inc(S["ln_mu"], 1)
                pe.wait_ge(S["ln_sq"], n + 1)
                for k in range(KT):
                    last = mm(PS[:, 7, 0:T], ones, L_["sq"][:, k], start=k == 0, stop=k == KT - 1)
                last.then_inc(S["ln_ss"], 1)

            def nsa(l):
                n0, p0, s = BASE["nsa", l], PAIR["nsa", l], SIDX["nsa", l]
                if s:
                    pe.wait_ge(S["x_ready"], s)
                else:
                    pe.wait_ge(S["x_load"], 16)
                for _ in pairs(n0, p0, W2_IN // 2, x):
                    pass
                pe.wait_ge(S["tm_load"], 16 * (l + 1))
                pe.wait_ge(S["row_load"], 16)
                for t in range(TT):
                    for k in range(KT):
                        mm(PS[:, 4 + t, 0:TMW], x[:, k, P * t:P * t + P], N["wtm"][:, k], start=k == 0, stop=False)
                    last = mm(PS[:, 4 + t, 0:TMW], ones[0:1, :], row[:, l, NG + NE:NG + NE + TMW], start=False, stop=True)
                last.then_inc(S["tm_mm"], 1)
                pe.wait_ge(S["x2_load"], 16 * (l + 1))
                pe.wait_ge(S["pair_evac"], p0 + 10)
                pe.wait_ge(S["blk_ok"], l + 1)

                def w(name, rows=P):
                    o, n = X2[name]
                    return N["x2"][0:rows, o:o + n]
                for q, name in ((0, "w1k"), (1, "w1v")):
                    for m in range(CB // 2):
                        last = mm(PS[0:HD, q, 0:2 * NC], w(name)[:, HD * m:HD * m + HD], N["blk"][:, q, m], start=m == 0, stop=m == CB // 2 - 1)
                last.then_inc(S["c1_mm"], 1)
                pe.wait_ge(S["xc_ok"], l + 1)
                pe.wait_ge(S["tm_ev"], l + 1)
                for q, name in ((0, "wa"), (1, "wx")):
                    for t in range(LT):
                        last = mm(PS[:, 4 + 2 * q + t // 2, T * (t % 2):T * (t % 2) + T], w(name)[:, P * t:P * t + P], N["xc"][:, t],
                                  start=True, stop=True)
                last.then_inc(S["ri_mm"], 1)
                pe.wait_ge(S["gvr_ok"], l + 1)
                pe.wait_ge(S["pads_zero"], l + 1)
                mm(PS[:, 0, 0:2 * NC], w("w2k", HD), N["gel"][0:HD, 0], start=True, stop=True)
                mm(PS[:, 1, 0:HD], N["gvr"][0:HD, :], w("w2v", HD), start=True, stop=False)
                mm(PS[:, 1, 0:HD], ones[0:1, :], row[:, l, NG + NE + TMW:], start=False, stop=True).then_inc(S["c2_mm"], 1)
                pe.wait_ge(S["c2_ev"], l + 1)
                q_ = N["p"][:, 8:12]
                for hh in range(NH):
                    o, j = HD * (hh % 2), hh // 2
                    for t in range(TT):
                        g = hh // REP
                        last = mm(PS[:, 2 + hh % 2, 64 * t + NCP * j:64 * t + NCP * j + NC], q_[o:o + HD, j, P * t:P * t + P],
                                  N["kc"][o:o + HD, NC * g:NC * g + NC], start=True, stop=True)
                last.then_inc(S["cs_mm"], 1)

                def scores(u):
                    br, t = UNITS[u]
                    for hh in range(NH):
                        o, j, g, nk = HD * (hh % 2), hh // 2, hh // REP, P * (t + 1)
                        c0 = (4 * (hh % 2) + j) * nk
                        last = mm(PS[:, 4 + c0 // 512, c0 % 512:c0 % 512 + nk], q_[o:o + HD, j, P * t:P * t + P],
                                  N["p"][o:o + HD, 16 + 2 * br + g, 0:nk], start=True, stop=True)
                    last.then_inc(S["att_mm"], 1)

                pe.wait_ge(S["ri_ev"], l + 1)
                scores(0)
                pe.wait_ge(S["cs_ok"], l + 1)
                for t in range(TT):
                    for par in range(2):
                        last = nc.tensor.transpose(PS[:, 2, P * (2 * t + par):P * (2 * t + par) + P],
                                                   N["cs"][:, t, 4 * par:4 * par + 4].rearrange("p a b -> p (a b)"), ident)
                last.then_inc(S["ct_mm"], 1)
                pe.wait_ge(S["ct_ev"], l + 1)
                for u, (br, t) in enumerate(UNITS):
                    k = 4 * l + u
                    pe.wait_ge(S["p_ok"], k + 1)
                    if u + 1 < len(UNITS):
                        scores(u + 1)
                    if u:
                        pe.wait_ge(S["att_tev"], k)
                    sv = N["s0"].rearrange("p a b -> p (a b)")
                    for hp in range(NH):
                        for kt in range(t + 1):
                            i = hp * (t + 1) + kt
                            last = nc.tensor.transpose(PS[:, i // 4, P * (i % 4):P * (i % 4) + P], sv[:, P * i:P * i + P], ident)
                    last.then_inc(S["att_t"], 1)
                pe.wait_ge(S["att_tev"], 4 * (l + 1))
                for t in range(TT):
                    for hh in range(NH):
                        par, j, g = hh % 2, hh // 2, hh // REP
                        dst = PS[HD * par:HD * par + HD, t, P * j:P * j + P]
                        mm(dst, N["vcz"][:, j], N["ct"][:, 2 * t + par], start=True, stop=False)
                        for br in range(2):
                            at_, _ = pt_at(br, t)
                            for kt in range(t + 1):
                                last = mm(dst, N["vtm"][:, kt, HD * (2 * br + g):HD * (2 * br + g) + HD],
                                          N["pt"][:, at_ + (4 * par + j) * (t + 1) + kt], start=False, stop=br == 1 and kt == t)
                last.then_inc(S["nsa_mm"], 1)
                pe.wait_ge(S["g_sq"], l + 1)
                for q in range(2):
                    for t in range(LT):
                        last = mm(PS[:, 7, T * q:T * q + T], ones, N["sq"][:, 4 * q + t], start=t == 0, stop=t == LT - 1)
                last.then_inc(S["g_ss"], 1)
                pe.wait_ge(S["mix2_ok"], l + 1)
                for _ in pairs(n0 + W2_IN, p0 + 10, 4, N["mix"]):
                    pass
                layer_norm(l, 0)

            def peer(l):
                n0, p0, s = BASE["peer", l], PAIR["peer", l], SIDX["peer", l]
                if s:
                    pe.wait_ge(S["x_ready"], s)
                else:
                    pe.wait_ge(S["x_load"], 16)
                def scores(hd):
                    pe.wait_ge(S["pair_evac"], p0 + hd + 1)
                    if hd >= 4:
                        pe.wait_ge(S["ps_ev"], PH * l + hd - 3)
                    for t in range(TT):
                        for c in range(2):
                            last = mm(PS[:, 4 + hd % 4, P * (2 * t + c):P * (2 * t + c) + P], Q["pq"][:, 2 * hd + c, P * t:P * t + P],
                                      Q["sk"][:, c], start=True, stop=True)
                    last.then_inc(S["ps_mm"], 1)
                for j in pairs(n0, p0, W2_Q // 2, x):
                    if j:
                        pe.wait_ge(S["sk_load"], 16 * (l + 1))
                        scores(j - 1)
                scores(PH - 1)
                pe.wait_ge(S["pk_ok"], l + 1)
                for m in range(3):
                    for t in range(TT):
                        c0 = T * m + P * t
                        src = Q["gate"][:, t] if m == 2 else Q["ab"][:, t, m]
                        last = nc.tensor.transpose(PS[:, c0 // 512, c0 % 512:c0 % 512 + P], src, ident)
                last.then_inc(S["pk_t"], 1)
                pe.wait_ge(S["ps_ev"], PH * (l + 1))

                def outer(i, first):
                    for j in range(16):
                        if not first and j % 4 == 0:
                            pe.wait_ge(S["g_ev"], T // 4 * l + 4 * i + j // 4 - 3)
                        pe.wait_ge(S["pt_a"], T * l + 16 * i + j + 1)
                        mm(PS[:, 4 + j // 4, P * (j % 4):P * (j % 4) + P], OA[:, j % 4], OB[:, j % 4], start=True, stop=True)\
                            .then_inc(S["pt_mm"], 1)
                outer(0, True)
                with pe.Fori(1, T // 16) as i:
                    outer(i, False)
                pe.wait_ge(S["g_ev"], T // 4 * (l + 1))
                pe.wait_ge(S["xs_ok"], l + 1)
                n0 += W2_Q

                def up(n, j, b, i=0, per=0, waits=True):
                    if waits:
                        pe.wait_ge(S["gelu_ok"], PK * l + b - 3)
                    wait_split(("peer", l), n, i, per)
                    for k in range(KT):
                        last = mm3(PS[:, 4 + j % 4, 0:T], parts(n, P * k, P * k + P), (x_hi[:, k], x_lo[:, k]), k == 0, k == KT - 1)
                    last.then_inc(S["slot_done"], 1)

                def down(n, j, b, i=0, per=0, start=False, stop=False):
                    pe.wait_ge(S["pw_ok"], PK * l + b + 1)
                    wait_split(("peer", l), n, i, per)
                    for t in range(TT):
                        for q in range(2):
                            last = mm3(PS[:, 2 * t + q, :], (pw_hi[:, j % 2, P * t:P * t + P], pw_lo[:, j % 2, P * t:P * t + P]),
                                       parts(n, 512 * q, 512 * q + 512), start, stop)
                    last.then_inc(S["slot_done"], 1)
                n = n0
                for b in range(PEER_STEP):
                    up(n, b, b, waits=False)
                    n += 1
                    if b:
                        down(n, b - 1, b - 1, start=b == 1)
                        n += 1
                with pe.Fori(1, PK // PEER_STEP) as i:
                    for j in range(PEER_STEP):
                        m, b = n + 2 * j - 8, PEER_STEP * i + j
                        up(m, j, b, i, 2)
                        down(m + 1, j + PEER_STEP - 1, b - 1, i, 2)
                down(n0 + PEER_SLOTS - 1, PEER_STEP - 1, PK - 1, stop=True)
                pe.wait_ge(S["y2_ev"], l + 1)
                for k in range(KT):
                    for t in range(TT):
                        last = nc.tensor.transpose(PS[:, 4 + k // 2, T * (k % 2) + P * t:T * (k % 2) + P * t + P],
                                                   L_["y"][:, t, P * k:P * k + P], ident)
                last.then_inc(S["y2t"], 1)
                layer_norm(l, 1)

            pe.wait_ge(S["cst_load"], 16)
            fns = {"mix": mix, "moe": moe, "nsa": nsa, "peer": peer}
            for kind, l in plan:
                fns[kind](l)


def _cst():
    c, tab = np.zeros((P, CST_N), np.float32), np.zeros((P, TAB_N), np.float32)

    def put(name, v):
        into, (o, n) = (c, CST[name]) if name in CST else (tab, TAB[name])
        into[:, o:o + n] = v.reshape(P, n)
    i, j = np.arange(P)[:, None], np.arange(P)[None, :]
    put("ident", (i == j).astype(np.float32))
    put("ones", np.ones((P, P), np.float32))
    put("headblk", (i // 64 == j // 64).astype(np.float32))
    put("sufneg", -(i >= j).astype(np.float32))
    put("negones", -np.ones((P, P), np.float32))
    before = np.where(i < j, 0.0, NEG)
    put("sbmask", np.concatenate([before, np.zeros((P, P)), before], 1))
    put("glamask", ((i // CHUNK == j // CHUNK) & (i <= j)).astype(np.float32))
    put("iota", np.broadcast_to(np.arange(P, dtype=np.float32), (P, P)))
    slopes = np.array([2.0 ** (-8.0 * (k + 1) / NH) for k in range(NH)], np.float32)
    slopes = np.concatenate([slopes[0::2], slopes[1::2]])
    for t in range(TT):
        q = P * t + np.arange(P)[:, None, None]
        k = np.arange(P * (t + 1))[None, None, :]
        put(f"alibi{t}", np.where(k <= q, -slopes[None, :, None] * np.abs(q - k), NEG).astype(np.float32))
    q = (P * np.arange(TT)[None, :] + np.arange(P)[:, None])[:, :, None, None]
    e = np.arange(NCP) * CS + CB - 1
    e = np.where(np.arange(NCP) < NC, e, 1 << 20)[None, None, None, :]
    put("alibic", np.where(e <= q, -slopes[None, None, :, None] * np.abs(q - e), NEG).astype(np.float32))
    put("anyc", (q[:, :, 0, 0] >= CB - 1).astype(np.float32))
    return c, tab


def _cols(items, table, width):
    c = np.zeros((P, DEPTH, width), np.float32)
    for name, v in items.items():
        o, n = table[name]
        c[:, :, o:o + n] = v
    return c


def _tiles(w):
    L, _, n = w.shape
    return w.reshape(L, KT, P, n // P, P).transpose(0, 3, 2, 1, 4).reshape(L, n // P, P, SLOT)


def _rows(w):
    L = w.shape[0]
    return w.reshape(L, 4, 2, P, 512).transpose(0, 1, 3, 2, 4).reshape(L, 4, P, SLOT)


def _col(v):
    return v.reshape(v.shape[0], -1, P).transpose(2, 0, 1)


def kernel(**inputs):
    import concourse.bacc as _bacc
    from concourse.bass_utils import run_bass_kernel_spmd as _run
    i = {k: np.asarray(v) for k, v in inputs.items()}
    L = DEPTH
    w_in = i["w_in"]
    dup = lambda v: np.concatenate([v, v], -1)
    fm = np.concatenate([w_in[:, :, 0:1024], w_in[:, :, 1536:2048], w_in[:, :, 2560:3072]], 2)
    a = {
        "x_fm": i["x"][0].reshape(T, KT, P).transpose(2, 1, 0),
        "c_col": i["c"][0].reshape(KT, P).T,
        "cst": _cst()[0],
        "tab": _cst()[1],
        "w_ada": i["w_ada"],
        "w1": np.concatenate([_tiles(fm), _rows(w_in[:, :, 1024:1536]), _rows(w_in[:, :, 2048:2560]), _tiles(i["w_out"])], 1),
        "w_glr": w_in[:, :, 3072:].reshape(L, KT, P, RANK).transpose(0, 2, 1, 3),
        "w_gk2": i["w_gk2"],
        "col1": _cols({
            "norm_mix": _col(i["norm_mix"]), "norm_ffn": _col(i["norm_ffn"]), "b_ada": _col(i["b_ada"]), "b_gk": _col(i["b_gk"]),
            "q_gain": _col(dup(i["q_gain"])), "k_gain": _col(dup(i["k_gain"])), "gla_gain": _col(i["gla_gain"]),
        }, C1, C1_N),
        "w_rt": np.concatenate([i["w_router_grp"], i["w_router_exp"]], 2).reshape(L, KT, P, NG + NE).transpose(0, 2, 1, 3),
    }
    gu = np.stack([i["w_gate"].reshape(L, NE, D, FE), i["w_up"].reshape(L, NE, D, FE)], 2)
    a["w_gu"] = gu.reshape(L, NE, 2, KT, P, FT, P).transpose(0, 1, 5, 2, 4, 3, 6).reshape(L, NE, 4, P, SLOT)
    a["w_down"] = i["w_down"].reshape(L, NE, FT, P, D)
    u = i["peer_u_2"].reshape(L, PK, PK, KT, P)
    a["u_t"] = u.transpose(0, 2, 4, 3, 1).reshape(L, PK, P, SLOT)
    a["v_t"] = i["peer_v_2"].reshape(L, PK, PK, D)
    w2, b2 = i["w_in_2"], i["b_in_2"]

    def fm2(w):
        t = [w[..., 0:1536]]
        for o in (1536, 1664, 1792, 2048):
            for g in range(NKV):
                t.append(dup(w[..., o + HD * g:o + HD * g + HD]))
        return np.concatenate(t, -1)

    def tm2(w):
        return np.concatenate([w[..., 1920:2048], w[..., 2176:2328]], -1)
    a["w2"] = np.concatenate([_tiles(fm2(w2)), _tiles(i["w_out_2"]), _tiles(i["peer_wq_2"])], 1)
    a["w_tm"] = tm2(w2).reshape(L, KT, P, TMW).transpose(0, 2, 1, 3)
    a["row"] = np.concatenate([i["b_router_grp"], i["b_router_exp"], tm2(b2), i["cmpv_b2_2"]], -1)[None]
    pad = lambda v: np.concatenate([v, np.zeros_like(v)], -1)
    pos = lambda v: v.reshape(L, CB // 2, 2 * HD).transpose(2, 0, 1)
    a["col2"] = _cols({
        "b_in": _col(fm2(b2)), "conv_w": i["conv_w_2"].reshape(L, 4, LT, P).transpose(3, 0, 1, 2).reshape(P, L, 16),
        "conv_b": _col(i["conv_b_2"]), "lru_ba": _col(i["lru_ba_2"]), "lru_bx": _col(i["lru_bx_2"]), "lam": _col(i["lru_lambda_2"]),
        "gn_lru": _col(i["gn_lru_g_2"]), "gn_nsa": _col(i["gn_nsa_g_2"]), "ln1_g": _col(i["ln1_g_2"]), "ln1_b": _col(i["ln1_b_2"]),
        "ln2_g": _col(i["ln2_g_2"]), "ln2_b": _col(i["ln2_b_2"]), "b1k": _col(pad(i["cmpk_b1_2"])), "b1v": _col(pad(i["cmpv_b1_2"])),
        "b2k": _col(dup(i["cmpk_b2_2"])), "pos_k": pos(i["cmp_pos_k_2"]), "pos_v": pos(i["cmp_pos_v_2"]),
    }, C2, C2_N)
    x2 = np.zeros((L, P, X2_N), np.float32)

    def put(name, v, rows=P):
        o, n = X2[name]
        x2[:, :rows, o:o + n] = v.reshape(L, rows, n)
    w1 = lambda v: v.reshape(L, 16, P, HD).transpose(0, 2, 1, 3)
    put("w1k", w1(i["cmpk_w1_2"]))
    put("w1v", w1(i["cmpv_w1_2"]))
    put("w2k", dup(i["cmpk_w2_2"]), HD)
    put("w2v", i["cmpv_w2_2"], HD)
    for name in ("wa", "wx"):
        blk = np.zeros((L, P, LT, P), np.float32)
        w = i[f"lru_{name}_2"]
        for t in range(LT):
            for q in range(2):
                blk[:, 64 * q:64 * q + 64, t, 64 * q:64 * q + 64] = w[:, 2 * t + q]
        put(name, blk)
    a["x2"] = x2
    a["sk_t"] = i["peer_subkeys_2"].transpose(0, 3, 1, 2)
    nc = _bacc.Bacc("TRN2", target_bir_lowering=False, num_devices=1)
    a = {k: np.ascontiguousarray(v) for k, v in a.items()}
    aps = {k: nc.dram_tensor(f"in_{k}", v.shape, F32, kind="ExternalInput").ap() for k, v in a.items()}
    out = nc.dram_tensor("out_fm", (P, KT, T), F32, kind="ExternalOutput").ap()
    program(nc, aps, out)
    r = _run(nc, [{f"in_{k}": v for k, v in a.items()}], core_ids=[0])
    return r.results[0]["out_fm"].transpose(2, 1, 0).reshape(1, T, D)
```
